# Optimizing a Trainium2 kernel written in Bass

```python
import jax
import jax.numpy as jnp
from jax import lax
import numpy as np

D_MODEL = 1024
BATCH = 1
SEQ = 1024
DEPTH = 1

HEAD_DIM = 64
SWA_HEADS = 8
SWA_KV_HEADS = 2
SWA_GROUP = SWA_HEADS // SWA_KV_HEADS
WINDOW = 128
SB_HEADS = 8
BLOCK = 128
SWA_WIDTH = SWA_HEADS * HEAD_DIM
SWA_KV_WIDTH = SWA_KV_HEADS * HEAD_DIM
SB_WIDTH = SB_HEADS * HEAD_DIM
IN_WIDTH = SWA_WIDTH + 2 * SWA_KV_WIDTH + 3 * SB_WIDTH + 2 * D_MODEL
N_EXPERTS = 32
TOP_K = 4
D_FF = D_MODEL
SWIGLU_LIMIT = 7.0
SWIGLU_ALPHA = 1.702
MOE_BLOCK = 128
NORM_EPS = 1e-5

kernel_name = "hybrid_swa_stickbreak_moe_block"

def rms_norm(x, w):
    xf = x.astype(jnp.float32)
    y = xf * lax.rsqrt(jnp.mean(xf * xf, axis=-1, keepdims=True) + NORM_EPS)
    return (y * w.astype(jnp.float32)).astype(x.dtype)

def alibi_slopes(n_heads):
    return jnp.asarray([2.0 ** (-8.0 * (i + 1) / n_heads) for i in range(n_heads)], dtype=jnp.float32)

def in_split_points():
    widths = (SWA_WIDTH, SWA_KV_WIDTH, SWA_KV_WIDTH, SB_WIDTH, SB_WIDTH, SB_WIDTH, D_MODEL, D_MODEL)
    points, acc = [], 0
    for w in widths[:-1]:
        acc += w
        points.append(acc)
    return points

def sliding_window_attention(q, k, v, q_norm_w, k_norm_w, sinks):
    B, S = q.shape[0], q.shape[1]
    nb = S // BLOCK
    q = rms_norm(q, q_norm_w)
    k = rms_norm(k, k_norm_w)
    qb = q.reshape(B, nb, BLOCK, SWA_KV_HEADS, SWA_GROUP, HEAD_DIM)

    def band(t):
        tb = t.reshape(B, nb, BLOCK, SWA_KV_HEADS, HEAD_DIM)
        prev = jnp.pad(tb[:, :-1], ((0, 0), (1, 0), (0, 0), (0, 0), (0, 0)))
        return jnp.concatenate([prev, tb], axis=2)

    kb, vb = band(k), band(v)
    scores = jnp.einsum('bnqhgd,bnkhd->bnhgqk', qb, kb).astype(jnp.float32) * (HEAD_DIM ** -0.5)
    q_pos = jnp.arange(BLOCK)[:, None] + BLOCK
    k_pos = jnp.arange(2 * BLOCK)[None, :]
    rel = q_pos - k_pos
    k_abs = jnp.arange(nb)[:, None, None] * BLOCK - BLOCK + k_pos
    valid = (rel >= 0) & (rel < WINDOW) & (k_abs >= 0)
    slopes = alibi_slopes(SWA_HEADS).reshape(SWA_KV_HEADS, SWA_GROUP)
    scores = scores - slopes[:, :, None, None] * rel.astype(jnp.float32)
    scores = jnp.where(valid[None, :, None, None], scores, -jnp.inf)
    sink = jnp.broadcast_to(sinks.astype(jnp.float32).reshape(1, 1, SWA_KV_HEADS, SWA_GROUP, 1, 1),
                            scores.shape[:-1] + (1,))
    probs = jax.nn.softmax(jnp.concatenate([scores, sink], axis=-1), axis=-1)[..., :-1]
    out = jnp.einsum('bnhgqk,bnkhd->bnqhgd', probs.astype(v.dtype), vb)
    return out.reshape(B, S, SWA_WIDTH)

def stick_breaking_attention(q, k, v):
    B, S = q.shape[0], q.shape[1]
    nb = S // BLOCK
    qb = q.reshape(B, nb, BLOCK, SB_HEADS, HEAD_DIM).transpose(1, 0, 2, 3, 4)
    k_pos = jnp.arange(S)
    scale = HEAD_DIM ** -0.5

    def one_block(args):
        q_blk, start = args
        z = jnp.einsum('bqhd,bkhd->bhqk', q_blk, k).astype(jnp.float32) * scale
        q_pos = start + jnp.arange(BLOCK)
        strict = k_pos[None, :] < q_pos[:, None]
        log_beta = jax.nn.log_sigmoid(z)
        log_keep = jnp.where(strict, jax.nn.log_sigmoid(-z), 0.0)
        between = lax.cumsum(log_keep, axis=3, reverse=True) - log_keep
        weights = jnp.where(strict, jnp.exp(log_beta + between), 0.0)
        return jnp.einsum('bhqk,bkhd->bqhd', weights.astype(v.dtype), v)

    out = lax.map(one_block, (qb, jnp.arange(nb) * BLOCK))
    return out.transpose(1, 0, 2, 3, 4).reshape(B, S, SB_WIDTH)

def moe_ffn(h, router_w, router_b, w_gate_up, b_gate_up, w_down, b_down):
    B, S, D = h.shape
    N = B * S
    xf = h.reshape(N, D)
    logits = (xf @ router_w + router_b).astype(jnp.float32)
    top_logit, top_idx = lax.top_k(logits, TOP_K)
    gate = jax.nn.softmax(top_logit, axis=-1)
    A = N * TOP_K
    flat_e = top_idx.reshape(A)
    order = jnp.argsort(flat_e)
    sorted_e = flat_e[order]
    slot_token = (order // TOP_K).astype(jnp.int32)
    slot_gate = gate.reshape(A)[order]
    counts = jnp.bincount(flat_e, length=N_EXPERTS)
    padded = (counts + MOE_BLOCK - 1) // MOE_BLOCK * MOE_BLOCK
    start = jnp.cumsum(counts) - counts
    pad_end = jnp.cumsum(padded)
    pad_start = pad_end - padded
    dest = pad_start[sorted_e] + jnp.arange(A) - start[sorted_e]
    cap = A + N_EXPERTS * MOE_BLOCK
    n_blocks = cap // MOE_BLOCK
    buf_token = jnp.zeros((cap,), jnp.int32).at[dest].set(slot_token)
    buf_gate = jnp.zeros((cap,), jnp.float32).at[dest].set(slot_gate)
    block_expert = jnp.minimum(
        jnp.searchsorted(pad_end, jnp.arange(n_blocks) * MOE_BLOCK, side='right'), N_EXPERTS - 1)
    xb = xf[buf_token].reshape(n_blocks, MOE_BLOCK, D)

    def expert_block(args):
        x_blk, e = args
        gu = x_blk @ w_gate_up[e] + b_gate_up[e]
        g = jnp.minimum(gu[:, :D_FF], SWIGLU_LIMIT)
        u = jnp.clip(gu[:, D_FF:], -SWIGLU_LIMIT, SWIGLU_LIMIT)
        act = (u + 1.0) * (g * jax.nn.sigmoid(SWIGLU_ALPHA * g))
        return act @ w_down[e] + b_down[e]

    yb = lax.map(expert_block, (xb, block_expert)).reshape(cap, D)
    out = jnp.zeros((N, D), h.dtype).at[buf_token].add(yb * buf_gate[:, None].astype(yb.dtype))
    return out.reshape(B, S, D)

def setup_inputs(seed: int = 0) -> dict:
    key = jax.random.key(seed)
    ks = jax.random.split(key, 16)
    L = DEPTH

    def nrm(k, shape, scale):
        return jax.random.normal(k, shape, jnp.float32) * scale

    return {
        "x": nrm(ks[0], (BATCH, SEQ, D_MODEL), 1.0),
        "attn_norm_w": 1.0 + nrm(ks[1], (L, D_MODEL), 0.02),
        "w_in": nrm(ks[2], (L, D_MODEL, IN_WIDTH), D_MODEL ** -0.5),
        "q_norm_w": 1.0 + nrm(ks[3], (L, HEAD_DIM), 0.02),
        "k_norm_w": 1.0 + nrm(ks[4], (L, HEAD_DIM), 0.02),
        "sinks": nrm(ks[5], (L, SWA_HEADS), 0.5),
        "w_proj_swa": nrm(ks[6], (L, SWA_WIDTH, D_MODEL), SWA_WIDTH ** -0.5),
        "w_proj_sb": nrm(ks[7], (L, SB_WIDTH, D_MODEL), SB_WIDTH ** -0.5),
        "w_out": nrm(ks[8], (L, D_MODEL, D_MODEL), D_MODEL ** -0.5),
        "ffn_norm_w": 1.0 + nrm(ks[9], (L, D_MODEL), 0.02),
        "router_w": nrm(ks[10], (L, D_MODEL, N_EXPERTS), D_MODEL ** -0.5),
        "router_b": nrm(ks[11], (L, N_EXPERTS), 0.01),
        "w_gate_up": nrm(ks[12], (L, N_EXPERTS, D_MODEL, 2 * D_FF), D_MODEL ** -0.5),
        "b_gate_up": nrm(ks[13], (L, N_EXPERTS, 2 * D_FF), 0.01),
        "w_down": nrm(ks[14], (L, N_EXPERTS, D_FF, D_MODEL), D_FF ** -0.5),
        "b_down": nrm(ks[15], (L, N_EXPERTS, D_MODEL), 0.01),
    }

def reference(x, attn_norm_w, w_in, q_norm_w, k_norm_w, sinks, w_proj_swa, w_proj_sb, w_out,
              ffn_norm_w, router_w, router_b, w_gate_up, b_gate_up, w_down, b_down):
    B, S = x.shape[0], x.shape[1]
    h = x
    for layer in range(DEPTH):
        xn = rms_norm(h, attn_norm_w[layer])
        proj = xn @ w_in[layer]
        q_a, k_a, v_a, q_b, k_b, v_b, g_a, g_b = jnp.split(proj, in_split_points(), axis=-1)
        y_a = sliding_window_attention(
            q_a.reshape(B, S, SWA_HEADS, HEAD_DIM),
            k_a.reshape(B, S, SWA_KV_HEADS, HEAD_DIM),
            v_a.reshape(B, S, SWA_KV_HEADS, HEAD_DIM),
            q_norm_w[layer], k_norm_w[layer], sinks[layer])
        y_b = stick_breaking_attention(
            q_b.reshape(B, S, SB_HEADS, HEAD_DIM),
            k_b.reshape(B, S, SB_HEADS, HEAD_DIM),
            v_b.reshape(B, S, SB_HEADS, HEAD_DIM))
        merged = (jax.nn.sigmoid(g_a) * (y_a @ w_proj_swa[layer])
                  + jax.nn.sigmoid(g_b) * (y_b @ w_proj_sb[layer]))
        h = h + merged @ w_out[layer]
        h = h + moe_ffn(rms_norm(h, ffn_norm_w[layer]), router_w[layer], router_b[layer],
                        w_gate_up[layer], b_gate_up[layer], w_down[layer], b_down[layer])
    return h


_drawn_inputs = setup_inputs


def setup_inputs(seed=0):
    import zlib

    import numpy as np

    out = dict(_drawn_inputs(seed))
    spreads = {}
    factors = {'q_norm_w': 3.728, 'k_norm_w': 4.637, 'sinks': 89.945, 'b_gate_up': 8.0, 'b_down': 8.0}
    for name, (base, spread) in spreads.items():
        noise = np.random.default_rng([zlib.crc32(name.encode()), seed]).standard_normal(out[name].shape)
        drawn = base * np.exp(spread * noise) if base else spread * noise
        out[name] = jnp.asarray(drawn.astype(out[name].dtype))
    for name, factor in factors.items():
        out[name] = (out[name] * factor).astype(out[name].dtype)
    return out
```

```python
from contextlib import ExitStack

import concourse.bass as bass
from concourse import mybir

F32 = mybir.dt.float32
F32R = mybir.dt.float32r
BF16 = mybir.dt.bfloat16
I32 = mybir.dt.int32
U32 = mybir.dt.uint32
ALU = mybir.AluOpType
ACT = mybir.ActivationFunctionType
AX_X = mybir.AxisListType.X

P = 128
T = 1024
D = 1024
NT = T // P
KD = D // P
HALF = 512
HD = 64
PAIRS = 4
WIN = 128
QA, KA, VA, QB, KB, VB, GA = 0, 512, 640, 768, 1280, 1792, 2304
IN_WIDTH = 4352
EPS = 1e-5
SCALE = HD ** -0.5
NEG = -1.0e30

NE = 32
TOPK = 4
FF = 1024
LIMIT = 7.0
ALPHA = 1.702
CAP = 160
CAP2 = CAP - P
MAXOVER = (T * TOPK) // CAP
NBLK = NE + MAXOVER
WIDTHS = (128, 144, 160)


def after(eng, sem, n):
    if not isinstance(n, int) or n > 0:
        eng.wait_ge(sem, n)


def split3(nc, out, w_hi, w_lo, x_hi, x_lo, first, last):
    nc.tensor.matmul(out, w_hi, x_hi, start=first, stop=False)
    nc.tensor.matmul(out, w_hi, x_lo, start=False, stop=False)
    return nc.tensor.matmul(out, w_lo, x_hi, start=False, stop=last)


def make_constants(nc, ident, eps_col, nhalf):
    with ExitStack() as ctx:
        cst = ctx.enter_context(nc.semaphore("cst_zeroed"))
        cst2 = ctx.enter_context(nc.semaphore("cst_done"))
        with nc.Block() as block:
            @block.gpsimd
            def _(pool):
                pool.memset(ident[:, :], 0.0).then_inc(cst, 1)
                pool.memset(eps_col[:, :], EPS).then_inc(cst, 1)
                pool.memset(nhalf[:, :], -0.5).then_inc(cst, 1)
                pool.wait_ge(cst, 3)
                pool.affine_select(out=ident[:, :], in_=ident[:, :], compare_op=ALU.not_equal, fill=1.0,
                                   base=0, pattern=[[-1, P]], channel_multiplier=1).then_inc(cst2, 1)
                pool.wait_ge(cst2, 1)


def norm_and_transpose(nc, x, attn_norm_w, ident, nhalf, xnT_hi, xnT_lo):
    with ExitStack() as ctx:
        sb = lambda n, s, d=F32: ctx.enter_context(nc.sbuf_tensor(n, s, d))
        sem = lambda n: ctx.enter_context(nc.semaphore(n))
        xin = sb("n1_x", [P, NT, D])
        wB = sb("n1_w", [P, D])
        xs = sb("n1_xs", [P, 2, D])
        junk = sb("n1_junk", [P, D])
        ssq = sb("n1_ssq", [P, NT])
        ms = sb("n1_ms", [P, NT])
        rstd = sb("n1_rstd", [P, NT])
        tr = ctx.enter_context(nc.psum_tensor("n1_tr", [P, 4, HALF], F32))
        x_in = [sem(f"n1_x_in{t}") for t in range(NT)]
        w_in_ = sem("n1_w_in")
        sq_done, ms_done, rstd_done = sem("n1_sq"), sem("n1_ms_d"), sem("n1_rstd_d")
        xs_done, tr_done, hi_done, lo_done = sem("n1_xs_d"), sem("n1_tr_d"), sem("n1_hi"), sem("n1_lo")
        x_t = x.rearrange("a (t p) d -> (a t) p d", p=P)
        with nc.Block() as block:
            @block.sync
            def _(sp):
                for t in range(NT):
                    sp.dma_start(xin[:, t, :], x_t[t]).then_inc(x_in[t], 16)
                    if t == 0:
                        sp.dma_start(wB[:, :], attn_norm_w[0:1, :].to_broadcast([P, D])).then_inc(w_in_, 16)

            @block.scalar
            def _(act):
                for t in range(NT):
                    act.wait_ge(x_in[t], 16)
                    if t:
                        act.wait_ge(sq_done, t)
                    nc.scalar.activation(junk[:, :], xin[:, t, :], ACT.Square,
                                         accum_out=ssq[:, t:t + 1]).then_inc(sq_done, 1)
                for m in range(2 * NT):
                    t, g = divmod(m, 2)
                    act.wait_ge(tr_done, m + 1)
                    nc.scalar.activation(xnT_hi[:, 4 * g:4 * g + 4, t * P:(t + 1) * P],
                                         tr[:, m % 4, :].rearrange("p (k c) -> p k c", k=4),
                                         ACT.Copy).then_inc(hi_done, 1)

            @block.gpsimd
            def _(pool):
                for t in range(NT):
                    pool.wait_ge(sq_done, t + 1)
                    nc.gpsimd.tensor_scalar(ms[:, t:t + 1], ssq[:, t:t + 1], 1.0 / D, EPS,
                                            ALU.mult, ALU.add).then_inc(ms_done, 1)
                    pool.wait_ge(ms_done, t + 1)
                    nc.gpsimd.tensor_tensor(rstd[:, t:t + 1], ms[:, t:t + 1], nhalf[:, 0:1],
                                            ALU.pow).then_inc(rstd_done, 1)

            @block.vector
            def _(dve):
                def scale_tile(t):
                    if t == 0:
                        dve.wait_ge(w_in_, 16)
                    dve.wait_ge(rstd_done, t + 1)
                    after(dve, tr_done, 2 * (t - 1))
                    nc.vector.scalar_tensor_tensor(out=xs[:, t % 2, :], in0=xin[:, t, :], scalar=rstd[:, t:t + 1],
                                                   in1=wB[:, :], op0=ALU.mult, op1=ALU.mult).then_inc(xs_done, 1)
                scale_tile(0)
                for t in range(NT):
                    if t + 1 < NT:
                        scale_tile(t + 1)
                    for g in range(2):
                        m = 2 * t + g
                        dve.wait_ge(hi_done, m + 1)
                        nc.vector.tensor_tensor(xnT_lo[:, 4 * g:4 * g + 4, t * P:(t + 1) * P],
                                                tr[:, m % 4, :].rearrange("p (k c) -> p k c", k=4),
                                                xnT_hi[:, 4 * g:4 * g + 4, t * P:(t + 1) * P].bitcast(F32),
                                                ALU.subtract).then_inc(lo_done, 1)

            @block.tensor
            def _(pe):
                for m in range(2 * NT):
                    t, g = divmod(m, 2)
                    pe.wait_ge(xs_done, t + 1)
                    after(pe, lo_done, m - 3)
                    for k in range(4):
                        last = nc.tensor.transpose(tr[:, m % 4, k * P:(k + 1) * P],
                                                   xs[:, t % 2, (4 * g + k) * P:(4 * g + k + 1) * P], ident[:, :])
                    last.then_inc(tr_done, 1)


def project_values(nc, w_in, xnT_hi, xnT_lo, va, vb):
    with ExitStack() as ctx:
        sb = lambda n, s, d=F32: ctx.enter_context(nc.sbuf_tensor(n, s, d))
        sem = lambda n: ctx.enter_context(nc.semaphore(n))
        raw = sb("pv_raw", [P, KD, HALF])
        raw_a = sb("pv_raw_a", [P, KD, P])
        w_hi = sb("pv_whi", [P, KD, HALF], F32R)
        w_lo = sb("pv_wlo", [P, KD, HALF], F32R)
        wa_hi = sb("pv_wahi", [P, KD, P], F32R)
        wa_lo = sb("pv_walo", [P, KD, P], F32R)
        acc = ctx.enter_context(nc.psum_tensor("pv_acc", [P, 4, HALF], F32))
        a_in, b_in = sem("pv_a_in"), sem("pv_b_in")
        hi_done, lo_done, mm_done, ev_done = sem("pv_hi"), sem("pv_lo"), sem("pv_mm"), sem("pv_ev")
        ev_even = sem("pv_ev_even")
        w_v = w_in.rearrange("a (k p) c -> p (a k) c", p=P)

        def evacuate(eng, n):
            eng.wait_ge(mm_done, n + 1)
            if n < NT:
                src = acc[:, n % 4, 0:P].rearrange("p (a o c) -> p a o c", a=2, o=1).to_broadcast([P, 2, 2, HD])
                dst = va[:, n, :].rearrange("p (a o c) -> p a o c", a=2, o=2)
            else:
                src, dst = acc[:, n % 4, :], vb[:, n - NT, :]
            if n % 2:
                nc.vector.tensor_copy(dst, src).then_inc(ev_done, 1)
            else:
                nc.scalar.activation(dst, src, ACT.Copy).then_inc(ev_even, 1)

        with nc.Block() as block:
            @block.sync
            def _(sp):
                sp.dma_start(raw_a[:, :, :], w_v[:, :, VA:VA + P]).then_inc(a_in, 16)
                sp.dma_start(raw[:, :, :], w_v[:, :, VB:VB + HALF]).then_inc(b_in, 16)

            @block.scalar
            def _(act):
                act.wait_ge(a_in, 16)
                nc.scalar.activation(wa_hi[:, :, :], raw_a[:, :, :], ACT.Copy).then_inc(hi_done, 1)
                act.wait_ge(b_in, 16)
                for k in range(0, KD, 2):
                    nc.scalar.activation(w_hi[:, k:k + 2, :], raw[:, k:k + 2, :], ACT.Copy).then_inc(hi_done, 1)
                for n in range(0, 2 * NT, 2):
                    evacuate(act, n)


            @block.vector
            def _(dve):
                dve.wait_ge(hi_done, 1)
                nc.vector.tensor_tensor(wa_lo[:, :, :], raw_a[:, :, :], wa_hi[:, :, :].bitcast(F32),
                                        ALU.subtract).then_inc(lo_done, 1)
                for k in range(0, KD, 2):
                    dve.wait_ge(hi_done, 2 + k // 2)
                    nc.vector.tensor_tensor(w_lo[:, k:k + 2, :], raw[:, k:k + 2, :],
                                            w_hi[:, k:k + 2, :].bitcast(F32), ALU.subtract).then_inc(lo_done, 1)
                for n in range(1, 2 * NT, 2):
                    evacuate(dve, n)

            @block.tensor
            def _(pe):
                for n in range(2 * NT):
                    if n == 0:
                        pe.wait_ge(lo_done, 1)
                    if n == NT:
                        pe.wait_ge(lo_done, 1 + KD // 2)
                    if n >= 4:
                        pe.wait_ge(ev_done if n % 2 else ev_even, n // 2 - 1)
                    t = n % NT
                    for k in range(KD):
                        wh, wl, out = ((wa_hi[:, k, :], wa_lo[:, k, :], acc[:, n % 4, 0:P]) if n < NT else
                                       (w_hi[:, k, :], w_lo[:, k, :], acc[:, n % 4, :]))
                        last = split3(nc, out, xnT_hi[:, k, t * P:(t + 1) * P], xnT_lo[:, k, t * P:(t + 1) * P],
                                      wh, wl, k == 0, k == KD - 1)
                    last.then_inc(mm_done, 1)


def hold(eng, sem, value, spare):
    eng.wait_ge(sem, value)
    eng.sem_inc(spare, 1)


SB_UNITS = [("sb", i, (h,)) for i in range(NT - 1, NT // 2 - 1, -1) for h in range(2)] + \
           [("sb", i, (0, 1)) for i in range(NT // 2 - 1, -1, -1)]
SWA_UNITS = [("swa", n, (0, 1)) for n in range(NT)]
UNITS = SB_UNITS + SWA_UNITS
NU, NSB, NSWA = len(UNITS), len(SB_UNITS), len(SWA_UNITS)


def unit_tiles(unit):
    kind, i, heads = unit
    first = max(i - 1, 0) if kind == "swa" else 0
    return [(s, kb) for s in range(len(heads)) for kb in range(first, i + 1)]


GROUPS = [-(-len(unit_tiles(u)) // 4) for u in UNITS]
GROUP0 = [sum(GROUPS[:n]) for n in range(NU)]
NG = sum(GROUPS)
PAIR_TILES = ["qa", "ka", "qb", "kb"]
GATE_TILES = ["g"] * 4


def attention(nc, w_in, q_norm_w, k_norm_w, sinks, ident, eps_col, xnT_hi, xnT_lo, va, vb, gT, y_s,
              y_slots):
    with ExitStack() as ctx:
        sb = lambda n, s, d=F32: ctx.enter_context(nc.sbuf_tensor(n, s, d))
        sem = lambda n: ctx.enter_context(nc.semaphore(n))
        ps = lambda n, s: ctx.enter_context(nc.psum_tensor(n, s, F32))
        raw = sb("at_raw", [P, 2, KD, P])
        w_hi = sb("at_whi", [P, 2, KD, P], F32R)
        w_lo = sb("at_wlo", [P, 2, KD, P], F32R)
        cur = {k: sb(f"at_cur_{k}", [P, T]) for k in PAIR_TILES}
        nxt = {k: sb(f"at_nxt_{k}", [P, T]) for k in PAIR_TILES}
        t1 = sb("at_t1", [P, 2, 2 * HALF])
        soft = sb("at_soft", [P, 2, 2 * HALF])
        logw = sb("at_logw", [P, 2, 2 * HALF])
        prob = sb("at_prob", [P, 2, 2 * HALF])
        probT = sb("at_probT", [P, 2, 8, P])
        sq = sb("at_sq", [P, HALF])
        rs = sb("at_rs", [P, HALF])
        gst = sb("at_gst", [P, 2, HALF])
        yst = sb("at_yst", [P, 2, P])
        bias = sb("at_bias", [P, 8, 2 * P])
        rel = sb("at_rel", [P, 2 * P])
        ones_blk = sb("at_ones_blk", [P, P])
        one_col = sb("at_one", [P, 1])
        wcol = sb("at_wcol", [P, 2])
        sinkB = sb("at_sink", [P, 8])
        nsinkB = sb("at_nsink", [P, 8])
        stat = {k: sb(f"at_{k}", [P, 2, 2]) for k in ("mx", "negm", "dsink", "rsum", "esink", "den", "rden")}
        z = ps("at_z", [P, 4, HALF])
        job = ps("at_job", [P, HALF])
        aux = ps("at_aux", [P, HALF])
        tr = ps("at_tr", [P, HALF])
        pv = ps("at_pv", [P, HALF])

        ZW = 500
        zeros = sb("at_zeros", [P, 1, ZW])
        z_out = sem("z_out")
        c_in, c_set, c_rel, c_bias, c_sink = (sem(n) for n in ("c_in", "c_set", "c_rel", "c_bias", "c_sink"))
        raw_in = [sem(f"raw_in{s}") for s in range(2)]
        whi_d, wlo_d = sem("whi_d"), sem("wlo_d")
        job_mm = sem("job_mm")
        job_ev = sem("job_ev")
        sq_d, ss_d, rs_d = sem("sq_d"), sem("ss_d"), sem("rs_d")
        g_out = [sem(f"g_out{s}") for s in range(2)]
        s_done = sem("s_done")
        z_free = sem("z_free")
        a_st = sem("a_st")
        d_soft = sem("d_soft")
        p_soft = sem("p_soft")
        d_scan = sem("d_scan")
        w_st = sem("w_st")
        a2_done = sem("a2_done")
        p_prob = sem("p_prob")
        tr_mm = sem("tr_mm")
        tr_ev = sem("tr_ev")
        pv_mm = sem("pv_mm")
        y_ev = sem("y_ev")
        y_out = [sem(f"y_out{s}") for s in range(2)]
        cur_d, cur_a = sem("cur_d"), sem("cur_a")
        spare_pool, spare_end = sem("spare_pool"), sem("spare_end")

        w_v = w_in.rearrange("a (k p) c -> p (a k) c", p=P)
        slot = lambda u: u % 2
        width = lambda unit: P * (unit[1] + 1)

        def zsl(u):
            kind, i, heads = UNITS[u]
            s = slot(u)
            if kind == "swa":
                return z[:, 2 * s:2 * s + 2, (0 if i else P):2 * P]
            if len(heads) == 2:
                return z[:, 2 * s:2 * s + 2, 0:width(UNITS[u])]
            return z[:, 2 * s:2 * s + 2, :].rearrange("p a c -> p (a c)")[:, 0:width(UNITS[u])]

        def bsl(buf, u):
            kind, i, heads = UNITS[u]
            s = slot(u)
            if kind == "swa":
                return buf[:, s, :].rearrange("p (a c) -> p a c", a=2)[:, :, (0 if i else P):2 * P]
            if len(heads) == 2:
                return buf[:, s, :].rearrange("p (a c) -> p a c", a=2)[:, :, 0:width(UNITS[u])]
            return buf[:, s, 0:width(UNITS[u])]

        def head_sl(buf, u, hs):
            v = bsl(buf, u)
            return v if len(UNITS[u][2]) == 1 else v[:, hs, :]

        def diag(buf, u):
            w = width(UNITS[u])
            v = bsl(buf, u)
            return v[:, w - P:w] if len(UNITS[u][2]) == 1 else v[:, :, w - P:w]

        block = ctx.enter_context(nc.Block())
        steps_full = {u: u for u in range(16)}
        steps_last = {2 * n: n for n in range(8)}

        def over_pairs(eng, body):
            with eng.Fori(0, PAIRS - 1) as p:
                body(p, PAIR_TILES + GATE_TILES, steps_full)
            body(PAIRS - 1, GATE_TILES, steps_last)

        @block.sync
        def _(sp):
            sp.dma_start(wcol[0:HD, 0:1], q_norm_w.rearrange("a (c b) -> (a c) b", b=1)).then_inc(c_in, 16)
            sp.dma_start(wcol[HD:P, 0:1], q_norm_w.rearrange("a (c b) -> (a c) b", b=1)).then_inc(c_in, 16)
            sp.dma_start(wcol[0:HD, 1:2], k_norm_w.rearrange("a (c b) -> (a c) b", b=1)).then_inc(c_in, 16)
            sp.dma_start(wcol[HD:P, 1:2], k_norm_w.rearrange("a (c b) -> (a c) b", b=1)).then_inc(c_in, 16)
            sp.dma_start(sinkB[:, :], sinks[0:1, :].to_broadcast([P, 8])).then_inc(c_in, 16)
            for s in range(2):
                sp.sem_inc(g_out[s], 16)

            def load(f, kind, pair, kvh, tl):
                s = tl % 2
                sp.wait_ge(wlo_d, f + 1)
                if kind == "ka":
                    for d in range(2):
                        sp.dma_start(raw[:, s, :, d * HD:(d + 1) * HD],
                                     w_v[:, :, bass.ds(KA + HD * kvh, HD)]).then_inc(raw_in[s], 16)
                    return
                col = {"qa": QA + P * pair, "qb": QB + P * pair, "kb": KB + P * pair, "g": GA + P * pair}[kind]
                sp.dma_start(raw[:, s, :, :], w_v[:, :, bass.ds(col, P)]).then_inc(raw_in[s], 32)

            for tl, kind in enumerate(PAIR_TILES):
                load(tl, kind, 0, 0, tl)

            def body(p, tiles, steps, kvh_next):
                fb = 4 + 8 * p

                def ld(tl):
                    kind = tiles[tl]
                    gate = tl - (len(tiles) - len(GATE_TILES))
                    load(fb + tl, kind, 4 * p + gate if kind == "g" else p + 1, kvh_next, tl)

                ld(0)
                for tl, kind in enumerate(tiles):
                    if tl + 1 < len(tiles):
                        ld(tl + 1)
                    if kind == "g":
                        g = 4 * p + tl - (len(tiles) - len(GATE_TILES))
                        for half in range(2):
                            sp.wait_ge(job_ev, 2 * (fb + tl) + half + 2)
                            sp.dma_start(gT[bass.ds(g, 1), :, half * HALF:(half + 1) * HALF].rearrange("a p c -> (a p) c"),
                                         gst[:, half, :]).then_inc(g_out[half], 16)

            body(0, PAIR_TILES + GATE_TILES, steps_full, 0)
            with sp.Fori(1, PAIRS - 1) as p:
                body(p, PAIR_TILES + GATE_TILES, steps_full, 1)
            body(PAIRS - 1, GATE_TILES, steps_last, 1)
            for s in range(2):
                sp.wait_ge(g_out[s], 16 * (16 + 1))

        @block.scalar
        def _(act):
            act.preload_act_table_set("natural_log_exp_and_others")
            act.sem_inc(a2_done, 2)
            act.sem_inc(tr_ev, 1)
            act.sem_inc(job_ev, 1)
            for s in range(2):
                act.sem_inc(y_out[s], 16)

            def split_hi(f, tl):
                s = tl % 2
                act.wait_ge(raw_in[s], 16 * (f + 2 - tl % 2))
                act.wait_ge(job_mm, 2 * f + 2)
                nc.scalar.activation(w_hi[:, s, :, :], raw[:, s, :, :], ACT.Copy).then_inc(whi_d, 1)

            def finish_job(j, jl, kind, nidx, g):
                half = jl % 2
                act.wait_ge(job_mm, j + 5)
                if kind in ("qb", "kb"):
                    nc.scalar.activation(nxt[kind][:, half * HALF:(half + 1) * HALF], job[:, :], ACT.Copy,
                                         scale=SCALE if kind == "qb" else 1.0).then_inc(job_ev, 1)
                elif kind == "g":
                    act.wait_ge(g_out[half], 16 * (g + 1))
                    nc.scalar.activation(gst[:, half, :], job[:, :], ACT.Copy).then_inc(job_ev, 1)
                else:
                    nc.scalar.activation(sq[:, :], job[:, :], ACT.Square).then_inc(sq_d, 1)

            def finish_norm(nidx):
                act.wait_ge(ss_d, nidx + 1)
                nc.scalar.activation(rs[:, :], aux[:, :], ACT.Ln, bias=eps_col[:, 0:1], scale=1.0 / HD)\
                    .then_inc(rs_d, 1)
                act.wait_ge(rs_d, 2 * nidx + 1)
                nc.scalar.activation(rs[:, :], rs[:, :], ACT.Exp, scale=-0.5).then_inc(rs_d, 1)

            def promote(p, j_last):
                after(act, s_done, NU * p)
                act.wait_ge(job_ev, j_last + 2)
                for kind in ("qb", "kb"):
                    nc.scalar.activation(cur[kind][:, :], nxt[kind][:, :], ACT.Copy).then_inc(cur_a, 1)

            def a1(p, u):
                if UNITS[u][0] != "sb":
                    return
                v = NSB * p + u
                act.wait_ge(s_done, NU * p + u + 1)
                act.wait_ge(d_soft, v + 1)
                nc.scalar.activation(bsl(t1, u), zsl(u), ACT.Abs).then_inc(a_st, 1)
                act.wait_ge(a_st, 3 * v + 1)
                nc.scalar.activation(bsl(t1, u), bsl(t1, u), ACT.Exp, scale=-1.0).then_inc(a_st, 1)
                act.wait_ge(a_st, 3 * v + 2)
                nc.scalar.activation(bsl(t1, u), bsl(t1, u), ACT.Ln, bias=1.0).then_inc(a_st, 1)

            def a2(p, u):
                s = slot(u)
                act.wait_ge(pv_mm, NU * p + u + 1)
                if UNITS[u][0] == "sb":
                    act.wait_ge(z_free, NU * p + u + 3)
                    nc.scalar.activation(bsl(prob, u), bsl(logw, u), ACT.Exp).then_inc(a2_done, 1)
                    return
                w = NSWA * p + u - NSB
                act.wait_ge(w_st, 5 * w + 3)
                for h in range(2):
                    nc.scalar.activation(head_sl(prob, u, h), head_sl(logw, u, h), ACT.Exp,
                                         bias=stat["negm"][:, s, h:h + 1], accum_out=stat["rsum"][:, s, h:h + 1])
                nc.scalar.activation(stat["esink"][:, s, :], stat["dsink"][:, s, :], ACT.Exp).then_inc(a2_done, 1)

            def evac_tr(p, u):
                tiles = unit_tiles(UNITS[u])
                for g in range(GROUPS[u]):
                    n = min(4, len(tiles) - 4 * g)
                    act.wait_ge(tr_mm, NG * p + GROUP0[u] + g + 1)
                    nc.scalar.activation(probT[:, slot(u), 4 * g:4 * g + n, :].rearrange("p a c -> p (a c)"),
                                         tr[:, 0:n * P], ACT.Copy).then_inc(tr_ev, 1)

            def store_y(p, u):
                kind, i, heads = UNITS[u]
                s, n = slot(u), len(heads) * HD
                act.wait_ge(y_ev, NU * p + u + 2)
                act.dma_start(y_s[1 if kind == "sb" else 0, i * P:(i + 1) * P, bass.ds(P * p + HD * heads[0], n)],
                              yst[:, s, 0:n]).then_inc(y_out[s], 16)

            for jl in range(8):
                if jl % 2 == 0:
                    split_hi(jl // 2, jl // 2)
                finish_job(jl, jl, PAIR_TILES[jl // 2], jl, 0)
                if jl < 4:
                    finish_norm(jl)
            promote(0, 7)

            def body(p, tiles, steps):
                fb = 4 + 8 * p
                split_hi(fb, 0)
                a1(p, 0)
                for u in range(NU):
                    if u + 1 < NU:
                        a1(p, u + 1)
                    if u:
                        store_y(p, u - 1)
                    a2(p, u)
                    if u in steps:
                        jl = steps[u]
                        tl = jl // 2
                        if jl % 2 == 0 and tl + 1 < len(tiles):
                            split_hi(fb + tl + 1, tl + 1)
                        finish_job(2 * fb + jl, jl, tiles[tl], None, 4 * p + tl - (len(tiles) - 4))
                    evac_tr(p, u)
                    if u in steps and tiles[steps[u] // 2] in ("qa", "ka"):
                        finish_norm(4 + 4 * p + steps[u])
                store_y(p, NU - 1)
                if len(tiles) > 4:
                    promote(p + 1, 2 * fb + 7)
            over_pairs(act, body)
            for s in range(2):
                act.wait_ge(y_out[s], 16 * (NU // 2 * PAIRS + 1))

        @block.gpsimd
        def _(pool):
            pool.sem_inc(wlo_d, 2)
            nc.gpsimd.memset(ones_blk[:, :], 0.0).then_inc(c_set, 1)
            nc.gpsimd.memset(one_col[:, :], 1.0).then_inc(c_set, 1)
            nc.gpsimd.memset(zeros[:, :, :], 0.0).then_inc(c_set, 1)
            pool.wait_ge(c_set, 3)
            for h in range(2):
                nc.gpsimd.memset(ones_blk[h * HD:(h + 1) * HD, h * HD:(h + 1) * HD], 1.0).then_inc(c_set, 1)
                pool.wait_ge(c_set, 4 + h)

            def split_lo(f, tl):
                s = tl % 2
                pool.wait_ge(whi_d, f + 1)
                nc.gpsimd.tensor_tensor(w_lo[:, s, :, :], raw[:, s, :, :], w_hi[:, s, :, :].bitcast(F32),
                                        ALU.subtract).then_inc(wlo_d, 1)

            further = y_slots[NE * CAP:NBLK * CAP, :].rearrange("r c -> (r c)").rearrange("(p n c) -> p n c", p=P, c=ZW)
            pool.dma_start(further, zeros[:, :, :].to_broadcast([P, MAXOVER * CAP * D // (P * ZW), ZW])).then_inc(z_out, 16)
            split_lo(0, 0)
            nc.gpsimd.iota(rel[:, :], [[-1, 2 * P]], base=P, channel_multiplier=1,
                           allow_small_or_imprecise_dtypes=True).then_inc(c_rel, 1)
            pool.wait_ge(c_rel, 1)
            for h in range(8):
                nc.gpsimd.tensor_scalar(bias[:, h, :], rel[:, :], -(2.0 ** -(h + 1)), None, ALU.mult).then_inc(c_bias, 1)
            pool.wait_ge(c_bias, 8)
            nc.gpsimd.affine_select(out=bias[:, :, :], in_=bias[:, :, :], compare_op=ALU.is_ge, fill=NEG, base=P,
                                    pattern=[[0, 8], [-1, 2 * P]], channel_multiplier=1).then_inc(c_bias, 1)
            pool.wait_ge(c_bias, 9)
            nc.gpsimd.affine_select(out=bias[:, :, :], in_=bias[:, :, :], compare_op=ALU.is_ge, fill=NEG, base=-1,
                                    pattern=[[0, 8], [1, 2 * P]], channel_multiplier=-1).then_inc(c_bias, 1)
            for tl in range(1, 4):
                split_lo(tl, tl)

            def mask(buf, u, done):
                d = diag(buf, u)
                pat = [[-1, P]] if len(UNITS[u][2]) == 1 else [[0, 2], [-1, P]]
                nc.gpsimd.affine_select(out=d, in_=d, compare_op=ALU.is_gt, fill=0.0, base=0, pattern=pat,
                                        channel_multiplier=1).then_inc(done, 1)

            def body(p, tiles, steps):
                fb = 4 + 8 * p
                split_lo(fb, 0)
                for u in range(NU):
                    if UNITS[u][0] == "sb":
                        v = NSB * p + u
                        hold(pool, d_soft, v + 3, spare_pool)
                        mask(soft, u, p_soft)
                        hold(pool, a2_done, NU * p + u + 3, spare_pool)
                        mask(prob, u, p_prob)
                    if u in steps and steps[u] % 2 == 0 and steps[u] // 2 + 1 < len(tiles):
                        tl = steps[u] // 2 + 1
                        split_lo(fb + tl, tl)
            over_pairs(pool, body)
            pool.wait_ge(z_out, 16)

        @block.vector
        def _(dve):
            dve.sem_inc(z_free, 2)
            dve.sem_inc(d_soft, 2)
            dve.sem_inc(y_ev, 1)
            dve.wait_ge(c_in, 80)
            nc.vector.tensor_scalar(nsinkB[:, :], sinkB[:, :], -1.0, None, ALU.mult).then_inc(c_sink, 1)
            nc.vector.tensor_scalar(wcol[:, 0:1], wcol[:, 0:1], SCALE, None, ALU.mult).then_inc(c_sink, 1)
            dve.wait_ge(c_sink, 2)

            def finish_norm(nidx, jl, kind):
                half = jl % 2
                c = 0 if kind == "qa" else 1
                dve.wait_ge(rs_d, 2 * nidx + 2)
                nc.vector.scalar_tensor_tensor(out=nxt[kind][:, half * HALF:(half + 1) * HALF], in0=job[:, :],
                                               scalar=wcol[:, c:c + 1], in1=rs[:, :], op0=ALU.mult,
                                               op1=ALU.mult).then_inc(job_ev, 1)

            def promote(p, j_last):
                after(dve, s_done, NU * p)
                dve.wait_ge(job_ev, j_last + 2)
                for kind in ("qa", "ka"):
                    nc.vector.tensor_copy(cur[kind][:, :], nxt[kind][:, :]).then_inc(cur_d, 1)

            def weights(p, u):
                v = NSB * p + u
                dve.wait_ge(a_st, 3 * v + 3)
                nc.vector.scalar_tensor_tensor(out=bsl(soft, u), in0=zsl(u), scalar=0.0, in1=bsl(t1, u),
                                               op0=ALU.max, op1=ALU.add).then_inc(d_soft, 1)
                dve.wait_ge(p_soft, v + 1)
                dve.wait_ge(a2_done, NU * p + u + 1)
                w = width(UNITS[u])
                for hs in range(len(UNITS[u][2])):
                    src, dst = head_sl(soft, u, hs), head_sl(logw, u, hs)
                    last = nc.vector.tensor_tensor_scan(out=dst[:, ::-1], data0=one_col[:, 0:1].to_broadcast([P, w]),
                                                        data1=src[:, ::-1], initial=0.0, op0=ALU.mult, op1=ALU.add)
                last.then_inc(d_scan, 1)
                dve.wait_ge(d_scan, v + 1)
                nc.vector.tensor_tensor(bsl(logw, u), zsl(u), bsl(logw, u), ALU.subtract).then_inc(z_free, 1)

            def scores(p, u):
                s, n = slot(u), UNITS[u][1]
                w = NSWA * p + u - NSB
                lo = 0 if n else P
                dve.wait_ge(s_done, NU * p + u + 1)
                dve.wait_ge(a2_done, NU * p + u + 1)
                nc.vector.tensor_tensor(bsl(logw, u), zsl(u), bias[:, bass.ds(2 * p, 2), lo:2 * P], ALU.add)\
                    .then_inc(z_free, 1)
                dve.wait_ge(z_free, NU * p + u + 3)
                nc.vector.tensor_reduce(stat["mx"][:, s, :], bsl(logw, u), AX_X, ALU.max).then_inc(w_st, 1)
                dve.wait_ge(w_st, 5 * w + 1)
                nc.vector.scalar_tensor_tensor(out=stat["negm"][:, s, :], in0=stat["mx"][:, s, :], scalar=-1.0,
                                               in1=nsinkB[:, bass.ds(2 * p, 2)], op0=ALU.mult, op1=ALU.min)\
                    .then_inc(w_st, 1)
                dve.wait_ge(w_st, 5 * w + 2)
                nc.vector.tensor_tensor(stat["dsink"][:, s, :], sinkB[:, bass.ds(2 * p, 2)], stat["negm"][:, s, :],
                                        ALU.add).then_inc(w_st, 1)

            def denominators(p, u):
                s = slot(u)
                w = NSWA * p + u - NSB
                dve.wait_ge(a2_done, NU * p + u + 3)
                nc.vector.tensor_tensor(stat["den"][:, s, :], stat["rsum"][:, s, :], stat["esink"][:, s, :],
                                        ALU.add).then_inc(w_st, 1)
                dve.wait_ge(w_st, 5 * w + 4)
                nc.vector.reciprocal(stat["rden"][:, s, :], stat["den"][:, s, :]).then_inc(w_st, 1)

            def result(p, u):
                kind, i, heads = UNITS[u]
                s, n = slot(u), len(heads) * HD
                if kind == "swa":
                    dve.wait_ge(w_st, 5 * (NSWA * p + u - NSB) + 5)
                dve.wait_ge(y_out[s], 16 * (NU // 2 * p + u // 2 + 1))
                dve.wait_ge(pv_mm, NU * p + u + 3)
                if kind == "sb":
                    nc.vector.tensor_copy(yst[:, s, 0:n], pv[:, 0:n]).then_inc(y_ev, 1)
                else:
                    nc.vector.tensor_scalar(yst[:, s, 0:HD], pv[:, 0:HD], stat["rden"][:, s, 0:1], None, ALU.mult)
                    nc.vector.tensor_scalar(yst[:, s, HD:P], pv[:, HD:P], stat["rden"][:, s, 1:2], None, ALU.mult)\
                        .then_inc(y_ev, 1)

            for jl in range(4):
                finish_norm(jl, jl, PAIR_TILES[jl // 2])
            promote(0, 7)
            dve.wait_ge(c_set, 5)
            dve.wait_ge(c_bias, 10)

            def body(p, tiles, steps):
                fb = 4 + 8 * p
                for u in range(NU):
                    if UNITS[u][0] == "sb":
                        weights(p, u)
                    else:
                        scores(p, u)
                        denominators(p, u)
                    if u in steps and tiles[steps[u] // 2] in ("qa", "ka"):
                        finish_norm(4 + 4 * p + steps[u], steps[u], tiles[steps[u] // 2])
                    result(p, u)
                if len(tiles) > 4:
                    promote(p + 1, 2 * fb + 7)
            over_pairs(dve, body)

        @block.tensor
        def _(pe):
            pe.sem_inc(job_mm, 4)
            pe.sem_inc(pv_mm, 2)

            def project(j, f, tl, half):
                s = tl % 2
                pe.wait_ge(wlo_d, f + 3)
                pe.wait_ge(job_ev, j + 1)
                for k in range(KD):
                    xh, xl = (v[:, k, half * HALF:(half + 1) * HALF] for v in (xnT_hi, xnT_lo))
                    last = split3(nc, job[:, :], w_hi[:, s, k, :], w_lo[:, s, k, :], xh, xl, k == 0, k == KD - 1)
                last.then_inc(job_mm, 1)

            def sum_squares(nidx):
                pe.wait_ge(sq_d, nidx + 1)
                nc.tensor.matmul(aux[:, :], ones_blk[:, :], sq[:, :], start=True, stop=True).then_inc(ss_d, 1)

            def score(p, u):
                kind, i, heads = UNITS[u]
                s = slot(u)
                q, k = (cur["qa"], cur["ka"]) if kind == "swa" else (cur["qb"], cur["kb"])
                pe.wait_ge(z_free, NU * p + u + 1)
                for hs, h in enumerate(heads):
                    lhs = q[h * HD:(h + 1) * HD, i * P:(i + 1) * P]
                    if kind == "swa":
                        lo = 0 if i else P
                        outs = [(z[:, 2 * s + hs, lo:2 * P], (i - 1) * P + lo, (i + 1) * P)]
                    elif len(heads) == 2:
                        outs = [(z[:, 2 * s + hs, 0:width(UNITS[u])], 0, width(UNITS[u]))]
                    else:
                        outs = [(z[:, 2 * s, :], 0, HALF), (z[:, 2 * s + 1, 0:width(UNITS[u]) - HALF], HALF, width(UNITS[u]))]
                    for out, k0, k1 in outs:
                        last = nc.tensor.matmul(out, lhs, k[h * HD:(h + 1) * HD, k0:k1], start=True, stop=True)
                last.then_inc(s_done, 1)

            def turn(p, u):
                kind, i, heads = UNITS[u]
                tiles = unit_tiles(UNITS[u])
                if kind == "sb":
                    pe.wait_ge(p_prob, NSB * p + u + 1)
                else:
                    pe.wait_ge(a2_done, NU * p + u + 3)
                first = tiles[0][1]
                for g in range(GROUPS[u]):
                    pe.wait_ge(tr_ev, NG * p + GROUP0[u] + g + 1)
                    for n, (hs, kb) in enumerate(tiles[4 * g:4 * g + 4]):
                        src = head_sl(prob, u, hs)
                        c = (kb - first) * P
                        last = nc.tensor.transpose(tr[:, n * P:(n + 1) * P], src[:, c:c + P], ident[:, :])
                    last.then_inc(tr_mm, 1)

            def weigh(p, u):
                kind, i, heads = UNITS[u]
                tiles = unit_tiles(UNITS[u])
                pe.wait_ge(tr_ev, NG * p + GROUP0[u] + GROUPS[u] + 1)
                pe.wait_ge(y_ev, NU * p + u + 1)
                for hs, h in enumerate(heads):
                    mine = [(n, kb) for n, (a, kb) in enumerate(tiles) if a == hs]
                    for m, (n, kb) in enumerate(mine):
                        v = vb[:, kb, bass.ds(P * p + HD * h, HD)] if kind == "sb" else va[:, kb, bass.ds(HD * p, HD)]
                        last = nc.tensor.matmul(pv[:, hs * HD:(hs + 1) * HD], probT[:, slot(u), n, :], v,
                                                start=m == 0, stop=m == len(mine) - 1)
                last.then_inc(pv_mm, 1)

            pe.wait_ge(c_set, 5)
            for jl in range(8):
                project(jl, jl // 2, jl // 2, jl % 2)
                if jl < 4:
                    sum_squares(jl)

            def body(p, tiles, steps):
                fb = 4 + 8 * p
                pe.wait_ge(cur_a, 2 * p + 2)
                pe.wait_ge(cur_d, 2 * p + 2)
                score(p, 0)
                for u in range(NU):
                    if u + 1 < NU:
                        score(p, u + 1)
                    if u in steps:
                        jl = steps[u]
                        project(2 * fb + jl, fb + jl // 2, jl // 2, jl % 2)
                    turn(p, u)
                    if u in steps and tiles[steps[u] // 2] in ("qa", "ka"):
                        sum_squares(4 + 4 * p + steps[u])
                    weigh(p, u)

            over_pairs(pe, body)


def merge(nc, w_proj_swa, w_proj_sb, ident, gT, y_s, mT_hi, mT_lo):
    KA4 = PAIRS
    with ExitStack() as ctx:
        sb = lambda n, s, d=F32: ctx.enter_context(nc.sbuf_tensor(n, s, d))
        sem = lambda n: ctx.enter_context(nc.semaphore(n))
        yT_hi = sb("mg_yThi", [P, 2, KA4, T], F32R)
        yT_lo = sb("mg_yTlo", [P, 2, KA4, T], F32R)
        ytok = sb("mg_ytok", [P, 4, HALF])
        raw = sb("mg_raw", [P, 2, 2, KA4, P])
        w_hi = sb("mg_whi", [P, 2, 2, KA4, P], F32R)
        w_lo = sb("mg_wlo", [P, 2, 2, KA4, P], F32R)
        g = sb("mg_g", [P, 2, 2, HALF])
        prod = sb("mg_prod", [P, 2, 2, HALF])
        acc = ctx.enter_context(nc.psum_tensor("mg_acc", [P, 4, HALF], F32))
        tr = ctx.enter_context(nc.psum_tensor("mg_tr", [P, 2, HALF], F32))
        y_in = [sem(f"mg_y_in{s}") for s in range(4)]
        raw_in = [sem(f"mg_raw_in{s}") for s in range(2)]
        g_in = [sem(f"mg_g_in{s}") for s in range(2)]
        tr_mm, yhi, ylo = sem("mg_tr_mm"), sem("mg_yhi"), sem("mg_ylo")
        whi_d, wlo_d = sem("mg_whi_d"), sem("mg_wlo_d")
        mm_done = sem("mg_mm")
        sg_done = sem("mg_sg")
        pr_done = sem("mg_pr")
        sum_done, mhi, mlo = sem("mg_sum"), sem("mg_mhi"), sem("mg_mlo")
        pa_v = w_proj_swa.rearrange("a (k p) c -> p (a k) c", p=P)
        pb_v = w_proj_sb.rearrange("a (k p) c -> p (a k) c", p=P)

        def over_tiles(eng, body):
            with eng.Fori(0, KD // 2 - 1) as i:
                for s in range(2):
                    body(2 * i + s, s, True)
            body(KD - 2, 0, True)
            body(KD - 1, 1, False)

        with nc.Block() as block:
            @block.sync
            def _(sp):
                def load_w(m, s):
                    sp.wait_ge(wlo_d, m + 1)
                    for n, v in enumerate((pa_v, pb_v)):
                        sp.dma_start(raw[:, s, n, :, :], v[:, :, bass.ds(m * P, P)]).then_inc(raw_in[s], 16)

                def body(m, s, more):
                    for half in range(2):
                        sp.wait_ge(pr_done, 2 * m + half + 1)
                        for n in range(2):
                            sp.dma_start(g[:, half, n, :],
                                         gT[bass.ds(KD * n + m, 1), :, half * HALF:(half + 1) * HALF]
                                         .rearrange("a p c -> (a p) c")).then_inc(g_in[half], 16)
                    if more:
                        load_w(m + 1, 1 - s)

                for n in range(2 * NT):
                    t, a = divmod(n, 2)
                    after(sp, tr_mm, n - 3)
                    sp.dma_start(ytok[:, n % 4, :], y_s[a, t * P:(t + 1) * P, :]).then_inc(y_in[n % 4], 16)
                load_w(0, 0)
                over_tiles(sp, body)

            @block.scalar
            def _(act):
                def split_hi(m, s):
                    act.wait_ge(raw_in[s], 16 * (m + 2 - s))
                    act.wait_ge(mm_done, 2 * m + 1)
                    nc.scalar.activation(w_hi[:, s], raw[:, s], ACT.Copy).then_inc(whi_d, 1)

                def body(m, s, more):
                    if more:
                        split_hi(m + 1, 1 - s)
                    for half in range(2):
                        n = 2 * m + half
                        act.wait_ge(g_in[half], 32 * (m + 1))
                        nc.scalar.activation(g[:, half], g[:, half], ACT.Sigmoid).then_inc(sg_done, 1)
                    for half in range(2):
                        n = 2 * m + half
                        act.wait_ge(sum_done, n + 1)
                        nc.scalar.activation(mT_hi[:, bass.ds(m, 1), half * HALF:(half + 1) * HALF]
                                             .rearrange("p a c -> p (a c)"),
                                             prod[:, half, 0, :], ACT.Copy).then_inc(mhi, 1)

                for n in range(2 * NT):
                    t, a = divmod(n, 2)
                    act.wait_ge(tr_mm, n + 1)
                    nc.scalar.activation(yT_hi[:, a, :, t * P:(t + 1) * P],
                                         tr[:, n % 2, :].rearrange("p (k c) -> p k c", k=4), ACT.Copy).then_inc(yhi, 1)
                split_hi(0, 0)
                over_tiles(act, body)

            @block.gpsimd
            def _(pool):
                pool.sem_inc(wlo_d, 2)

                def split_lo(m, s):
                    pool.wait_ge(whi_d, m + 1)
                    nc.gpsimd.tensor_tensor(w_lo[:, s], raw[:, s], w_hi[:, s].bitcast(F32), ALU.subtract)\
                        .then_inc(wlo_d, 1)
                split_lo(0, 0)
                over_tiles(pool, lambda m, s, more: split_lo(m + 1, 1 - s) if more else None)

            @block.vector
            def _(dve):
                dve.sem_inc(pr_done, 2)
                dve.sem_inc(mlo, 2)
                for n in range(2 * NT):
                    t, a = divmod(n, 2)
                    dve.wait_ge(yhi, n + 1)
                    nc.vector.tensor_tensor(yT_lo[:, a, :, t * P:(t + 1) * P],
                                            tr[:, n % 2, :].rearrange("p (k c) -> p k c", k=4),
                                            yT_hi[:, a, :, t * P:(t + 1) * P].bitcast(F32), ALU.subtract).then_inc(ylo, 1)

                def body(m, s, more):
                    for half in range(2):
                        n = 2 * m + half
                        dve.wait_ge(mm_done, n + 5)
                        dve.wait_ge(sg_done, n + 1)
                        dve.wait_ge(mlo, n + 1)
                        nc.vector.tensor_tensor(prod[:, half], acc[:, 2 * half:2 * half + 2, :], g[:, half],
                                                ALU.mult).then_inc(pr_done, 1)
                        dve.wait_ge(pr_done, n + 3)
                        nc.vector.tensor_tensor(prod[:, half, 0, :], prod[:, half, 0, :], prod[:, half, 1, :],
                                                ALU.add).then_inc(sum_done, 1)
                    for half in range(2):
                        n = 2 * m + half
                        dve.wait_ge(mhi, n + 1)
                        sl = (slice(None), bass.ds(m, 1), slice(half * HALF, (half + 1) * HALF))
                        nc.vector.tensor_tensor(mT_lo[sl].rearrange("p a c -> p (a c)"), prod[:, half, 0, :],
                                                mT_hi[sl].rearrange("p a c -> p (a c)").bitcast(F32),
                                                ALU.subtract).then_inc(mlo, 1)
                over_tiles(dve, body)

            @block.tensor
            def _(pe):
                pe.sem_inc(mm_done, 4)
                for n in range(2 * NT):
                    t, a = divmod(n, 2)
                    pe.wait_ge(y_in[n % 4], 16 * (n // 4 + 1))
                    after(pe, ylo, n - 1)
                    for k in range(4):
                        last = nc.tensor.transpose(tr[:, n % 2, k * P:(k + 1) * P], ytok[:, n % 4, k * P:(k + 1) * P],
                                                   ident[:, :])
                    last.then_inc(tr_mm, 1)
                pe.wait_ge(ylo, 2 * NT)

                def body(m, s, more):
                    pe.wait_ge(wlo_d, m + 3)
                    for half in range(2):
                        pe.wait_ge(pr_done, 2 * m + half + 1)
                        for a in range(2):
                            for k in range(KA4):
                                last = split3(nc, acc[:, 2 * half + a, :], w_hi[:, s, a, k, :], w_lo[:, s, a, k, :],
                                              yT_hi[:, a, k, half * HALF:(half + 1) * HALF],
                                              yT_lo[:, a, k, half * HALF:(half + 1) * HALF], k == 0, k == KA4 - 1)
                        last.then_inc(mm_done, 1)
                over_tiles(pe, body)


def output_and_logits(nc, x, w_out, ffn_norm_w, router_w, router_b, ident, nhalf, mT_hi, mT_lo, h_s, xn_s, logits):
    with ExitStack() as ctx:
        sb = lambda n, s, d=F32: ctx.enter_context(nc.sbuf_tensor(n, s, d))
        sem = lambda n: ctx.enter_context(nc.semaphore(n))
        raw = sb("op_raw", [P, 2, D])
        w_hi = sb("op_whi", [P, KD, D], F32R)
        w_lo = sb("op_wlo", [P, KD, D], F32R)
        xt = sb("op_x", [P, 2, D])
        ht = sb("op_h", [P, 2, D])
        xn = sb("op_xn", [P, 2, D])
        xnT = sb("op_xnT", [P, KD, P])
        junk = sb("op_junk", [P, D])
        wB = sb("op_wB", [P, D])
        rw = sb("op_rw", [P, KD, NE])
        rbB = sb("op_rb", [P, NE])
        ssq, ms, rstd = (sb(f"op_{n}", [P, NT]) for n in ("ssq", "ms", "rstd"))
        acc = ctx.enter_context(nc.psum_tensor("op_acc", [P, 4, HALF], F32))
        tr = ctx.enter_context(nc.psum_tensor("op_tr", [P, 2, HALF], F32))
        lg = ctx.enter_context(nc.psum_tensor("op_lg", [P, HALF], F32))
        raw_in = [sem(f"op_raw_in{s}") for s in range(2)]
        x_in = [sem(f"op_x_in{s}") for s in range(2)]
        h_out = [sem(f"op_h_out{s}") for s in range(2)]
        xn_out = [sem(f"op_xn_out{s}") for s in range(2)]
        c_in = sem("op_c_in")
        whi_d, wlo_d, mm_done, h_done = sem("op_whi_d"), sem("op_wlo_d"), sem("op_mm"), sem("op_h_d")
        sq_done, ms_done, rstd_done, xn_done = sem("op_sq"), sem("op_ms_d"), sem("op_rstd_d"), sem("op_xn_d")
        tr_mm, tr_ev, lg_mm, lg_ev = sem("op_tr_mm"), sem("op_tr_ev"), sem("op_lg_mm"), sem("op_lg_ev")
        x_t = x.rearrange("a (t p) d -> (a t) p d", p=P)
        h_t = h_s.rearrange("(t p) d -> t p d", p=P)
        xn_t = xn_s.rearrange("(t p) d -> t p d", p=P)
        with nc.Block() as block:
            @block.sync
            def _(sp):
                for k in range(KD):
                    after(sp, wlo_d, k - 1)
                    sp.dma_start(raw[:, k % 2, :], w_out[0, k * P:(k + 1) * P, :]).then_inc(raw_in[k % 2], 16)
                    if k == 1:
                        for t in range(2):
                            sp.dma_start(xt[:, t, :], x_t[t]).then_inc(x_in[t], 16)
                sp.dma_start(wB[:, :], ffn_norm_w[0:1, :].to_broadcast([P, D])).then_inc(c_in, 16)
                sp.dma_start(rbB[:, :], router_b[0:1, :].to_broadcast([P, NE])).then_inc(c_in, 16)
                sp.dma_start(rw[:, :, :], router_w.rearrange("a (k p) c -> p (a k) c", p=P)).then_inc(c_in, 16)
                for t in range(NT):
                    sp.wait_ge(h_done, t + 1)
                    sp.dma_start(h_t[t], ht[:, t % 2, :]).then_inc(h_out[t % 2], 16)
                    if t + 2 < NT:
                        sp.dma_start(xt[:, t % 2, :], x_t[t + 2]).then_inc(x_in[t % 2], 16)
                    sp.wait_ge(xn_done, t + 1)
                    sp.dma_start(xn_t[t], xn[:, t % 2, :]).then_inc(xn_out[t % 2], 16)
                for s in range(2):
                    sp.wait_ge(h_out[s], 16 * NT // 2)
                    sp.wait_ge(xn_out[s], 16 * NT // 2)

            @block.scalar
            def _(act):
                for k in range(KD):
                    act.wait_ge(raw_in[k % 2], 16 * (k // 2 + 1))
                    nc.scalar.activation(w_hi[:, k, :], raw[:, k % 2, :], ACT.Copy).then_inc(whi_d, 1)
                for t in range(NT):
                    act.wait_ge(h_done, t + 1)
                    if t:
                        act.wait_ge(sq_done, t)
                    nc.scalar.activation(junk[:, :], ht[:, t % 2, :], ACT.Square, accum_out=ssq[:, t:t + 1])\
                        .then_inc(sq_done, 1)
                    act.wait_ge(tr_mm, t + 1)
                    after(act, lg_mm, t)
                    nc.scalar.activation(xnT[:, :, :].rearrange("p k c -> p (k c)"),
                                         tr[:, :, :].rearrange("p a c -> p (a c)"), ACT.Copy).then_inc(tr_ev, 1)

            @block.gpsimd
            def _(pool):
                for t in range(NT):
                    pool.wait_ge(sq_done, t + 1)
                    nc.gpsimd.tensor_scalar(ms[:, t:t + 1], ssq[:, t:t + 1], 1.0 / D, EPS,
                                            ALU.mult, ALU.add).then_inc(ms_done, 1)
                    pool.wait_ge(ms_done, t + 1)
                    nc.gpsimd.tensor_tensor(rstd[:, t:t + 1], ms[:, t:t + 1], nhalf[:, 0:1],
                                            ALU.pow).then_inc(rstd_done, 1)

            @block.vector
            def _(dve):
                for k in range(KD):
                    dve.wait_ge(whi_d, k + 1)
                    nc.vector.tensor_tensor(w_lo[:, k, :], raw[:, k % 2, :], w_hi[:, k, :].bitcast(F32),
                                            ALU.subtract).then_inc(wlo_d, 1)
                dve.wait_ge(c_in, 48)

                def residual(t):
                    s = t % 2
                    dve.wait_ge(mm_done, t + 1)
                    dve.wait_ge(x_in[s], 16 * (t // 2 + 1))
                    after(dve, h_out[s], 16 * (t // 2))
                    nc.vector.tensor_tensor(ht[:, s, :], acc[:, 2 * s:2 * s + 2, :].rearrange("p a c -> p (a c)"),
                                            xt[:, s, :], ALU.add).then_inc(h_done, 1)

                residual(0)
                for t in range(NT):
                    s = t % 2
                    if t + 1 < NT:
                        residual(t + 1)
                    dve.wait_ge(rstd_done, t + 1)
                    after(dve, xn_out[s], 16 * (t // 2))
                    after(dve, tr_mm, t - 1)
                    nc.vector.scalar_tensor_tensor(out=xn[:, s, :], in0=ht[:, s, :], scalar=rstd[:, t:t + 1],
                                                   in1=wB[:, :], op0=ALU.mult, op1=ALU.mult).then_inc(xn_done, 1)
                    dve.wait_ge(lg_mm, t + 1)
                    nc.vector.tensor_tensor(logits[:, t, :], lg[:, 0:NE], rbB[:, :], ALU.add).then_inc(lg_ev, 1)

            @block.tensor
            def _(pe):
                def project(t):
                    after(pe, h_done, t - 1)
                    for nh in range(2):
                        for k in range(KD):
                            if t == 0 and nh == 0:
                                pe.wait_ge(wlo_d, k + 1)
                            last = split3(nc, acc[:, 2 * (t % 2) + nh, :], mT_hi[:, k, t * P:(t + 1) * P],
                                          mT_lo[:, k, t * P:(t + 1) * P], w_hi[:, k, nh * HALF:(nh + 1) * HALF],
                                          w_lo[:, k, nh * HALF:(nh + 1) * HALF], k == 0, k == KD - 1)
                    last.then_inc(mm_done, 1)

                project(0)
                for t in range(NT):
                    if t + 1 < NT:
                        project(t + 1)
                    pe.wait_ge(xn_done, t + 1)
                    after(pe, tr_ev, t)
                    for k in range(KD):
                        last = nc.tensor.transpose(tr[:, k // 4, (k % 4) * P:(k % 4 + 1) * P],
                                                   xn[:, t % 2, k * P:(k + 1) * P], ident[:, :])
                    last.then_inc(tr_mm, 1)
                    pe.wait_ge(tr_ev, t + 1)
                    after(pe, lg_ev, t)
                    for k in range(KD):
                        last = nc.tensor.matmul(lg[:, 0:NE], xnT[:, k, :], rw[:, k, :], start=k == 0, stop=k == KD - 1)
                    last.then_inc(lg_mm, 1)


SLOTS = (NBLK + 1) * CAP
TABLE = -(-SLOTS // P) * P


def route(nc, logits, gates, dest, tabs, slot_token):
    with ExitStack() as ctx:
        sb = lambda n, s, d=F32: ctx.enter_context(nc.sbuf_tensor(n, s, d))
        sem = lambda n: ctx.enter_context(nc.semaphore(n))
        top = sb("rt_top", [P, NT, 8])
        idx = sb("rt_idx", [P, NT, 8], U32)
        idxf = sb("rt_idxf", [P, NT, TOPK])
        ex = sb("rt_ex", [P, NT, TOPK])
        den = sb("rt_den", [P, NT])
        iota_e = sb("rt_iota", [P, NE])
        oh = sb("rt_oh", [P, NT, TOPK, NE])
        prod = sb("rt_prod", [P, NT, TOPK, NE])
        chosen = sb("rt_chosen", [P, NT, NE])
        chosen16 = sb("rt_chosen16", [P, NT, NE], BF16)
        upper = sb("rt_upper", [P, P], BF16)
        ones = sb("rt_ones", [P, P], BF16)
        one_col = sb("rt_one", [P, 1])
        cnt, over, cum, base0, base1, step_b = (sb(f"rt_{n}", [P, NE]) for n in
                                               ("cnt", "over", "cum", "base0", "base1", "stepb"))
        rank = sb("rt_rank", [P, NT, NE])
        place = sb("rt_place", [P, NT, NE])
        destf = sb("rt_destf", [P, NT * TOPK])
        cmp = sb("rt_cmp", [1, MAXOVER, NE])
        iota_b = sb("rt_iotab", [1, MAXOVER])
        tabf = sb("rt_tabf", [1, NE + MAXOVER + 1])
        zero = sb("rt_zero", [P, TABLE // P], I32)
        prk = ctx.enter_context(nc.psum_tensor("rt_prk", [P, HALF], F32))
        pct = ctx.enter_context(nc.psum_tensor("rt_pct", [P, HALF], F32))
        c_set, v, a_exp, mm, z_out = sem("rt_cset"), sem("rt_v"), sem("rt_exp"), sem("rt_mm"), sem("rt_zout")
        m16 = sem("rt_m16")
        with nc.Block() as block:
            @block.sync
            def _(sp):
                sp.wait_ge(c_set, 6)
                sp.dma_start(slot_token.rearrange("(p n) a -> p (n a)", p=P), zero[:, :]).then_inc(z_out, 16)
                sp.wait_ge(z_out, 16)

            @block.gpsimd
            def _(pool):
                nc.gpsimd.iota(iota_e[:, :], [[1, NE]], base=0, channel_multiplier=0,
                               allow_small_or_imprecise_dtypes=True).then_inc(c_set, 1)
                nc.gpsimd.iota(iota_b[:, :], [[1, MAXOVER]], base=0, channel_multiplier=0,
                               allow_small_or_imprecise_dtypes=True).then_inc(c_set, 1)
                nc.gpsimd.memset(ones[:, :], 1.0).then_inc(c_set, 1)
                nc.gpsimd.memset(upper[:, :], 1.0).then_inc(c_set, 1)
                nc.gpsimd.memset(one_col[:, :], 1.0).then_inc(c_set, 1)
                nc.gpsimd.memset(zero[:, :], 0).then_inc(c_set, 1)
                pool.wait_ge(c_set, 6)
                nc.gpsimd.affine_select(out=upper[:, :], in_=upper[:, :], compare_op=ALU.is_gt, fill=0.0, base=0,
                                        pattern=[[1, P]], channel_multiplier=-1).then_inc(c_set, 1)

            @block.scalar
            def _(act):
                act.wait_ge(v, 2 * NT + 1)
                nc.scalar.activation(ex[:, :, :], ex[:, :, :], ACT.Exp).then_inc(a_exp, 1)

            @block.vector
            def _(dve):
                n = [0]

                def step(ins):
                    n[0] += 1
                    ins.then_inc(v, 1)
                    dve.wait_ge(v, n[0])

                for t in range(NT):
                    step(nc.vector.max(top[:, t, :], logits[:, t, :]))
                    step(nc.vector.max_index(idx[:, t, :], top[:, t, :], logits[:, t, :]))
                step(nc.vector.tensor_tensor(ex[:, :, :], top[:, :, 0:TOPK], top[:, :, 0:1].to_broadcast([P, NT, TOPK]),
                                             ALU.subtract))
                step(nc.vector.tensor_copy(idxf[:, :, :], idx[:, :, 0:TOPK]))
                dve.wait_ge(c_set, 7)
                step(nc.vector.tensor_tensor(
                    oh[:, :, :, :].rearrange("p t j e -> p (t j) e"),
                    iota_e[:, :].rearrange("p (o e) -> p o e", o=1).to_broadcast([P, NT * TOPK, NE]),
                    idxf[:, :, :].rearrange("p t (j o) -> p (t j) o", o=1).to_broadcast([P, NT * TOPK, NE]), ALU.is_equal))
                step(nc.vector.tensor_reduce(chosen[:, :, :], oh[:, :, :, :].rearrange("p t j e -> p t e j"), AX_X, ALU.add))
                nc.vector.tensor_copy(chosen16[:, :, :], chosen[:, :, :]).then_inc(m16, 1)
                dve.wait_ge(a_exp, 1)
                step(nc.vector.tensor_reduce(den[:, :], ex[:, :, :], AX_X, ALU.add))
                step(nc.vector.reciprocal(den[:, :], den[:, :]))
                step(nc.vector.tensor_tensor(gates[:, :, :], ex[:, :, :],
                                             den[:, :].rearrange("p (t o) -> p t o", o=1).to_broadcast([P, NT, TOPK]),
                                             ALU.mult))
                dve.wait_ge(mm, 2)
                step(nc.vector.tensor_copy(cnt[:, :], pct[:, 0:NE]))
                step(nc.vector.tensor_scalar(over[:, :], cnt[:, :], float(CAP), None, ALU.is_gt))
                for m in range(2, -(-T // CAP)):
                    step(nc.vector.scalar_tensor_tensor(out=over[:, :], in0=cnt[:, :], scalar=float(CAP * m), in1=over[:, :],
                                                        op0=ALU.is_gt, op1=ALU.add))
                step(nc.vector.tensor_tensor_scan(out=cum[:, :], data0=one_col[:, 0:1].to_broadcast([P, NE]),
                                                  data1=over[:, :], initial=0.0, op0=ALU.mult, op1=ALU.add))
                step(nc.vector.tensor_tensor(base1[:, :], cum[:, :], over[:, :], ALU.subtract))
                step(nc.vector.tensor_scalar(base1[:, :], base1[:, :], float(NE - 1), float(CAP), ALU.add, ALU.mult))
                step(nc.vector.tensor_scalar(base0[:, :], iota_e[:, :], float(CAP), None, ALU.mult))
                step(nc.vector.tensor_tensor(step_b[:, :], base0[:, :], base1[:, :], ALU.subtract))
                step(nc.vector.tensor_copy(rank[:, :, :], prk[:, 0:NT * NE].rearrange("p (t e) -> p t e", e=NE)))
                step(nc.vector.tensor_scalar(place[:, :, :], rank[:, :, :], float(CAP), None, ALU.is_lt))
                over_t = lambda b: b[:, :].rearrange("p (o e) -> p o e", o=1).to_broadcast([P, NT, NE])
                step(nc.vector.tensor_tensor(place[:, :, :], place[:, :, :], over_t(step_b), ALU.mult))
                step(nc.vector.tensor_tensor(place[:, :, :], place[:, :, :], over_t(base1), ALU.add))
                step(nc.vector.tensor_tensor(place[:, :, :], place[:, :, :], rank[:, :, :], ALU.add))
                for j in range(TOPK):
                    step(nc.vector.tensor_tensor(prod[:, :, j, :], oh[:, :, j, :], place[:, :, :], ALU.mult))
                step(nc.vector.tensor_reduce(destf[:, :], prod[:, :, :, :].rearrange("p t j e -> p (t j) e"), AX_X, ALU.add))
                step(nc.vector.tensor_copy(dest[:, :], destf[:, :]))
                step(nc.vector.tensor_tensor(cmp[:, :, :],
                                             cum[0:1, :].rearrange("p (o e) -> p o e", o=1).to_broadcast([1, MAXOVER, NE]),
                                             iota_b[:, :].rearrange("p (b o) -> p b o", o=1).to_broadcast([1, MAXOVER, NE]),
                                             ALU.is_le))
                step(nc.vector.tensor_reduce(tabf[:, NE:NE + MAXOVER], cmp[:, :, :], AX_X, ALU.add))
                step(nc.vector.tensor_scalar(tabf[:, NE:NE + MAXOVER], tabf[:, NE:NE + MAXOVER], float(NE - 1), None, ALU.min))
                step(nc.vector.tensor_copy(tabf[:, 0:NE], cnt[0:1, :]))
                step(nc.vector.tensor_copy(tabf[:, NE + MAXOVER:NE + MAXOVER + 1], cum[0:1, NE - 1:NE]))
                step(nc.vector.tensor_copy(tabs[:, :], tabf[:, :]))

            @block.tensor
            def _(pe):
                pe.wait_ge(c_set, 7)
                pe.wait_ge(m16, 1)
                for t in range(NT):
                    for b in range(t + 1):
                        last = nc.tensor.matmul(prk[:, t * NE:(t + 1) * NE], (upper if b == t else ones)[:, :],
                                                chosen16[:, b, :], start=b == 0, stop=b == t)
                last.then_inc(mm, 1)
                for b in range(NT):
                    last = nc.tensor.matmul(pct[:, 0:NE], ones[:, :], chosen16[:, b, :], start=b == 0, stop=b == NT - 1)
                last.then_inc(mm, 1)


CHUNKS = 6
CW = 4096
PIECE = 1024
POOL_FROM = 3
FT = FF // P


def experts(nc, xn_s, w_gate_up, b_gate_up, w_down, b_down, ident, dest, tabs, slot_token, y_slots):
    with ExitStack() as ctx:
        sb = lambda n, s, d=F32: ctx.enter_context(nc.sbuf_tensor(n, s, d))
        sem = lambda n: ctx.enter_context(nc.semaphore(n))
        raw = sb("ex_raw", [P, 3, CW])
        w_hi = sb("ex_whi", [P, 2, CW], F32R)
        w_lo = sb("ex_wlo", [P, 2, CW], F32R)
        idx = sb("ex_idx", [P, 2], U32)
        xg = sb("ex_xg", [P, D])
        xg2 = sb("ex_xg2", [CAP2, D])
        xT_hi = sb("ex_xThi", [P, KD, CAP], F32R)
        xT_lo = sb("ex_xTlo", [P, KD, CAP], F32R)
        gs = sb("ex_g", [P, 2, CAP])
        us = sb("ex_u", [P, 2, CAP])
        sg = sb("ex_sg", [P, 2, CAP])
        act_f = sb("ex_act", [P, FT, CAP])
        act_hi = sb("ex_acthi", [P, FT, CAP], F32R)
        act_lo = sb("ex_actlo", [P, FT, CAP], F32R)
        yT = sb("ex_yT", [P, KD, CAP])
        ytok = sb("ex_ytok", [P, D])
        ytok2 = sb("ex_ytok2", [P, D])
        bT = sb("ex_bT", [P, 3 * KD, NE])
        bcur = sb("ex_bcur", [P, 3 * KD])
        brow = yT[0:NE, :, :].rearrange("p a c -> p (a c)")
        tokid = sb("ex_tokid", [P, NT], I32)
        ps = lambda n, s: ctx.enter_context(nc.psum_tensor(n, s, F32))
        gu = ps("ex_gu", [P, 4, HALF])
        yp = ps("ex_yp", [P, 2, HALF])
        tr = ps("ex_tr", [P, 2, HALF])

        b_in, b_mm, b_ev, b_d = sem("b_in"), sem("b_mm"), sem("b_ev"), sem("b_d")
        ini, tok_out, tok_set = sem("ini"), sem("tok_out"), sem("tok_set")
        raw_in = [sem(f"w_raw_in{s}") for s in range(3)]
        whi_d = sem("w_hi_d")
        lo_dve, lo_pool = sem("lo_dve"), sem("lo_pool")
        idx_in, x_in = sem("idx_in"), sem("x_in")
        tr_mm, xhi_d = sem("e_tr_mm"), sem("xhi_d")
        tr_ev = sem("e_tr_ev")
        gu_mm = sem("gu_mm")
        g_d = sem("g_d")
        gu_ev = sem("gu_ev")
        sg_d, t_d, act_d, ahi_d, alo_d = sem("sg_d"), sem("t_d"), sem("act_d"), sem("ahi_d"), sem("alo_d")
        yp_mm = sem("yp_mm")
        yp_ev = sem("yp_ev")
        y_out = sem("e_y_out")
        spare = sem("spare")
        spare_sp, spare_pe = sem("spare_sp"), sem("spare_pe")

        gate_up_v = w_gate_up.rearrange("a e (k p) c -> (a e) p k c", p=P)
        down_v = w_down.rearrange("a e (k p) c -> (a e) p k c", p=P)
        nov_ap = tabs[0:1, NE + MAXOVER:NE + MAXOVER + 1]

        def over_blocks(eng, body, first=0):
            with eng.Fori(first, NE) as b:
                body(b, False)
            nov = eng.value_load(nov_ap, min_val=0, max_val=MAXOVER)
            with eng.Fori(0, MAXOVER) as i:
                with eng.If(i < nov):
                    body(NE + i, True)
            return nov

        def over_expert(eng, b):
            return eng.value_load(tabs[0:1, bass.ds(b, 1)], min_val=0, max_val=NE - 1)

        def chunk_tile(w, c, j, k, part=0):
            if c < 4:
                return w[:, c % 2, :].rearrange("p (h k q) -> p h k q", h=2, k=KD)[:, part, k, j * P:(j + 1) * P]
            return w[:, c % 2, :].rearrange("p (k q) -> p k q", k=KD)[:, k, j * P:(j + 1) * P]

        block = ctx.enter_context(nc.Block())

        @block.sync
        def _(sp):
            sp.dma_start(brow[:, 0:D], b_gate_up[0, :, 0:D]).then_inc(b_in, 16)

            def load(n, c, e):
                s = c % 3
                sp.wait_ge(lo_dve, n + 1)
                sp.wait_ge(lo_pool, n + 1)
                if c < 4:
                    v = raw[:, s, :].rearrange("p (h k q) -> p h k q", h=2, k=KD)
                    for h in range(2):
                        sp.dma_start(v[:, h, :, :], gate_up_v[bass.ds(e, 1), :, :, h * FF + 2 * P * c:h * FF + 2 * P * (c + 1)]
                                     .rearrange("a p k c -> (a p) k c")).then_inc(raw_in[s], 16)
                else:
                    v = raw[:, s, :].rearrange("p (k q) -> p k q", k=KD)
                    for h in range(2):
                        sp.dma_start(v[:, 4 * h:4 * h + 4, :],
                                     down_v[bass.ds(e, 1), :, 4 * h:4 * h + 4, (c - 4) * HALF:(c - 3) * HALF]
                                     .rearrange("a p k c -> (a p) k c")).then_inc(raw_in[s], 16)

            def store(b):
                sp.wait_ge(tr_ev, 8 * b + 8 + 4 + 2)
                sp.dma_start(y_slots[bass.ds(b * CAP, P), :], ytok[:, :]).then_inc(y_out, 16)
                sp.dma_start(y_slots[bass.ds(b * CAP + P, CAP2), :], ytok2[P - CAP2:P, :]).then_inc(y_out, 16)

            def body(b, over):
                e = over_expert(sp, b) if over else b
                for c in range(CHUNKS):
                    load(CHUNKS * b + c, c, e)
                    if c == 3:
                        store(b - 1)
            for c in range(CHUNKS):
                load(c, c, 0)
                if c == 0:
                    for part, src in ((1, b_gate_up[0, :, D:2 * D]), (2, b_down[0, :, :])):
                        sp.wait_ge(b_mm, part)
                        sp.dma_start(brow[:, 0:D], src).then_inc(b_in, 16)
            nov = over_blocks(sp, body, first=1)
            load(CHUNKS * (NE + nov), 0, 0)
            store(nov + (NE - 1))
            sp.wait_ge(y_out, 32 * (NE + nov) + 32)
            sp.sem_inc(spare_sp, 1)

        @block.scalar
        def _(act):
            act.sem_inc(yp_ev, 2)

            def xT_evac(b, r0):
                for g in range(4):
                    act.wait_ge(tr_mm, r0 + g + 1)
                    k = 4 * (g % 2)
                    if g < 2:
                        dst, src = xT_hi[:, k:k + 4, 0:P], tr[:, g % 2, :].rearrange("p (k c) -> p k c", k=4)
                    else:
                        dst = xT_hi[:, k:k + 4, P:CAP]
                        src = tr[:, g % 2, 0:4 * CAP2].rearrange("p (k c) -> p k c", k=4)
                    nc.scalar.activation(dst, src, ACT.Copy).then_inc(xhi_d, 1)

            act.wait_ge(raw_in[0], 32)
            for m in range(0, CW, PIECE):
                nc.scalar.activation(w_hi[:, 0, m:m + PIECE], raw[:, 0, m:m + PIECE], ACT.Copy).then_inc(whi_d, 1)
            xT_evac(0, 0)

            def body(b, over):
                for c in range(CHUNKS):
                    cn = (c + 1) % CHUNKS
                    act.wait_ge(raw_in[cn % 3], 64 * b + 32 * ((c + 1) // 3 + 1))
                    if c == 0:
                        act.wait_ge(yp_mm, KD * b + 1)
                    elif c < 5:
                        act.wait_ge(gu_mm, FT * b + 2 * c)
                    else:
                        act.wait_ge(yp_mm, KD * b + 5)
                    for m in range(0, CW, PIECE):
                        nc.scalar.activation(w_hi[:, cn % 2, m:m + PIECE], raw[:, cn % 3, m:m + PIECE], ACT.Copy)\
                            .then_inc(whi_d, 1)
                    if c < 4:
                        for ft in (2 * c, 2 * c + 1):
                            act.wait_ge(g_d, FT * b + ft + 1)
                            nc.scalar.activation(sg[:, ft % 2, :], gs[:, ft % 2, :], ACT.Sigmoid, scale=ALPHA)\
                                .then_inc(sg_d, 1)
                        for ft in (2 * c, 2 * c + 1):
                            act.wait_ge(act_d, FT * b + ft + 1)
                            nc.scalar.activation(act_hi[:, ft, :], act_f[:, ft, :], ACT.Copy).then_inc(ahi_d, 1)
                    if c == 3:
                        xT_evac(b + 1, 8 * b + 4)
                    if c >= 4:
                        if c == 4:
                            act.wait_ge(b_d, b + 1)
                        for dt in range(4 * (c - 4), 4 * (c - 3)):
                            act.wait_ge(yp_mm, KD * b + dt + 2)
                            nc.scalar.activation(yT[:, dt, :], yp[:, dt % 2, 0:CAP], ACT.Identity,
                                                 bias=bcur[:, 2 * KD + dt:2 * KD + dt + 1]).then_inc(yp_ev, 1)
            over_blocks(act, body)

        @block.gpsimd
        def _(pool):
            pool.sem_inc(lo_pool, 3)
            nc.gpsimd.iota(tokid[:, :], [[P, NT]], base=0, channel_multiplier=1).then_inc(tok_set, 1)
            pool.wait_ge(tok_set, 1)
            for t in range(NT):
                for j in range(TOPK):
                    pool.indirect_dma_start(out=slot_token[:, :], out_offset=bass.IndirectOffsetOnAxis(
                        ap=dest[:, t * TOPK + j:t * TOPK + j + 1], axis=0), in_=tokid[:, t:t + 1],
                        in_offset=None).then_inc(tok_out, 16)
            pool.wait_ge(tok_out, 16 * NT * TOPK)

            def load_idx(b):
                pool.dma_start(idx[:, 0:1].bitcast(I32), slot_token[bass.ds(b * CAP, P), :]).then_inc(idx_in, 16)
                pool.dma_start(idx[0:CAP2, 1:2].bitcast(I32), slot_token[bass.ds(b * CAP + P, CAP2), :]).then_inc(idx_in, 16)

            def gather():
                pool.indirect_dma_start(out=xg[:, :], out_offset=None, in_=xn_s[:, :],
                                        in_offset=bass.IndirectOffsetOnAxis(ap=idx[:, 0:1], axis=0)).then_inc(x_in, 16)
                pool.indirect_dma_start(out=xg2[:, :], out_offset=None, in_=xn_s[:, :],
                                        in_offset=bass.IndirectOffsetOnAxis(ap=idx[0:CAP2, 1:2], axis=0)).then_inc(x_in, 16)

            def split_lo(n, cn):
                pool.wait_ge(whi_d, 4 * n + 4)
                m = POOL_FROM * PIECE
                nc.gpsimd.tensor_tensor(w_lo[:, cn % 2, m:CW], raw[:, cn % 3, m:CW], w_hi[:, cn % 2, m:CW].bitcast(F32),
                                        ALU.subtract).then_inc(lo_pool, 1)

            load_idx(0)
            pool.wait_ge(idx_in, 32)
            gather()
            split_lo(0, 0)
            pool.wait_ge(tr_ev, 6)

            def body(b, over):
                for c in range(CHUNKS):
                    split_lo(CHUNKS * b + c + 1, (c + 1) % CHUNKS)
                    if c == 0:
                        hold(pool, x_in, 32 * b + 32, spare)
                        load_idx(b + 1)
                    if c == 1:
                        hold(pool, idx_in, 32 * b + 64, spare)
                        hold(pool, tr_ev, 8 * b + 2, spare)
                        gather()
                    if c < 4:
                        for ft in (2 * c, 2 * c + 1):
                            pool.wait_ge(ahi_d, FT * b + ft + 1)
                            nc.gpsimd.tensor_tensor(act_lo[:, ft, :], act_f[:, ft, :], act_hi[:, ft, :].bitcast(F32),
                                                    ALU.subtract).then_inc(alo_d, 1)
            over_blocks(pool, body)

        @block.vector
        def _(dve):
            dve.sem_inc(lo_dve, 3)
            dve.sem_inc(gu_ev, 4)
            dve.sem_inc(tr_ev, 2)
            dve.sem_inc(y_out, 32)
            for bank in (gu, yp):
                nc.vector.memset(bank[:, :, :], 0.0).then_inc(ini, 1)

            for part in range(3):
                dve.wait_ge(b_mm, part + 1)
                nc.vector.tensor_scalar(bT[:, part * KD:(part + 1) * KD, :],
                                        tr[:, part % 2, 0:KD * NE].rearrange("p (k e) -> p k e", k=KD),
                                        1.0 if part == 1 else 0.0, None, ALU.add).then_inc(b_ev, 1)

            def split_lo(n, cn):
                for q in range(POOL_FROM):
                    m = q * PIECE
                    dve.wait_ge(whi_d, 4 * n + q + 1)
                    ins = nc.vector.tensor_tensor(w_lo[:, cn % 2, m:m + PIECE], raw[:, cn % 3, m:m + PIECE],
                                                  w_hi[:, cn % 2, m:m + PIECE].bitcast(F32), ALU.subtract)
                ins.then_inc(lo_dve, 1)

            def xT_evac(b):
                for g in range(4):
                    dve.wait_ge(xhi_d, 4 * b + g + 1)
                    k = 4 * (g % 2)
                    cols = slice(0, P) if g < 2 else slice(P, CAP)
                    w = 4 * P if g < 2 else 4 * CAP2
                    nc.vector.tensor_tensor(xT_lo[:, k:k + 4, cols], tr[:, g % 2, 0:w].rearrange("p (k c) -> p k c", k=4),
                                            xT_hi[:, k:k + 4, cols].bitcast(F32), ALU.subtract).then_inc(tr_ev, 1)

            split_lo(0, 0)
            xT_evac(0)

            def body(b, over):
                e = over_expert(dve, b) if over else b
                nc.vector.tensor_copy(bcur[:, :], bT[:, :, bass.ds(e, 1)].rearrange("p k a -> p (k a)")).then_inc(b_d, 1)
                dve.wait_ge(b_d, b + 1)
                for c in range(CHUNKS):
                    split_lo(CHUNKS * b + c + 1, (c + 1) % CHUNKS)
                    if c < 4:
                        for ft in (2 * c, 2 * c + 1):
                            f = FT * b + ft
                            dve.wait_ge(gu_mm, f + 1)
                            nc.vector.tensor_scalar(gs[:, ft % 2, :], gu[:, ft % 4, 0:CAP], bcur[:, ft:ft + 1], LIMIT,
                                                    ALU.add, ALU.min).then_inc(g_d, 1)
                            nc.vector.tensor_scalar(us[:, ft % 2, :], gu[:, ft % 4, 256:256 + CAP],
                                                    bcur[:, KD + ft:KD + ft + 1], 1.0 - LIMIT, ALU.add, ALU.max)\
                                .then_inc(gu_ev, 1)
                        for ft in (2 * c, 2 * c + 1):
                            f = FT * b + ft
                            dve.wait_ge(sg_d, f + 1)
                            nc.vector.tensor_tensor(gs[:, ft % 2, :], gs[:, ft % 2, :], sg[:, ft % 2, :], ALU.mult)\
                                .then_inc(t_d, 1)
                            dve.wait_ge(t_d, f + 1)
                            dve.wait_ge(gu_ev, f + 5)
                            nc.vector.scalar_tensor_tensor(out=act_f[:, ft, :], in0=us[:, ft % 2, :], scalar=1.0 + LIMIT,
                                                           in1=gs[:, ft % 2, :], op0=ALU.min, op1=ALU.mult)\
                                .then_inc(act_d, 1)
                    if c == 3:
                        xT_evac(b + 1)
                dve.wait_ge(y_out, 32 * b + 32)
                for g in range(4):
                    dve.wait_ge(tr_mm, 8 * b + 8 + g + 1)
                    half = (g % 2) * HALF
                    if g < 2:
                        nc.vector.tensor_copy(ytok[:, half:half + HALF], tr[:, g % 2, :]).then_inc(tr_ev, 1)
                    else:
                        nc.vector.tensor_copy(ytok2[P - CAP2:P, half:half + HALF], tr[P - CAP2:P, g % 2, :])\
                            .then_inc(tr_ev, 1)
            over_blocks(dve, body)

        @block.tensor
        def _(pe):
            pe.sem_inc(yp_mm, 1)

            def turn_x(b, r0):
                hold(pe, x_in, 32 * b + 32, spare_pe)
                for g in range(4):
                    hold(pe, tr_ev, r0 + g + 1, spare_pe)
                    src, m = (xg, P) if g < 2 else (xg2, CAP2)
                    for k in range(4):
                        col = (4 * (g % 2) + k) * P
                        last = nc.tensor.transpose(tr[:, g % 2, k * m:(k + 1) * m], src[0:m, col:col + P],
                                                   ident[0:m, 0:m])
                    last.then_inc(tr_mm, 1)

            for part in range(3):
                pe.wait_ge(b_in, 16 * (part + 1))
                after(pe, b_ev, part - 1)
                for k in range(KD):
                    last = nc.tensor.transpose(tr[:, part % 2, k * NE:(k + 1) * NE], brow[:, k * P:(k + 1) * P],
                                               ident[0:NE, 0:NE])
                last.then_inc(b_mm, 1)
            pe.wait_ge(b_ev, 3)
            turn_x(0, 0)
            pe.wait_ge(ini, 2)
            pe.wait_ge(tr_ev, 6)

            def gate_up(b, width):
                for c in range(4):
                    pe.wait_ge(lo_dve, CHUNKS * b + c + 4)
                    pe.wait_ge(lo_pool, CHUNKS * b + c + 4)
                    for j in range(2):
                        ft = 2 * c + j
                        pe.wait_ge(gu_ev, FT * b + ft + 1)
                        for part in range(2):
                            out = gu[:, ft % 4, 256 * part:256 * part + width]
                            for k in range(KD):
                                last = split3(nc, out, chunk_tile(w_hi, c, j, k, part), chunk_tile(w_lo, c, j, k, part),
                                              xT_hi[:, k, 0:width], xT_lo[:, k, 0:width], k == 0, k == KD - 1)
                        last.then_inc(gu_mm, 1)

            def down(b, width):
                for c in (4, 5):
                    pe.wait_ge(lo_dve, CHUNKS * b + c + 4)
                    pe.wait_ge(lo_pool, CHUNKS * b + c + 4)
                    for j in range(4):
                        dt = 4 * (c - 4) + j
                        pe.wait_ge(yp_ev, KD * b + dt + 1)
                        for k in range(KD):
                            if dt == 0:
                                pe.wait_ge(alo_d, FT * b + k + 1)
                            last = split3(nc, yp[:, dt % 2, 0:width], chunk_tile(w_hi, c, j, k), chunk_tile(w_lo, c, j, k),
                                          act_hi[:, k, 0:width], act_lo[:, k, 0:width], k == 0, k == KD - 1)
                        last.then_inc(yp_mm, 1)

            def turn_y(b):
                for g in range(4):
                    hold(pe, tr_ev, 8 * b + 8 + g + 1, spare_pe)
                    hold(pe, yp_ev, KD * b + 4 * (g % 2) + 6, spare_pe)
                    first = 0 if g < 2 else CAP - P
                    for k in range(4):
                        last = nc.tensor.transpose(tr[:, g % 2, k * P:(k + 1) * P],
                                                   yT[:, 4 * (g % 2) + k, first:first + P], ident[:, :])
                    last.then_inc(tr_mm, 1)

            def multiply(b, width):
                gate_up(b, width)
                turn_x(b + 1, 8 * b + 4)
                down(b, width)
                turn_y(b)

            def body(b, over):
                if over:
                    multiply(b, CAP)
                    return
                count = pe.value_load(tabs[0:1, bass.ds(b, 1)], min_val=0, max_val=T)
                with pe.If(count < WIDTHS[0] + 1):
                    multiply(b, WIDTHS[0])
                with pe.Else():
                    with pe.If(count < WIDTHS[1] + 1):
                        multiply(b, WIDTHS[1])
                    with pe.Else():
                        multiply(b, WIDTHS[2])
            over_blocks(pe, body)


def combine(nc, h_s, y_slots, gates, dest, out):
    SLOTS_ = 2
    with ExitStack() as ctx:
        sb = lambda n, s, d=F32: ctx.enter_context(nc.sbuf_tensor(n, s, d))
        sem = lambda n: ctx.enter_context(nc.semaphore(n))
        hbuf = sb("co_h", [P, NT, D])
        y = sb("co_y", [P, SLOTS_, TOPK, D])
        acc = sb("co_acc", [P, NT, 2, D])
        h_in = [sem(f"co_h_in{t}") for t in range(NT)]
        y_in = [sem(f"co_y_in{s}") for s in range(SLOTS_)]
        add_d, sum_d, y_out = sem("co_add"), sem("co_sum"), sem("co_out")
        out_t = out.rearrange("a (t p) d -> (a t) p d", p=P)
        h_t = h_s.rearrange("(t p) d -> t p d", p=P)
        with nc.Block() as block:
            @block.sync
            def _(sp):
                for t in range(NT):
                    sp.dma_start(hbuf[:, t, :], h_t[t]).then_inc(h_in[t], 16)
                for t in range(NT):
                    sp.wait_ge(sum_d, t + 1)
                    sp.dma_start(out_t[t], acc[:, t, 1, :]).then_inc(y_out, 16)
                sp.wait_ge(y_out, 16 * NT)

            @block.gpsimd
            def _(pool):
                for t in range(NT):
                    if t >= SLOTS_:
                        pool.wait_ge(sum_d, t - SLOTS_ + 1)
                    for j in range(TOPK):
                        pool.indirect_dma_start(out=y[:, t % SLOTS_, j, :], out_offset=None, in_=y_slots[:, :],
                                                in_offset=bass.IndirectOffsetOnAxis(
                                                    ap=dest[:, t * TOPK + j:t * TOPK + j + 1], axis=0))\
                            .then_inc(y_in[t % SLOTS_], 16)

            @block.vector
            def _(dve):
                for t in range(NT):
                    dve.wait_ge(h_in[t], 16)
                    dve.wait_ge(y_in[t % SLOTS_], 16 * TOPK * (t // SLOTS_ + 1))
                    for j in range(TOPK):
                        if j:
                            dve.wait_ge(add_d, (TOPK - 1) * t + j)
                        src = hbuf[:, t, :] if j == 0 else acc[:, t, (j - 1) % 2, :]
                        nc.vector.scalar_tensor_tensor(out=acc[:, t, j % 2, :], in0=y[:, t % SLOTS_, j, :],
                                                       scalar=gates[:, t, j:j + 1], in1=src,
                                                       op0=ALU.mult, op1=ALU.add)\
                            .then_inc(sum_d if j == TOPK - 1 else add_d, 1)


def build(nc, x, attn_norm_w, w_in, q_norm_w, k_norm_w, sinks, w_proj_swa, w_proj_sb, w_out, ffn_norm_w,
          router_w, router_b, w_gate_up, b_gate_up, w_down, b_down, out):
    dram = lambda n, s, d=F32: nc.dram_tensor(n, s, d, kind="Internal").ap()
    gT = dram("gT", (2 * KD, P, T))
    y_s = dram("y_s", (2, T, PAIRS * P))
    h_s = dram("h_s", (T, D))
    xn_s = dram("xn_s", (T, D))
    slot_token = dram("slot_token", (TABLE, 1), I32)
    y_slots = dram("y_slots", (NBLK * CAP, D))
    with ExitStack() as top:
        sbt = lambda n, s, d=F32: top.enter_context(nc.sbuf_tensor(n, s, d))
        ident = sbt("ident", [P, P])
        eps_col = sbt("eps_col", [P, 1])
        nhalf = sbt("nhalf", [P, 1])
        logits = sbt("logits", [P, NT, NE])
        gates = sbt("gates", [P, NT, TOPK])
        dest = sbt("dest", [P, NT * TOPK], U32)
        tabs = sbt("tabs", [1, NE + MAXOVER + 1], I32)
        make_constants(nc, ident, eps_col, nhalf)
        with ExitStack() as front:
            sbf = lambda n, s, d=F32: front.enter_context(nc.sbuf_tensor(n, s, d))
            xnT_hi = sbf("xnT_hi", [P, KD, T], F32R)
            xnT_lo = sbf("xnT_lo", [P, KD, T], F32R)
            norm_and_transpose(nc, x, attn_norm_w, ident, nhalf, xnT_hi, xnT_lo)
            va = sbf("va", [P, NT, PAIRS * HD])
            vb = sbf("vb", [P, NT, PAIRS * P])
            project_values(nc, w_in, xnT_hi, xnT_lo, va, vb)
            attention(nc, w_in, q_norm_w, k_norm_w, sinks, ident, eps_col, xnT_hi, xnT_lo, va, vb, gT,
                      y_s, y_slots)
        with ExitStack() as mid:
            sbm = lambda n, s, d=F32: mid.enter_context(nc.sbuf_tensor(n, s, d))
            mT_hi = sbm("mT_hi", [P, KD, T], F32R)
            mT_lo = sbm("mT_lo", [P, KD, T], F32R)
            merge(nc, w_proj_swa, w_proj_sb, ident, gT, y_s, mT_hi, mT_lo)
            output_and_logits(nc, x, w_out, ffn_norm_w, router_w, router_b, ident, nhalf, mT_hi, mT_lo,
                              h_s, xn_s, logits)
        route(nc, logits, gates, dest, tabs, slot_token)
        experts(nc, xn_s, w_gate_up, b_gate_up, w_down, b_down, ident, dest, tabs, slot_token, y_slots)
        combine(nc, h_s, y_slots, gates, dest, out)


_INS = ["x", "attn_norm_w", "w_in", "q_norm_w", "k_norm_w", "sinks", "w_proj_swa", "w_proj_sb", "w_out",
        "ffn_norm_w", "router_w", "router_b", "w_gate_up", "b_gate_up", "w_down", "b_down"]


def kernel(**inputs):
    import numpy as _np
    import concourse.bacc as _bacc
    from concourse import mybir as _mybir
    from concourse.bass_utils import run_bass_kernel_spmd as _run

    nc = _bacc.Bacc("TRN2", target_bir_lowering=False, num_devices=1)
    arrays, args = {}, []
    for name in _INS:
        a = _np.ascontiguousarray(inputs[name])
        arrays[f"in_{name}_dram"] = a
        args.append(nc.dram_tensor(f"in_{name}_dram", a.shape, _mybir.dt.from_np(a.dtype), kind="ExternalInput").ap())
    args.append(nc.dram_tensor("out_0_dram", (1, T, D), _mybir.dt.float32, kind="ExternalOutput").ap())
    build(nc, *args)
    r = _run(nc, [arrays], core_ids=[0])
    return r.results[0]["out_0_dram"]
```

```python
from contextlib import ExitStack

import concourse.bass as bass
from concourse import mybir

F32 = mybir.dt.float32
F32R = mybir.dt.float32r
BF16 = mybir.dt.bfloat16
I32 = mybir.dt.int32
U32 = mybir.dt.uint32
ALU = mybir.AluOpType
ACT = mybir.ActivationFunctionType
AX_X = mybir.AxisListType.X

P = 128
T = 1024
D = 1024
NT = T // P
KD = D // P
HALF = 512
HD = 64
PAIRS = 4
WIN = 128
QA, KA, VA, QB, KB, VB, GA = 0, 512, 640, 768, 1280, 1792, 2304
IN_WIDTH = 4352
EPS = 1e-5
SCALE = HD ** -0.5
NEG = -1.0e30

NE = 32
TOPK = 4
FF = 1024
LIMIT = 7.0
ALPHA = 1.702
CAP = 160
CAP2 = CAP - P
MAXOVER = (T * TOPK) // CAP
NBLK = NE + MAXOVER
WIDTHS = (128, 136, 144, 152, CAP)


def after(eng, sem, n):
    if not isinstance(n, int) or n > 0:
        eng.wait_ge(sem, n)


def split3(nc, out, w_hi, w_lo, x_hi, x_lo, first, last):
    nc.tensor.matmul(out, w_hi, x_hi, start=first, stop=False)
    nc.tensor.matmul(out, w_hi, x_lo, start=False, stop=False)
    return nc.tensor.matmul(out, w_lo, x_hi, start=False, stop=last)


def make_constants(nc, ident, eps_col, nhalf):
    with ExitStack() as ctx:
        cst = ctx.enter_context(nc.semaphore("cst_zeroed"))
        cst2 = ctx.enter_context(nc.semaphore("cst_done"))
        with nc.Block() as block:
            @block.gpsimd
            def _(pool):
                pool.memset(ident[:, :], 0.0).then_inc(cst, 1)
                pool.memset(eps_col[:, :], EPS).then_inc(cst, 1)
                pool.memset(nhalf[:, :], -0.5).then_inc(cst, 1)
                pool.wait_ge(cst, 3)
                pool.affine_select(out=ident[:, :], in_=ident[:, :], compare_op=ALU.not_equal, fill=1.0,
                                   base=0, pattern=[[-1, P]], channel_multiplier=1).then_inc(cst2, 1)
                pool.wait_ge(cst2, 1)


def norm_and_transpose(nc, x, attn_norm_w, ident, nhalf, xnT_hi, xnT_lo):
    with ExitStack() as ctx:
        sb = lambda n, s, d=F32: ctx.enter_context(nc.sbuf_tensor(n, s, d))
        sem = lambda n: ctx.enter_context(nc.semaphore(n))
        xin = sb("n1_x", [P, NT, D])
        wB = sb("n1_w", [P, D])
        xs = sb("n1_xs", [P, 2, D])
        junk = sb("n1_junk", [P, D])
        ssq = sb("n1_ssq", [P, NT])
        ms = sb("n1_ms", [P, NT])
        rstd = sb("n1_rstd", [P, NT])
        tr = ctx.enter_context(nc.psum_tensor("n1_tr", [P, 4, HALF], F32))
        x_in = [sem(f"n1_x_in{t}") for t in range(NT)]
        w_in_ = sem("n1_w_in")
        sq_done, ms_done, rstd_done = sem("n1_sq"), sem("n1_ms_d"), sem("n1_rstd_d")
        xs_done, tr_done, hi_done, lo_done = sem("n1_xs_d"), sem("n1_tr_d"), sem("n1_hi"), sem("n1_lo")
        x_t = x.rearrange("a (t p) d -> (a t) p d", p=P)
        with nc.Block() as block:
            @block.sync
            def _(sp):
                for t in range(NT):
                    sp.dma_start(xin[:, t, :], x_t[t]).then_inc(x_in[t], 16)
                    if t == 0:
                        sp.dma_start(wB[:, :], attn_norm_w[0:1, :].to_broadcast([P, D])).then_inc(w_in_, 16)

            @block.scalar
            def _(act):
                for t in range(NT):
                    act.wait_ge(x_in[t], 16)
                    if t:
                        act.wait_ge(sq_done, t)
                    nc.scalar.activation(junk[:, :], xin[:, t, :], ACT.Square,
                                         accum_out=ssq[:, t:t + 1]).then_inc(sq_done, 1)
                for m in range(2 * NT):
                    t, g = divmod(m, 2)
                    act.wait_ge(tr_done, m + 1)
                    nc.scalar.activation(xnT_hi[:, 4 * g:4 * g + 4, t * P:(t + 1) * P],
                                         tr[:, m % 4, :].rearrange("p (k c) -> p k c", k=4),
                                         ACT.Copy).then_inc(hi_done, 1)

            @block.gpsimd
            def _(pool):
                for t in range(NT):
                    pool.wait_ge(sq_done, t + 1)
                    nc.gpsimd.tensor_scalar(ms[:, t:t + 1], ssq[:, t:t + 1], 1.0 / D, EPS,
                                            ALU.mult, ALU.add).then_inc(ms_done, 1)
                    pool.wait_ge(ms_done, t + 1)
                    nc.gpsimd.tensor_tensor(rstd[:, t:t + 1], ms[:, t:t + 1], nhalf[:, 0:1],
                                            ALU.pow).then_inc(rstd_done, 1)

            @block.vector
            def _(dve):
                def scale_tile(t):
                    if t == 0:
                        dve.wait_ge(w_in_, 16)
                    dve.wait_ge(rstd_done, t + 1)
                    after(dve, tr_done, 2 * (t - 1))
                    nc.vector.scalar_tensor_tensor(out=xs[:, t % 2, :], in0=xin[:, t, :], scalar=rstd[:, t:t + 1],
                                                   in1=wB[:, :], op0=ALU.mult, op1=ALU.mult).then_inc(xs_done, 1)
                scale_tile(0)
                for t in range(NT):
                    if t + 1 < NT:
                        scale_tile(t + 1)
                    for g in range(2):
                        m = 2 * t + g
                        dve.wait_ge(hi_done, m + 1)
                        nc.vector.tensor_tensor(xnT_lo[:, 4 * g:4 * g + 4, t * P:(t + 1) * P],
                                                tr[:, m % 4, :].rearrange("p (k c) -> p k c", k=4),
                                                xnT_hi[:, 4 * g:4 * g + 4, t * P:(t + 1) * P].bitcast(F32),
                                                ALU.subtract).then_inc(lo_done, 1)

            @block.tensor
            def _(pe):
                for m in range(2 * NT):
                    t, g = divmod(m, 2)
                    pe.wait_ge(xs_done, t + 1)
                    after(pe, lo_done, m - 3)
                    for k in range(4):
                        last = nc.tensor.transpose(tr[:, m % 4, k * P:(k + 1) * P],
                                                   xs[:, t % 2, (4 * g + k) * P:(4 * g + k + 1) * P], ident[:, :])
                    last.then_inc(tr_done, 1)


def project_values(nc, w_in, xnT_hi, xnT_lo, va, vb):
    with ExitStack() as ctx:
        sb = lambda n, s, d=F32: ctx.enter_context(nc.sbuf_tensor(n, s, d))
        sem = lambda n: ctx.enter_context(nc.semaphore(n))
        raw = sb("pv_raw", [P, KD, HALF])
        raw_a = sb("pv_raw_a", [P, KD, P])
        w_hi = sb("pv_whi", [P, KD, HALF], F32R)
        w_lo = sb("pv_wlo", [P, KD, HALF], F32R)
        wa_hi = sb("pv_wahi", [P, KD, P], F32R)
        wa_lo = sb("pv_walo", [P, KD, P], F32R)
        acc = ctx.enter_context(nc.psum_tensor("pv_acc", [P, 4, HALF], F32))
        a_in, b_in = sem("pv_a_in"), sem("pv_b_in")
        hi_done, lo_done, mm_done, ev_done = sem("pv_hi"), sem("pv_lo"), sem("pv_mm"), sem("pv_ev")
        ev_even = sem("pv_ev_even")
        w_v = w_in.rearrange("a (k p) c -> p (a k) c", p=P)

        def evacuate(eng, n):
            eng.wait_ge(mm_done, n + 1)
            if n < NT:
                src = acc[:, n % 4, 0:P].rearrange("p (a o c) -> p a o c", a=2, o=1).to_broadcast([P, 2, 2, HD])
                dst = va[:, n, :].rearrange("p (a o c) -> p a o c", a=2, o=2)
            else:
                src, dst = acc[:, n % 4, :], vb[:, n - NT, :]
            if n % 2:
                nc.vector.tensor_copy(dst, src).then_inc(ev_done, 1)
            else:
                nc.scalar.activation(dst, src, ACT.Copy).then_inc(ev_even, 1)

        with nc.Block() as block:
            @block.sync
            def _(sp):
                sp.dma_start(raw_a[:, :, :], w_v[:, :, VA:VA + P]).then_inc(a_in, 16)
                sp.dma_start(raw[:, :, :], w_v[:, :, VB:VB + HALF]).then_inc(b_in, 16)

            @block.scalar
            def _(act):
                act.wait_ge(a_in, 16)
                nc.scalar.activation(wa_hi[:, :, :], raw_a[:, :, :], ACT.Copy).then_inc(hi_done, 1)
                act.wait_ge(b_in, 16)
                for k in range(0, KD, 2):
                    nc.scalar.activation(w_hi[:, k:k + 2, :], raw[:, k:k + 2, :], ACT.Copy).then_inc(hi_done, 1)
                for n in range(0, 2 * NT, 2):
                    evacuate(act, n)


            @block.vector
            def _(dve):
                dve.wait_ge(hi_done, 1)
                nc.vector.tensor_tensor(wa_lo[:, :, :], raw_a[:, :, :], wa_hi[:, :, :].bitcast(F32),
                                        ALU.subtract).then_inc(lo_done, 1)
                for k in range(0, KD, 2):
                    dve.wait_ge(hi_done, 2 + k // 2)
                    nc.vector.tensor_tensor(w_lo[:, k:k + 2, :], raw[:, k:k + 2, :],
                                            w_hi[:, k:k + 2, :].bitcast(F32), ALU.subtract).then_inc(lo_done, 1)
                for n in range(1, 2 * NT, 2):
                    evacuate(dve, n)

            @block.tensor
            def _(pe):
                for n in range(2 * NT):
                    if n == 0:
                        pe.wait_ge(lo_done, 1)
                    if n == NT:
                        pe.wait_ge(lo_done, 1 + KD // 2)
                    if n >= 4:
                        pe.wait_ge(ev_done if n % 2 else ev_even, n // 2 - 1)
                    t = n % NT
                    for k in range(KD):
                        wh, wl, out = ((wa_hi[:, k, :], wa_lo[:, k, :], acc[:, n % 4, 0:P]) if n < NT else
                                       (w_hi[:, k, :], w_lo[:, k, :], acc[:, n % 4, :]))
                        last = split3(nc, out, xnT_hi[:, k, t * P:(t + 1) * P], xnT_lo[:, k, t * P:(t + 1) * P],
                                      wh, wl, k == 0, k == KD - 1)
                    last.then_inc(mm_done, 1)


def hold(eng, sem, value, spare):
    eng.wait_ge(sem, value)
    eng.sem_inc(spare, 1)


SB_UNITS = [("sb", i, (h,)) for i in range(NT - 1, NT // 2 - 1, -1) for h in range(2)] + \
           [("sb", i, (0, 1)) for i in range(NT // 2 - 1, -1, -1)]
SWA_UNITS = [("swa", n, (0, 1)) for n in range(NT)]
UNITS = SB_UNITS + SWA_UNITS
NU, NSB, NSWA = len(UNITS), len(SB_UNITS), len(SWA_UNITS)


def unit_tiles(unit):
    kind, i, heads = unit
    first = max(i - 1, 0) if kind == "swa" else 0
    return [(s, kb) for s in range(len(heads)) for kb in range(first, i + 1)]


GROUPS = [-(-len(unit_tiles(u)) // 4) for u in UNITS]
GROUP0 = [sum(GROUPS[:n]) for n in range(NU)]
NG = sum(GROUPS)
PAIR_TILES = ["qa", "ka", "qb", "kb"]
GATE_TILES = ["g"] * 4


def attention(nc, w_in, q_norm_w, k_norm_w, sinks, ident, eps_col, xnT_hi, xnT_lo, va, vb, gT, y_s,
              y_slots):
    with ExitStack() as ctx:
        sb = lambda n, s, d=F32: ctx.enter_context(nc.sbuf_tensor(n, s, d))
        sem = lambda n: ctx.enter_context(nc.semaphore(n))
        ps = lambda n, s: ctx.enter_context(nc.psum_tensor(n, s, F32))
        raw = sb("at_raw", [P, 2, KD, P])
        w_hi = sb("at_whi", [P, 2, KD, P], F32R)
        w_lo = sb("at_wlo", [P, 2, KD, P], F32R)
        cur = {k: sb(f"at_cur_{k}", [P, T]) for k in PAIR_TILES}
        nxt = {k: sb(f"at_nxt_{k}", [P, T]) for k in PAIR_TILES}
        t1 = sb("at_t1", [P, 2, 2 * HALF])
        soft = sb("at_soft", [P, 2, 2 * HALF])
        logw = sb("at_logw", [P, 2, 2 * HALF])
        prob = sb("at_prob", [P, 2, 2 * HALF])
        probT = sb("at_probT", [P, 2, 8, P])
        sq = sb("at_sq", [P, HALF])
        rs = sb("at_rs", [P, HALF])
        gst = sb("at_gst", [P, 2, HALF])
        yst = sb("at_yst", [P, 2, P])
        bias = sb("at_bias", [P, 8, 2 * P])
        rel = sb("at_rel", [P, 2 * P])
        ones_blk = sb("at_ones_blk", [P, P])
        one_col = sb("at_one", [P, 1])
        wcol = sb("at_wcol", [P, 2])
        sinkB = sb("at_sink", [P, 8])
        nsinkB = sb("at_nsink", [P, 8])
        stat = {k: sb(f"at_{k}", [P, 2, 2]) for k in ("mx", "negm", "dsink", "rsum", "esink", "den", "rden")}
        z = ps("at_z", [P, 4, HALF])
        job = ps("at_job", [P, HALF])
        aux = ps("at_aux", [P, HALF])
        tr = ps("at_tr", [P, HALF])
        pv = ps("at_pv", [P, HALF])

        ZW = 500
        zeros = sb("at_zeros", [P, 1, ZW])
        z_out = sem("z_out")
        c_in, c_set, c_rel, c_bias, c_sink = (sem(n) for n in ("c_in", "c_set", "c_rel", "c_bias", "c_sink"))
        raw_in = [sem(f"raw_in{s}") for s in range(2)]
        whi_d, wlo_d = sem("whi_d"), sem("wlo_d")
        job_mm = sem("job_mm")
        job_ev = sem("job_ev")
        sq_d, ss_d, rs_d = sem("sq_d"), sem("ss_d"), sem("rs_d")
        g_out = [sem(f"g_out{s}") for s in range(2)]
        s_done = sem("s_done")
        z_free = sem("z_free")
        a_st = sem("a_st")
        d_soft = sem("d_soft")
        p_soft = sem("p_soft")
        d_scan = sem("d_scan")
        w_st = sem("w_st")
        a2_done = sem("a2_done")
        p_prob = sem("p_prob")
        tr_mm = sem("tr_mm")
        tr_ev = sem("tr_ev")
        pv_mm = sem("pv_mm")
        y_ev = sem("y_ev")
        y_out = [sem(f"y_out{s}") for s in range(2)]
        cur_d, cur_a = sem("cur_d"), sem("cur_a")
        spare_pool, spare_end = sem("spare_pool"), sem("spare_end")

        w_v = w_in.rearrange("a (k p) c -> p (a k) c", p=P)
        slot = lambda u: u % 2
        width = lambda unit: P * (unit[1] + 1)

        def zsl(u):
            kind, i, heads = UNITS[u]
            s = slot(u)
            if kind == "swa":
                return z[:, 2 * s:2 * s + 2, (0 if i else P):2 * P]
            if len(heads) == 2:
                return z[:, 2 * s:2 * s + 2, 0:width(UNITS[u])]
            return z[:, 2 * s:2 * s + 2, :].rearrange("p a c -> p (a c)")[:, 0:width(UNITS[u])]

        def bsl(buf, u):
            kind, i, heads = UNITS[u]
            s = slot(u)
            if kind == "swa":
                return buf[:, s, :].rearrange("p (a c) -> p a c", a=2)[:, :, (0 if i else P):2 * P]
            if len(heads) == 2:
                return buf[:, s, :].rearrange("p (a c) -> p a c", a=2)[:, :, 0:width(UNITS[u])]
            return buf[:, s, 0:width(UNITS[u])]

        def head_sl(buf, u, hs):
            v = bsl(buf, u)
            return v if len(UNITS[u][2]) == 1 else v[:, hs, :]

        def diag(buf, u):
            w = width(UNITS[u])
            v = bsl(buf, u)
            return v[:, w - P:w] if len(UNITS[u][2]) == 1 else v[:, :, w - P:w]

        block = ctx.enter_context(nc.Block())
        steps_full = {u: u for u in range(16)}
        steps_last = {2 * n: n for n in range(8)}

        def over_pairs(eng, body):
            with eng.Fori(0, PAIRS - 1) as p:
                body(p, PAIR_TILES + GATE_TILES, steps_full)
            body(PAIRS - 1, GATE_TILES, steps_last)

        @block.sync
        def _(sp):
            sp.dma_start(wcol[0:HD, 0:1], q_norm_w.rearrange("a (c b) -> (a c) b", b=1)).then_inc(c_in, 16)
            sp.dma_start(wcol[HD:P, 0:1], q_norm_w.rearrange("a (c b) -> (a c) b", b=1)).then_inc(c_in, 16)
            sp.dma_start(wcol[0:HD, 1:2], k_norm_w.rearrange("a (c b) -> (a c) b", b=1)).then_inc(c_in, 16)
            sp.dma_start(wcol[HD:P, 1:2], k_norm_w.rearrange("a (c b) -> (a c) b", b=1)).then_inc(c_in, 16)
            sp.dma_start(sinkB[:, :], sinks[0:1, :].to_broadcast([P, 8])).then_inc(c_in, 16)
            for s in range(2):
                sp.sem_inc(g_out[s], 16)

            def load(f, kind, pair, kvh, tl):
                s = tl % 2
                sp.wait_ge(wlo_d, f + 1)
                if kind == "ka":
                    for d in range(2):
                        sp.dma_start(raw[:, s, :, d * HD:(d + 1) * HD],
                                     w_v[:, :, bass.ds(KA + HD * kvh, HD)]).then_inc(raw_in[s], 16)
                    return
                col = {"qa": QA + P * pair, "qb": QB + P * pair, "kb": KB + P * pair, "g": GA + P * pair}[kind]
                sp.dma_start(raw[:, s, :, :], w_v[:, :, bass.ds(col, P)]).then_inc(raw_in[s], 32)

            for tl, kind in enumerate(PAIR_TILES):
                load(tl, kind, 0, 0, tl)

            def body(p, tiles, steps, kvh_next):
                fb = 4 + 8 * p

                def ld(tl):
                    kind = tiles[tl]
                    gate = tl - (len(tiles) - len(GATE_TILES))
                    load(fb + tl, kind, 4 * p + gate if kind == "g" else p + 1, kvh_next, tl)

                ld(0)
                for tl, kind in enumerate(tiles):
                    if tl + 1 < len(tiles):
                        ld(tl + 1)
                    if kind == "g":
                        g = 4 * p + tl - (len(tiles) - len(GATE_TILES))
                        for half in range(2):
                            sp.wait_ge(job_ev, 2 * (fb + tl) + half + 2)
                            sp.dma_start(gT[bass.ds(g, 1), :, half * HALF:(half + 1) * HALF].rearrange("a p c -> (a p) c"),
                                         gst[:, half, :]).then_inc(g_out[half], 16)

            body(0, PAIR_TILES + GATE_TILES, steps_full, 0)
            with sp.Fori(1, PAIRS - 1) as p:
                body(p, PAIR_TILES + GATE_TILES, steps_full, 1)
            body(PAIRS - 1, GATE_TILES, steps_last, 1)
            for s in range(2):
                sp.wait_ge(g_out[s], 16 * (16 + 1))

        @block.scalar
        def _(act):
            act.preload_act_table_set("natural_log_exp_and_others")
            act.sem_inc(a2_done, 2)
            act.sem_inc(tr_ev, 1)
            act.sem_inc(job_ev, 1)
            for s in range(2):
                act.sem_inc(y_out[s], 16)

            def split_hi(f, tl):
                s = tl % 2
                act.wait_ge(raw_in[s], 16 * (f + 2 - tl % 2))
                act.wait_ge(job_mm, 2 * f + 2)
                nc.scalar.activation(w_hi[:, s, :, :], raw[:, s, :, :], ACT.Copy).then_inc(whi_d, 1)

            def finish_job(j, jl, kind, nidx, g):
                half = jl % 2
                act.wait_ge(job_mm, j + 5)
                if kind in ("qb", "kb"):
                    nc.scalar.activation(nxt[kind][:, half * HALF:(half + 1) * HALF], job[:, :], ACT.Copy,
                                         scale=SCALE if kind == "qb" else 1.0).then_inc(job_ev, 1)
                elif kind == "g":
                    act.wait_ge(g_out[half], 16 * (g + 1))
                    nc.scalar.activation(gst[:, half, :], job[:, :], ACT.Copy).then_inc(job_ev, 1)
                else:
                    nc.scalar.activation(sq[:, :], job[:, :], ACT.Square).then_inc(sq_d, 1)

            def finish_norm(nidx):
                act.wait_ge(ss_d, nidx + 1)
                nc.scalar.activation(rs[:, :], aux[:, :], ACT.Ln, bias=eps_col[:, 0:1], scale=1.0 / HD)\
                    .then_inc(rs_d, 1)
                act.wait_ge(rs_d, 2 * nidx + 1)
                nc.scalar.activation(rs[:, :], rs[:, :], ACT.Exp, scale=-0.5).then_inc(rs_d, 1)

            def promote(p, j_last):
                after(act, s_done, NU * p)
                act.wait_ge(job_ev, j_last + 2)
                for kind in ("qb", "kb"):
                    nc.scalar.activation(cur[kind][:, :], nxt[kind][:, :], ACT.Copy).then_inc(cur_a, 1)

            def a1(p, u):
                if UNITS[u][0] != "sb":
                    return
                v = NSB * p + u
                act.wait_ge(s_done, NU * p + u + 1)
                act.wait_ge(d_soft, v + 1)
                nc.scalar.activation(bsl(t1, u), zsl(u), ACT.Abs).then_inc(a_st, 1)
                act.wait_ge(a_st, 3 * v + 1)
                nc.scalar.activation(bsl(t1, u), bsl(t1, u), ACT.Exp, scale=-1.0).then_inc(a_st, 1)
                act.wait_ge(a_st, 3 * v + 2)
                nc.scalar.activation(bsl(t1, u), bsl(t1, u), ACT.Ln, bias=1.0).then_inc(a_st, 1)

            def a2(p, u):
                s = slot(u)
                act.wait_ge(pv_mm, NU * p + u + 1)
                if UNITS[u][0] == "sb":
                    act.wait_ge(z_free, NU * p + u + 3)
                    nc.scalar.activation(bsl(prob, u), bsl(logw, u), ACT.Exp).then_inc(a2_done, 1)
                    return
                w = NSWA * p + u - NSB
                act.wait_ge(w_st, 5 * w + 3)
                for h in range(2):
                    nc.scalar.activation(head_sl(prob, u, h), head_sl(logw, u, h), ACT.Exp,
                                         bias=stat["negm"][:, s, h:h + 1], accum_out=stat["rsum"][:, s, h:h + 1])
                nc.scalar.activation(stat["esink"][:, s, :], stat["dsink"][:, s, :], ACT.Exp).then_inc(a2_done, 1)

            def evac_tr(p, u):
                tiles = unit_tiles(UNITS[u])
                for g in range(GROUPS[u]):
                    n = min(4, len(tiles) - 4 * g)
                    act.wait_ge(tr_mm, NG * p + GROUP0[u] + g + 1)
                    nc.scalar.activation(probT[:, slot(u), 4 * g:4 * g + n, :].rearrange("p a c -> p (a c)"),
                                         tr[:, 0:n * P], ACT.Copy).then_inc(tr_ev, 1)

            def store_y(p, u):
                kind, i, heads = UNITS[u]
                s, n = slot(u), len(heads) * HD
                act.wait_ge(y_ev, NU * p + u + 2)
                act.dma_start(y_s[1 if kind == "sb" else 0, i * P:(i + 1) * P, bass.ds(P * p + HD * heads[0], n)],
                              yst[:, s, 0:n]).then_inc(y_out[s], 16)

            for jl in range(8):
                if jl % 2 == 0:
                    split_hi(jl // 2, jl // 2)
                finish_job(jl, jl, PAIR_TILES[jl // 2], jl, 0)
                if jl < 4:
                    finish_norm(jl)
            promote(0, 7)

            def body(p, tiles, steps):
                fb = 4 + 8 * p
                split_hi(fb, 0)
                a1(p, 0)
                for u in range(NU):
                    if u + 1 < NU:
                        a1(p, u + 1)
                    if u:
                        store_y(p, u - 1)
                    a2(p, u)
                    if u in steps:
                        jl = steps[u]
                        tl = jl // 2
                        if jl % 2 == 0 and tl + 1 < len(tiles):
                            split_hi(fb + tl + 1, tl + 1)
                        finish_job(2 * fb + jl, jl, tiles[tl], None, 4 * p + tl - (len(tiles) - 4))
                    evac_tr(p, u)
                    if u in steps and tiles[steps[u] // 2] in ("qa", "ka"):
                        finish_norm(4 + 4 * p + steps[u])
                store_y(p, NU - 1)
                if len(tiles) > 4:
                    promote(p + 1, 2 * fb + 7)
            over_pairs(act, body)
            for s in range(2):
                act.wait_ge(y_out[s], 16 * (NU // 2 * PAIRS + 1))

        @block.gpsimd
        def _(pool):
            pool.sem_inc(wlo_d, 2)
            nc.gpsimd.memset(ones_blk[:, :], 0.0).then_inc(c_set, 1)
            nc.gpsimd.memset(one_col[:, :], 1.0).then_inc(c_set, 1)
            nc.gpsimd.memset(zeros[:, :, :], 0.0).then_inc(c_set, 1)
            pool.wait_ge(c_set, 3)
            for h in range(2):
                nc.gpsimd.memset(ones_blk[h * HD:(h + 1) * HD, h * HD:(h + 1) * HD], 1.0).then_inc(c_set, 1)
                pool.wait_ge(c_set, 4 + h)

            def split_lo(f, tl):
                s = tl % 2
                pool.wait_ge(whi_d, f + 1)
                nc.gpsimd.tensor_tensor(w_lo[:, s, :, :], raw[:, s, :, :], w_hi[:, s, :, :].bitcast(F32),
                                        ALU.subtract).then_inc(wlo_d, 1)

            split_lo(0, 0)
            nc.gpsimd.iota(rel[:, :], [[-1, 2 * P]], base=P, channel_multiplier=1,
                           allow_small_or_imprecise_dtypes=True).then_inc(c_rel, 1)
            pool.wait_ge(c_rel, 1)
            for h in range(8):
                nc.gpsimd.tensor_scalar(bias[:, h, :], rel[:, :], -(2.0 ** -(h + 1)), None, ALU.mult).then_inc(c_bias, 1)
            pool.wait_ge(c_bias, 8)
            nc.gpsimd.affine_select(out=bias[:, :, :], in_=bias[:, :, :], compare_op=ALU.is_ge, fill=NEG, base=P,
                                    pattern=[[0, 8], [-1, 2 * P]], channel_multiplier=1).then_inc(c_bias, 1)
            pool.wait_ge(c_bias, 9)
            nc.gpsimd.affine_select(out=bias[:, :, :], in_=bias[:, :, :], compare_op=ALU.is_ge, fill=NEG, base=-1,
                                    pattern=[[0, 8], [1, 2 * P]], channel_multiplier=-1).then_inc(c_bias, 1)
            for tl in range(1, 4):
                split_lo(tl, tl)
            further = y_slots[NE * CAP:NBLK * CAP, :].rearrange("r c -> (r c)").rearrange("(p n c) -> p n c", p=P, c=ZW)
            pool.dma_start(further, zeros[:, :, :].to_broadcast([P, MAXOVER * CAP * D // (P * ZW), ZW])).then_inc(z_out, 16)

            def mask(buf, u, done):
                d = diag(buf, u)
                pat = [[-1, P]] if len(UNITS[u][2]) == 1 else [[0, 2], [-1, P]]
                nc.gpsimd.affine_select(out=d, in_=d, compare_op=ALU.is_gt, fill=0.0, base=0, pattern=pat,
                                        channel_multiplier=1).then_inc(done, 1)

            def body(p, tiles, steps):
                fb = 4 + 8 * p
                split_lo(fb, 0)
                for u in range(NU):
                    if UNITS[u][0] == "sb":
                        v = NSB * p + u
                        hold(pool, d_soft, v + 3, spare_pool)
                        mask(soft, u, p_soft)
                        hold(pool, a2_done, NU * p + u + 3, spare_pool)
                        mask(prob, u, p_prob)
                    if u in steps and steps[u] % 2 == 0 and steps[u] // 2 + 1 < len(tiles):
                        tl = steps[u] // 2 + 1
                        split_lo(fb + tl, tl)
            over_pairs(pool, body)
            pool.wait_ge(z_out, 16)

        @block.vector
        def _(dve):
            dve.sem_inc(z_free, 2)
            dve.sem_inc(d_soft, 2)
            dve.sem_inc(y_ev, 1)
            dve.wait_ge(c_in, 80)
            nc.vector.tensor_scalar(nsinkB[:, :], sinkB[:, :], -1.0, None, ALU.mult).then_inc(c_sink, 1)
            nc.vector.tensor_scalar(wcol[:, 0:1], wcol[:, 0:1], SCALE, None, ALU.mult).then_inc(c_sink, 1)
            dve.wait_ge(c_sink, 2)

            def finish_norm(nidx, jl, kind):
                half = jl % 2
                c = 0 if kind == "qa" else 1
                dve.wait_ge(rs_d, 2 * nidx + 2)
                nc.vector.scalar_tensor_tensor(out=nxt[kind][:, half * HALF:(half + 1) * HALF], in0=job[:, :],
                                               scalar=wcol[:, c:c + 1], in1=rs[:, :], op0=ALU.mult,
                                               op1=ALU.mult).then_inc(job_ev, 1)

            def promote(p, j_last):
                after(dve, s_done, NU * p)
                dve.wait_ge(job_ev, j_last + 2)
                for kind in ("qa", "ka"):
                    nc.vector.tensor_copy(cur[kind][:, :], nxt[kind][:, :]).then_inc(cur_d, 1)

            def weights(p, u):
                v = NSB * p + u
                dve.wait_ge(a_st, 3 * v + 3)
                nc.vector.scalar_tensor_tensor(out=bsl(soft, u), in0=zsl(u), scalar=0.0, in1=bsl(t1, u),
                                               op0=ALU.max, op1=ALU.add).then_inc(d_soft, 1)
                dve.wait_ge(p_soft, v + 1)
                dve.wait_ge(a2_done, NU * p + u + 1)
                w = width(UNITS[u])
                for hs in range(len(UNITS[u][2])):
                    src, dst = head_sl(soft, u, hs), head_sl(logw, u, hs)
                    last = nc.vector.tensor_tensor_scan(out=dst[:, ::-1], data0=one_col[:, 0:1].to_broadcast([P, w]),
                                                        data1=src[:, ::-1], initial=0.0, op0=ALU.mult, op1=ALU.add)
                last.then_inc(d_scan, 1)
                dve.wait_ge(d_scan, v + 1)
                nc.vector.tensor_tensor(bsl(logw, u), zsl(u), bsl(logw, u), ALU.subtract).then_inc(z_free, 1)

            def scores(p, u):
                s, n = slot(u), UNITS[u][1]
                w = NSWA * p + u - NSB
                lo = 0 if n else P
                dve.wait_ge(s_done, NU * p + u + 1)
                dve.wait_ge(a2_done, NU * p + u + 1)
                nc.vector.tensor_tensor(bsl(logw, u), zsl(u), bias[:, bass.ds(2 * p, 2), lo:2 * P], ALU.add)\
                    .then_inc(z_free, 1)
                dve.wait_ge(z_free, NU * p + u + 3)
                nc.vector.tensor_reduce(stat["mx"][:, s, :], bsl(logw, u), AX_X, ALU.max).then_inc(w_st, 1)
                dve.wait_ge(w_st, 5 * w + 1)
                nc.vector.scalar_tensor_tensor(out=stat["negm"][:, s, :], in0=stat["mx"][:, s, :], scalar=-1.0,
                                               in1=nsinkB[:, bass.ds(2 * p, 2)], op0=ALU.mult, op1=ALU.min)\
                    .then_inc(w_st, 1)
                dve.wait_ge(w_st, 5 * w + 2)
                nc.vector.tensor_tensor(stat["dsink"][:, s, :], sinkB[:, bass.ds(2 * p, 2)], stat["negm"][:, s, :],
                                        ALU.add).then_inc(w_st, 1)

            def denominators(p, u):
                s = slot(u)
                w = NSWA * p + u - NSB
                dve.wait_ge(a2_done, NU * p + u + 3)
                nc.vector.tensor_tensor(stat["den"][:, s, :], stat["rsum"][:, s, :], stat["esink"][:, s, :],
                                        ALU.add).then_inc(w_st, 1)
                dve.wait_ge(w_st, 5 * w + 4)
                nc.vector.reciprocal(stat["rden"][:, s, :], stat["den"][:, s, :]).then_inc(w_st, 1)

            def result(p, u):
                kind, i, heads = UNITS[u]
                s, n = slot(u), len(heads) * HD
                if kind == "swa":
                    dve.wait_ge(w_st, 5 * (NSWA * p + u - NSB) + 5)
                dve.wait_ge(y_out[s], 16 * (NU // 2 * p + u // 2 + 1))
                dve.wait_ge(pv_mm, NU * p + u + 3)
                if kind == "sb":
                    nc.vector.tensor_copy(yst[:, s, 0:n], pv[:, 0:n]).then_inc(y_ev, 1)
                else:
                    nc.vector.tensor_scalar(yst[:, s, 0:HD], pv[:, 0:HD], stat["rden"][:, s, 0:1], None, ALU.mult)
                    nc.vector.tensor_scalar(yst[:, s, HD:P], pv[:, HD:P], stat["rden"][:, s, 1:2], None, ALU.mult)\
                        .then_inc(y_ev, 1)

            for jl in range(4):
                finish_norm(jl, jl, PAIR_TILES[jl // 2])
            promote(0, 7)
            dve.wait_ge(c_set, 5)
            dve.wait_ge(c_bias, 10)

            def body(p, tiles, steps):
                fb = 4 + 8 * p
                for u in range(NU):
                    if UNITS[u][0] == "sb":
                        weights(p, u)
                    else:
                        scores(p, u)
                        denominators(p, u)
                    if u in steps and tiles[steps[u] // 2] in ("qa", "ka"):
                        finish_norm(4 + 4 * p + steps[u], steps[u], tiles[steps[u] // 2])
                    result(p, u)
                if len(tiles) > 4:
                    promote(p + 1, 2 * fb + 7)
            over_pairs(dve, body)

        @block.tensor
        def _(pe):
            pe.sem_inc(job_mm, 4)
            pe.sem_inc(pv_mm, 2)

            def project(j, f, tl, half):
                s = tl % 2
                pe.wait_ge(wlo_d, f + 3)
                pe.wait_ge(job_ev, j + 1)
                for k in range(KD):
                    xh, xl = (v[:, k, half * HALF:(half + 1) * HALF] for v in (xnT_hi, xnT_lo))
                    last = split3(nc, job[:, :], w_hi[:, s, k, :], w_lo[:, s, k, :], xh, xl, k == 0, k == KD - 1)
                last.then_inc(job_mm, 1)

            def sum_squares(nidx):
                pe.wait_ge(sq_d, nidx + 1)
                nc.tensor.matmul(aux[:, :], ones_blk[:, :], sq[:, :], start=True, stop=True).then_inc(ss_d, 1)

            def score(p, u):
                kind, i, heads = UNITS[u]
                s = slot(u)
                q, k = (cur["qa"], cur["ka"]) if kind == "swa" else (cur["qb"], cur["kb"])
                pe.wait_ge(z_free, NU * p + u + 1)
                for hs, h in enumerate(heads):
                    lhs = q[h * HD:(h + 1) * HD, i * P:(i + 1) * P]
                    if kind == "swa":
                        lo = 0 if i else P
                        outs = [(z[:, 2 * s + hs, lo:2 * P], (i - 1) * P + lo, (i + 1) * P)]
                    elif len(heads) == 2:
                        outs = [(z[:, 2 * s + hs, 0:width(UNITS[u])], 0, width(UNITS[u]))]
                    else:
                        outs = [(z[:, 2 * s, :], 0, HALF), (z[:, 2 * s + 1, 0:width(UNITS[u]) - HALF], HALF, width(UNITS[u]))]
                    for out, k0, k1 in outs:
                        last = nc.tensor.matmul(out, lhs, k[h * HD:(h + 1) * HD, k0:k1], start=True, stop=True)
                last.then_inc(s_done, 1)

            def turn(p, u):
                kind, i, heads = UNITS[u]
                tiles = unit_tiles(UNITS[u])
                if kind == "sb":
                    pe.wait_ge(p_prob, NSB * p + u + 1)
                else:
                    pe.wait_ge(a2_done, NU * p + u + 3)
                first = tiles[0][1]
                for g in range(GROUPS[u]):
                    pe.wait_ge(tr_ev, NG * p + GROUP0[u] + g + 1)
                    for n, (hs, kb) in enumerate(tiles[4 * g:4 * g + 4]):
                        src = head_sl(prob, u, hs)
                        c = (kb - first) * P
                        last = nc.tensor.transpose(tr[:, n * P:(n + 1) * P], src[:, c:c + P], ident[:, :])
                    last.then_inc(tr_mm, 1)

            def weigh(p, u):
                kind, i, heads = UNITS[u]
                tiles = unit_tiles(UNITS[u])
                pe.wait_ge(tr_ev, NG * p + GROUP0[u] + GROUPS[u] + 1)
                pe.wait_ge(y_ev, NU * p + u + 1)
                for hs, h in enumerate(heads):
                    mine = [(n, kb) for n, (a, kb) in enumerate(tiles) if a == hs]
                    for m, (n, kb) in enumerate(mine):
                        v = vb[:, kb, bass.ds(P * p + HD * h, HD)] if kind == "sb" else va[:, kb, bass.ds(HD * p, HD)]
                        last = nc.tensor.matmul(pv[:, hs * HD:(hs + 1) * HD], probT[:, slot(u), n, :], v,
                                                start=m == 0, stop=m == len(mine) - 1)
                last.then_inc(pv_mm, 1)

            pe.wait_ge(c_set, 5)
            for jl in range(8):
                project(jl, jl // 2, jl // 2, jl % 2)
                if jl < 4:
                    sum_squares(jl)

            def body(p, tiles, steps):
                fb = 4 + 8 * p
                pe.wait_ge(cur_a, 2 * p + 2)
                pe.wait_ge(cur_d, 2 * p + 2)
                score(p, 0)
                for u in range(NU):
                    if u + 1 < NU:
                        score(p, u + 1)
                    if u in steps:
                        jl = steps[u]
                        project(2 * fb + jl, fb + jl // 2, jl // 2, jl % 2)
                    turn(p, u)
                    if u in steps and tiles[steps[u] // 2] in ("qa", "ka"):
                        sum_squares(4 + 4 * p + steps[u])
                    weigh(p, u)

            over_pairs(pe, body)


def merge(nc, w_proj_swa, w_proj_sb, ident, gT, y_s, mT_hi, mT_lo):
    KA4 = PAIRS
    with ExitStack() as ctx:
        sb = lambda n, s, d=F32: ctx.enter_context(nc.sbuf_tensor(n, s, d))
        sem = lambda n: ctx.enter_context(nc.semaphore(n))
        yT_hi = sb("mg_yThi", [P, 2, KA4, T], F32R)
        yT_lo = sb("mg_yTlo", [P, 2, KA4, T], F32R)
        ytok = sb("mg_ytok", [P, 4, HALF])
        raw = sb("mg_raw", [P, 2, 2, KA4, P])
        w_hi = sb("mg_whi", [P, 2, 2, KA4, P], F32R)
        w_lo = sb("mg_wlo", [P, 2, 2, KA4, P], F32R)
        g = sb("mg_g", [P, 2, 2, HALF])
        prod = sb("mg_prod", [P, 2, 2, HALF])
        acc = ctx.enter_context(nc.psum_tensor("mg_acc", [P, 4, HALF], F32))
        tr = ctx.enter_context(nc.psum_tensor("mg_tr", [P, 2, HALF], F32))
        y_in = [sem(f"mg_y_in{s}") for s in range(4)]
        raw_in = [sem(f"mg_raw_in{s}") for s in range(2)]
        g_in = [sem(f"mg_g_in{s}") for s in range(2)]
        tr_mm, yhi, ylo = sem("mg_tr_mm"), sem("mg_yhi"), sem("mg_ylo")
        whi_d, wlo_d = sem("mg_whi_d"), sem("mg_wlo_d")
        mm_done = sem("mg_mm")
        sg_done = sem("mg_sg")
        pr_done = sem("mg_pr")
        sum_done, mhi, mlo = sem("mg_sum"), sem("mg_mhi"), sem("mg_mlo")
        pa_v = w_proj_swa.rearrange("a (k p) c -> p (a k) c", p=P)
        pb_v = w_proj_sb.rearrange("a (k p) c -> p (a k) c", p=P)

        def over_tiles(eng, body):
            with eng.Fori(0, KD // 2 - 1) as i:
                for s in range(2):
                    body(2 * i + s, s, True)
            body(KD - 2, 0, True)
            body(KD - 1, 1, False)

        with nc.Block() as block:
            @block.sync
            def _(sp):
                def load_w(m, s):
                    sp.wait_ge(wlo_d, m + 1)
                    for n, v in enumerate((pa_v, pb_v)):
                        sp.dma_start(raw[:, s, n, :, :], v[:, :, bass.ds(m * P, P)]).then_inc(raw_in[s], 16)

                def body(m, s, more):
                    for half in range(2):
                        sp.wait_ge(pr_done, 2 * m + half + 1)
                        for n in range(2):
                            sp.dma_start(g[:, half, n, :],
                                         gT[bass.ds(KD * n + m, 1), :, half * HALF:(half + 1) * HALF]
                                         .rearrange("a p c -> (a p) c")).then_inc(g_in[half], 16)
                    if more:
                        load_w(m + 1, 1 - s)

                for n in range(2 * NT):
                    t, a = divmod(n, 2)
                    after(sp, tr_mm, n - 3)
                    sp.dma_start(ytok[:, n % 4, :], y_s[a, t * P:(t + 1) * P, :]).then_inc(y_in[n % 4], 16)
                load_w(0, 0)
                over_tiles(sp, body)

            @block.scalar
            def _(act):
                def split_hi(m, s):
                    act.wait_ge(raw_in[s], 16 * (m + 2 - s))
                    act.wait_ge(mm_done, 2 * m + 1)
                    nc.scalar.activation(w_hi[:, s], raw[:, s], ACT.Copy).then_inc(whi_d, 1)

                def body(m, s, more):
                    if more:
                        split_hi(m + 1, 1 - s)
                    for half in range(2):
                        n = 2 * m + half
                        act.wait_ge(g_in[half], 32 * (m + 1))
                        nc.scalar.activation(g[:, half], g[:, half], ACT.Sigmoid).then_inc(sg_done, 1)
                    for half in range(2):
                        n = 2 * m + half
                        act.wait_ge(sum_done, n + 1)
                        nc.scalar.activation(mT_hi[:, bass.ds(m, 1), half * HALF:(half + 1) * HALF]
                                             .rearrange("p a c -> p (a c)"),
                                             prod[:, half, 0, :], ACT.Copy).then_inc(mhi, 1)

                for n in range(2 * NT):
                    t, a = divmod(n, 2)
                    act.wait_ge(tr_mm, n + 1)
                    nc.scalar.activation(yT_hi[:, a, :, t * P:(t + 1) * P],
                                         tr[:, n % 2, :].rearrange("p (k c) -> p k c", k=4), ACT.Copy).then_inc(yhi, 1)
                split_hi(0, 0)
                over_tiles(act, body)

            @block.gpsimd
            def _(pool):
                pool.sem_inc(wlo_d, 2)

                def split_lo(m, s):
                    pool.wait_ge(whi_d, m + 1)
                    nc.gpsimd.tensor_tensor(w_lo[:, s], raw[:, s], w_hi[:, s].bitcast(F32), ALU.subtract)\
                        .then_inc(wlo_d, 1)
                split_lo(0, 0)
                over_tiles(pool, lambda m, s, more: split_lo(m + 1, 1 - s) if more else None)

            @block.vector
            def _(dve):
                dve.sem_inc(pr_done, 2)
                dve.sem_inc(mlo, 2)
                for n in range(2 * NT):
                    t, a = divmod(n, 2)
                    dve.wait_ge(yhi, n + 1)
                    nc.vector.tensor_tensor(yT_lo[:, a, :, t * P:(t + 1) * P],
                                            tr[:, n % 2, :].rearrange("p (k c) -> p k c", k=4),
                                            yT_hi[:, a, :, t * P:(t + 1) * P].bitcast(F32), ALU.subtract).then_inc(ylo, 1)

                def body(m, s, more):
                    for half in range(2):
                        n = 2 * m + half
                        dve.wait_ge(mm_done, n + 5)
                        dve.wait_ge(sg_done, n + 1)
                        dve.wait_ge(mlo, n + 1)
                        nc.vector.tensor_tensor(prod[:, half], acc[:, 2 * half:2 * half + 2, :], g[:, half],
                                                ALU.mult).then_inc(pr_done, 1)
                        dve.wait_ge(pr_done, n + 3)
                        nc.vector.tensor_tensor(prod[:, half, 0, :], prod[:, half, 0, :], prod[:, half, 1, :],
                                                ALU.add).then_inc(sum_done, 1)
                    for half in range(2):
                        n = 2 * m + half
                        dve.wait_ge(mhi, n + 1)
                        sl = (slice(None), bass.ds(m, 1), slice(half * HALF, (half + 1) * HALF))
                        nc.vector.tensor_tensor(mT_lo[sl].rearrange("p a c -> p (a c)"), prod[:, half, 0, :],
                                                mT_hi[sl].rearrange("p a c -> p (a c)").bitcast(F32),
                                                ALU.subtract).then_inc(mlo, 1)
                over_tiles(dve, body)

            @block.tensor
            def _(pe):
                pe.sem_inc(mm_done, 4)
                for n in range(2 * NT):
                    t, a = divmod(n, 2)
                    pe.wait_ge(y_in[n % 4], 16 * (n // 4 + 1))
                    after(pe, ylo, n - 1)
                    for k in range(4):
                        last = nc.tensor.transpose(tr[:, n % 2, k * P:(k + 1) * P], ytok[:, n % 4, k * P:(k + 1) * P],
                                                   ident[:, :])
                    last.then_inc(tr_mm, 1)
                pe.wait_ge(ylo, 2 * NT)

                def body(m, s, more):
                    pe.wait_ge(wlo_d, m + 3)
                    for half in range(2):
                        pe.wait_ge(pr_done, 2 * m + half + 1)
                        for a in range(2):
                            for k in range(KA4):
                                last = split3(nc, acc[:, 2 * half + a, :], w_hi[:, s, a, k, :], w_lo[:, s, a, k, :],
                                              yT_hi[:, a, k, half * HALF:(half + 1) * HALF],
                                              yT_lo[:, a, k, half * HALF:(half + 1) * HALF], k == 0, k == KA4 - 1)
                        last.then_inc(mm_done, 1)
                over_tiles(pe, body)


def output_and_logits(nc, x, w_out, ffn_norm_w, router_w, router_b, ident, nhalf, mT_hi, mT_lo, h_s, xn_s, logits):
    with ExitStack() as ctx:
        sb = lambda n, s, d=F32: ctx.enter_context(nc.sbuf_tensor(n, s, d))
        sem = lambda n: ctx.enter_context(nc.semaphore(n))
        raw = sb("op_raw", [P, 2, D])
        w_hi = sb("op_whi", [P, KD, D], F32R)
        w_lo = sb("op_wlo", [P, KD, D], F32R)
        xt = sb("op_x", [P, 2, D])
        ht = sb("op_h", [P, 2, D])
        xn = sb("op_xn", [P, 2, D])
        xnT = sb("op_xnT", [P, KD, P])
        junk = sb("op_junk", [P, D])
        wB = sb("op_wB", [P, D])
        rw = sb("op_rw", [P, KD, NE])
        rbB = sb("op_rb", [P, NE])
        ssq, ms, rstd = (sb(f"op_{n}", [P, NT]) for n in ("ssq", "ms", "rstd"))
        acc = ctx.enter_context(nc.psum_tensor("op_acc", [P, 4, HALF], F32))
        tr = ctx.enter_context(nc.psum_tensor("op_tr", [P, 2, HALF], F32))
        lg = ctx.enter_context(nc.psum_tensor("op_lg", [P, HALF], F32))
        raw_in = [sem(f"op_raw_in{s}") for s in range(2)]
        x_in = [sem(f"op_x_in{s}") for s in range(2)]
        h_out = [sem(f"op_h_out{s}") for s in range(2)]
        xn_out = [sem(f"op_xn_out{s}") for s in range(2)]
        c_in = sem("op_c_in")
        whi_d, wlo_d, mm_done, h_done = sem("op_whi_d"), sem("op_wlo_d"), sem("op_mm"), sem("op_h_d")
        sq_done, ms_done, rstd_done, xn_done = sem("op_sq"), sem("op_ms_d"), sem("op_rstd_d"), sem("op_xn_d")
        tr_mm, tr_ev, lg_mm, lg_ev = sem("op_tr_mm"), sem("op_tr_ev"), sem("op_lg_mm"), sem("op_lg_ev")
        x_t = x.rearrange("a (t p) d -> (a t) p d", p=P)
        h_t = h_s.rearrange("(t p) d -> t p d", p=P)
        xn_t = xn_s.rearrange("(t p) d -> t p d", p=P)
        with nc.Block() as block:
            @block.sync
            def _(sp):
                for k in range(KD):
                    after(sp, wlo_d, k - 1)
                    sp.dma_start(raw[:, k % 2, :], w_out[0, k * P:(k + 1) * P, :]).then_inc(raw_in[k % 2], 16)
                    if k == 1:
                        for t in range(2):
                            sp.dma_start(xt[:, t, :], x_t[t]).then_inc(x_in[t], 16)
                sp.dma_start(wB[:, :], ffn_norm_w[0:1, :].to_broadcast([P, D])).then_inc(c_in, 16)
                sp.dma_start(rbB[:, :], router_b[0:1, :].to_broadcast([P, NE])).then_inc(c_in, 16)
                sp.dma_start(rw[:, :, :], router_w.rearrange("a (k p) c -> p (a k) c", p=P)).then_inc(c_in, 16)
                for t in range(NT):
                    sp.wait_ge(h_done, t + 1)
                    sp.dma_start(h_t[t], ht[:, t % 2, :]).then_inc(h_out[t % 2], 16)
                    if t + 2 < NT:
                        sp.dma_start(xt[:, t % 2, :], x_t[t + 2]).then_inc(x_in[t % 2], 16)
                    sp.wait_ge(xn_done, t + 1)
                    sp.dma_start(xn_t[t], xn[:, t % 2, :]).then_inc(xn_out[t % 2], 16)
                for s in range(2):
                    sp.wait_ge(h_out[s], 16 * NT // 2)
                    sp.wait_ge(xn_out[s], 16 * NT // 2)

            @block.scalar
            def _(act):
                for k in range(KD):
                    act.wait_ge(raw_in[k % 2], 16 * (k // 2 + 1))
                    nc.scalar.activation(w_hi[:, k, :], raw[:, k % 2, :], ACT.Copy).then_inc(whi_d, 1)
                for t in range(NT):
                    act.wait_ge(h_done, t + 1)
                    if t:
                        act.wait_ge(sq_done, t)
                    nc.scalar.activation(junk[:, :], ht[:, t % 2, :], ACT.Square, accum_out=ssq[:, t:t + 1])\
                        .then_inc(sq_done, 1)
                    act.wait_ge(tr_mm, t + 1)
                    after(act, lg_mm, t)
                    nc.scalar.activation(xnT[:, :, :].rearrange("p k c -> p (k c)"),
                                         tr[:, :, :].rearrange("p a c -> p (a c)"), ACT.Copy).then_inc(tr_ev, 1)

            @block.gpsimd
            def _(pool):
                for t in range(NT):
                    pool.wait_ge(sq_done, t + 1)
                    nc.gpsimd.tensor_scalar(ms[:, t:t + 1], ssq[:, t:t + 1], 1.0 / D, EPS,
                                            ALU.mult, ALU.add).then_inc(ms_done, 1)
                    pool.wait_ge(ms_done, t + 1)
                    nc.gpsimd.tensor_tensor(rstd[:, t:t + 1], ms[:, t:t + 1], nhalf[:, 0:1],
                                            ALU.pow).then_inc(rstd_done, 1)

            @block.vector
            def _(dve):
                for k in range(KD):
                    dve.wait_ge(whi_d, k + 1)
                    nc.vector.tensor_tensor(w_lo[:, k, :], raw[:, k % 2, :], w_hi[:, k, :].bitcast(F32),
                                            ALU.subtract).then_inc(wlo_d, 1)
                dve.wait_ge(c_in, 48)

                def residual(t):
                    s = t % 2
                    dve.wait_ge(mm_done, t + 1)
                    dve.wait_ge(x_in[s], 16 * (t // 2 + 1))
                    after(dve, h_out[s], 16 * (t // 2))
                    nc.vector.tensor_tensor(ht[:, s, :], acc[:, 2 * s:2 * s + 2, :].rearrange("p a c -> p (a c)"),
                                            xt[:, s, :], ALU.add).then_inc(h_done, 1)

                residual(0)
                for t in range(NT):
                    s = t % 2
                    if t + 1 < NT:
                        residual(t + 1)
                    dve.wait_ge(rstd_done, t + 1)
                    after(dve, xn_out[s], 16 * (t // 2))
                    after(dve, tr_mm, t - 1)
                    nc.vector.scalar_tensor_tensor(out=xn[:, s, :], in0=ht[:, s, :], scalar=rstd[:, t:t + 1],
                                                   in1=wB[:, :], op0=ALU.mult, op1=ALU.mult).then_inc(xn_done, 1)
                    dve.wait_ge(lg_mm, t + 1)
                    nc.vector.tensor_tensor(logits[:, t, :], lg[:, 0:NE], rbB[:, :], ALU.add).then_inc(lg_ev, 1)

            @block.tensor
            def _(pe):
                def project(t):
                    after(pe, h_done, t - 1)
                    for nh in range(2):
                        for k in range(KD):
                            if t == 0 and nh == 0:
                                pe.wait_ge(wlo_d, k + 1)
                            last = split3(nc, acc[:, 2 * (t % 2) + nh, :], mT_hi[:, k, t * P:(t + 1) * P],
                                          mT_lo[:, k, t * P:(t + 1) * P], w_hi[:, k, nh * HALF:(nh + 1) * HALF],
                                          w_lo[:, k, nh * HALF:(nh + 1) * HALF], k == 0, k == KD - 1)
                    last.then_inc(mm_done, 1)

                project(0)
                for t in range(NT):
                    if t + 1 < NT:
                        project(t + 1)
                    pe.wait_ge(xn_done, t + 1)
                    after(pe, tr_ev, t)
                    for k in range(KD):
                        last = nc.tensor.transpose(tr[:, k // 4, (k % 4) * P:(k % 4 + 1) * P],
                                                   xn[:, t % 2, k * P:(k + 1) * P], ident[:, :])
                    last.then_inc(tr_mm, 1)
                    pe.wait_ge(tr_ev, t + 1)
                    after(pe, lg_ev, t)
                    for k in range(KD):
                        last = nc.tensor.matmul(lg[:, 0:NE], xnT[:, k, :], rw[:, k, :], start=k == 0, stop=k == KD - 1)
                    last.then_inc(lg_mm, 1)


SLOTS = (NBLK + 1) * CAP
TABLE = -(-SLOTS // P) * P


def route(nc, logits, gates, dest, tabs, slot_token):
    with ExitStack() as ctx:
        sb = lambda n, s, d=F32: ctx.enter_context(nc.sbuf_tensor(n, s, d))
        sem = lambda n: ctx.enter_context(nc.semaphore(n))
        top = sb("rt_top", [P, NT, 8])
        idx = sb("rt_idx", [P, NT, 8], U32)
        idxf = sb("rt_idxf", [P, NT, TOPK])
        ex = sb("rt_ex", [P, NT, TOPK])
        den = sb("rt_den", [P, NT])
        iota_e = sb("rt_iota", [P, NE])
        oh = sb("rt_oh", [P, NT, TOPK, NE])
        prod = sb("rt_prod", [P, NT, TOPK, NE])
        chosen = sb("rt_chosen", [P, NT, NE])
        chosen16 = sb("rt_chosen16", [P, NT, NE], BF16)
        upper = sb("rt_upper", [P, P], BF16)
        ones = sb("rt_ones", [P, P], BF16)
        one_col = sb("rt_one", [P, 1])
        cnt, over, cum, base0, base1, step_b = (sb(f"rt_{n}", [P, NE]) for n in
                                               ("cnt", "over", "cum", "base0", "base1", "stepb"))
        rank = sb("rt_rank", [P, NT, NE])
        place = sb("rt_place", [P, NT, NE])
        destf = sb("rt_destf", [P, NT * TOPK])
        cmp = sb("rt_cmp", [1, MAXOVER, NE])
        iota_b = sb("rt_iotab", [1, MAXOVER])
        tabf = sb("rt_tabf", [1, NE + MAXOVER + 1])
        zero = sb("rt_zero", [P, TABLE // P], I32)
        prk = ctx.enter_context(nc.psum_tensor("rt_prk", [P, HALF], F32))
        pct = ctx.enter_context(nc.psum_tensor("rt_pct", [P, HALF], F32))
        c_set, v, a_exp, mm, z_out = sem("rt_cset"), sem("rt_v"), sem("rt_exp"), sem("rt_mm"), sem("rt_zout")
        m16 = sem("rt_m16")
        with nc.Block() as block:
            @block.sync
            def _(sp):
                sp.wait_ge(c_set, 6)
                sp.dma_start(slot_token.rearrange("(p n) a -> p (n a)", p=P), zero[:, :]).then_inc(z_out, 16)
                sp.wait_ge(z_out, 16)

            @block.gpsimd
            def _(pool):
                nc.gpsimd.iota(iota_e[:, :], [[1, NE]], base=0, channel_multiplier=0,
                               allow_small_or_imprecise_dtypes=True).then_inc(c_set, 1)
                nc.gpsimd.iota(iota_b[:, :], [[1, MAXOVER]], base=0, channel_multiplier=0,
                               allow_small_or_imprecise_dtypes=True).then_inc(c_set, 1)
                nc.gpsimd.memset(ones[:, :], 1.0).then_inc(c_set, 1)
                nc.gpsimd.memset(upper[:, :], 1.0).then_inc(c_set, 1)
                nc.gpsimd.memset(one_col[:, :], 1.0).then_inc(c_set, 1)
                nc.gpsimd.memset(zero[:, :], 0).then_inc(c_set, 1)
                pool.wait_ge(c_set, 6)
                nc.gpsimd.affine_select(out=upper[:, :], in_=upper[:, :], compare_op=ALU.is_gt, fill=0.0, base=0,
                                        pattern=[[1, P]], channel_multiplier=-1).then_inc(c_set, 1)

            @block.scalar
            def _(act):
                act.wait_ge(v, 2 * NT + 1)
                nc.scalar.activation(ex[:, :, :], ex[:, :, :], ACT.Exp).then_inc(a_exp, 1)

            @block.vector
            def _(dve):
                n = [0]

                def step(ins):
                    n[0] += 1
                    ins.then_inc(v, 1)
                    dve.wait_ge(v, n[0])

                for t in range(NT):
                    step(nc.vector.max(top[:, t, :], logits[:, t, :]))
                    step(nc.vector.max_index(idx[:, t, :], top[:, t, :], logits[:, t, :]))
                step(nc.vector.tensor_tensor(ex[:, :, :], top[:, :, 0:TOPK], top[:, :, 0:1].to_broadcast([P, NT, TOPK]),
                                             ALU.subtract))
                step(nc.vector.tensor_copy(idxf[:, :, :], idx[:, :, 0:TOPK]))
                dve.wait_ge(c_set, 7)
                step(nc.vector.tensor_tensor(
                    oh[:, :, :, :].rearrange("p t j e -> p (t j) e"),
                    iota_e[:, :].rearrange("p (o e) -> p o e", o=1).to_broadcast([P, NT * TOPK, NE]),
                    idxf[:, :, :].rearrange("p t (j o) -> p (t j) o", o=1).to_broadcast([P, NT * TOPK, NE]), ALU.is_equal))
                step(nc.vector.tensor_reduce(chosen[:, :, :], oh[:, :, :, :].rearrange("p t j e -> p t e j"), AX_X, ALU.add))
                nc.vector.tensor_copy(chosen16[:, :, :], chosen[:, :, :]).then_inc(m16, 1)
                dve.wait_ge(a_exp, 1)
                step(nc.vector.tensor_reduce(den[:, :], ex[:, :, :], AX_X, ALU.add))
                step(nc.vector.reciprocal(den[:, :], den[:, :]))
                step(nc.vector.tensor_tensor(gates[:, :, :], ex[:, :, :],
                                             den[:, :].rearrange("p (t o) -> p t o", o=1).to_broadcast([P, NT, TOPK]),
                                             ALU.mult))
                dve.wait_ge(mm, 2)
                step(nc.vector.tensor_copy(cnt[:, :], pct[:, 0:NE]))
                step(nc.vector.tensor_scalar(over[:, :], cnt[:, :], float(CAP), None, ALU.is_gt))
                for m in range(2, -(-T // CAP)):
                    step(nc.vector.scalar_tensor_tensor(out=over[:, :], in0=cnt[:, :], scalar=float(CAP * m), in1=over[:, :],
                                                        op0=ALU.is_gt, op1=ALU.add))
                step(nc.vector.tensor_tensor_scan(out=cum[:, :], data0=one_col[:, 0:1].to_broadcast([P, NE]),
                                                  data1=over[:, :], initial=0.0, op0=ALU.mult, op1=ALU.add))
                step(nc.vector.tensor_tensor(base1[:, :], cum[:, :], over[:, :], ALU.subtract))
                step(nc.vector.tensor_scalar(base1[:, :], base1[:, :], float(NE - 1), float(CAP), ALU.add, ALU.mult))
                step(nc.vector.tensor_scalar(base0[:, :], iota_e[:, :], float(CAP), None, ALU.mult))
                step(nc.vector.tensor_tensor(step_b[:, :], base0[:, :], base1[:, :], ALU.subtract))
                step(nc.vector.tensor_copy(rank[:, :, :], prk[:, 0:NT * NE].rearrange("p (t e) -> p t e", e=NE)))
                step(nc.vector.tensor_scalar(place[:, :, :], rank[:, :, :], float(CAP), None, ALU.is_lt))
                over_t = lambda b: b[:, :].rearrange("p (o e) -> p o e", o=1).to_broadcast([P, NT, NE])
                step(nc.vector.tensor_tensor(place[:, :, :], place[:, :, :], over_t(step_b), ALU.mult))
                step(nc.vector.tensor_tensor(place[:, :, :], place[:, :, :], over_t(base1), ALU.add))
                step(nc.vector.tensor_tensor(place[:, :, :], place[:, :, :], rank[:, :, :], ALU.add))
                for j in range(TOPK):
                    step(nc.vector.tensor_tensor(prod[:, :, j, :], oh[:, :, j, :], place[:, :, :], ALU.mult))
                step(nc.vector.tensor_reduce(destf[:, :], prod[:, :, :, :].rearrange("p t j e -> p (t j) e"), AX_X, ALU.add))
                step(nc.vector.tensor_copy(dest[:, :], destf[:, :]))
                step(nc.vector.tensor_tensor(cmp[:, :, :],
                                             cum[0:1, :].rearrange("p (o e) -> p o e", o=1).to_broadcast([1, MAXOVER, NE]),
                                             iota_b[:, :].rearrange("p (b o) -> p b o", o=1).to_broadcast([1, MAXOVER, NE]),
                                             ALU.is_le))
                step(nc.vector.tensor_reduce(tabf[:, NE:NE + MAXOVER], cmp[:, :, :], AX_X, ALU.add))
                step(nc.vector.tensor_scalar(tabf[:, NE:NE + MAXOVER], tabf[:, NE:NE + MAXOVER], float(NE - 1), None, ALU.min))
                step(nc.vector.tensor_copy(tabf[:, 0:NE], cnt[0:1, :]))
                step(nc.vector.tensor_copy(tabf[:, NE + MAXOVER:NE + MAXOVER + 1], cum[0:1, NE - 1:NE]))
                step(nc.vector.tensor_copy(tabs[:, :], tabf[:, :]))

            @block.tensor
            def _(pe):
                pe.wait_ge(c_set, 7)
                pe.wait_ge(m16, 1)
                for t in range(NT):
                    for b in range(t + 1):
                        last = nc.tensor.matmul(prk[:, t * NE:(t + 1) * NE], (upper if b == t else ones)[:, :],
                                                chosen16[:, b, :], start=b == 0, stop=b == t)
                last.then_inc(mm, 1)
                for b in range(NT):
                    last = nc.tensor.matmul(pct[:, 0:NE], ones[:, :], chosen16[:, b, :], start=b == 0, stop=b == NT - 1)
                last.then_inc(mm, 1)


CHUNKS = 6
CW = 4096
FT = FF // P
Q = P // CAP2
XW = D // Q


def experts(nc, xn_s, w_gate_up, b_gate_up, w_down, b_down, ident, dest, tabs, slot_token, y_slots):
    with ExitStack() as ctx:
        sb = lambda n, s, d=F32: ctx.enter_context(nc.sbuf_tensor(n, s, d))
        sem = lambda n: ctx.enter_context(nc.semaphore(n))
        w = sb("ex_w", [P, CHUNKS, CW])
        idx = sb("ex_idx", [P, 2], U32)
        idx2 = sb("ex_idx2", [P, 1], U32)
        quarter = sb("ex_quarter", [P, 1])
        xg = sb("ex_xg", [P, D])
        xg2 = sb("ex_xg2", [P, XW])
        xT = sb("ex_xT", [P, KD, CAP])
        gs = sb("ex_g", [P, 2, CAP])
        us = sb("ex_u", [P, 2, CAP])
        sg = sb("ex_sg", [P, 2, CAP])
        hid = sb("ex_hid", [P, FT, CAP])
        yT = sb("ex_yT", [P, KD, P])
        yT2 = sb("ex_yT2", [P, KD, CAP2])
        ytok = sb("ex_ytok", [P, D])
        ytok2 = sb("ex_ytok2", [P, 2, P])
        bT = sb("ex_bT", [P, 3 * KD, NE])
        bcur = sb("ex_bcur", [P, 3 * KD])
        brow = hid[0:NE, :, :].rearrange("p a c -> p (a c)")
        tokid = sb("ex_tokid", [P, NT], I32)
        ps = lambda n, s: ctx.enter_context(nc.psum_tensor(n, s, F32))
        gu = ps("ex_gu", [P, 4, HALF])
        yp = ps("ex_yp", [P, 2, HALF])
        tr = ps("ex_tr", [P, 2, HALF])

        b_in, b_mm, b_ev, b_d = sem("b_in"), sem("b_mm"), sem("b_ev"), sem("b_d")
        ini, tok_out, tok_set = sem("ini"), sem("tok_out"), sem("tok_set")
        w_in_ = [sem(f"e_w_in{c}") for c in range(CHUNKS)]
        idx_in, idx2_d, x_in = sem("idx_in"), sem("idx2_d"), sem("x_in")
        tr_mm = sem("e_tr_mm")
        tr_ev = sem("e_tr_ev")
        gu_mm = sem("gu_mm")
        g_d = sem("g_d")
        gu_ev = sem("gu_ev")
        sg_d, t_d, hid_d = sem("sg_d"), sem("t_d"), sem("hid_d")
        yp_mm = sem("yp_mm")
        yp_ev = sem("yp_ev")
        y_out = sem("e_y_out")
        spare, spare_sp, spare_dve = sem("spare"), sem("spare_sp"), sem("spare_dve")
        STORE = 16 * (1 + Q)

        gate_up_v = w_gate_up.rearrange("a e (k p) c -> (a e) p k c", p=P)
        down_v = w_down.rearrange("a e (k p) c -> (a e) p k c", p=P)
        nov_ap = tabs[0:1, NE + MAXOVER:NE + MAXOVER + 1]

        def over_blocks(eng, body, first=0):
            with eng.Fori(first, NE) as b:
                body(b, False)
            nov = eng.value_load(nov_ap, min_val=0, max_val=MAXOVER)
            with eng.Fori(0, MAXOVER) as i:
                with eng.If(i < nov):
                    body(NE + i, True)
            return nov

        def over_expert(eng, b):
            return eng.value_load(tabs[0:1, bass.ds(b, 1)], min_val=0, max_val=NE - 1)

        def w_tile(c, j, k, part=0):
            if c < 4:
                return w[:, c, :].rearrange("p (h k q) -> p h k q", h=2, k=KD)[:, part, k, j * P:(j + 1) * P]
            return w[:, c, :].rearrange("p (k q) -> p k q", k=KD)[:, k, j * P:(j + 1) * P]

        block = ctx.enter_context(nc.Block())

        @block.sync
        def _(sp):
            def load(c, e):
                if c < 4:
                    v = w[:, c, :].rearrange("p (h k q) -> p h k q", h=2, k=KD)
                    for h in range(2):
                        sp.dma_start(v[:, h, :, :],
                                     gate_up_v[bass.ds(e, 1), :, :, h * FF + 2 * P * c:h * FF + 2 * P * (c + 1)]
                                     .rearrange("a p k c -> (a p) k c")).then_inc(w_in_[c], 16)
                else:
                    v = w[:, c, :].rearrange("p (k q) -> p k q", k=KD)
                    for h in range(2):
                        sp.dma_start(v[:, 4 * h:4 * h + 4, :],
                                     down_v[bass.ds(e, 1), :, 4 * h:4 * h + 4, (c - 4) * HALF:(c - 3) * HALF]
                                     .rearrange("a p k c -> (a p) k c")).then_inc(w_in_[c], 16)

            def store(b):
                sp.wait_ge(tr_ev, 6 * b + 14)
                sp.dma_start(y_slots[bass.ds(b * CAP, P), :], ytok[:, :]).then_inc(y_out, 16)
                for d in range(Q):
                    sp.dma_start(y_slots[bass.ds(b * CAP + P, CAP2), :]
                                 .rearrange("s (g d f) -> s g d f", g=2, d=Q)[:, :, d, :],
                                 ytok2[d * CAP2:(d + 1) * CAP2, :, :]).then_inc(y_out, 16)

            def body(b, over):
                e = over_expert(sp, b) if over else b
                for c in range(CHUNKS):
                    if c < 4:
                        sp.wait_ge(gu_mm, FT * (b - 1) + 2 * c + 2)
                    else:
                        sp.wait_ge(yp_mm, KD * (b - 1) + 4 * (c - 3))
                    load(c, e)
                    if c == 5:
                        store(b - 1)

            sp.dma_start(brow[:, 0:D], b_gate_up[0, :, 0:D]).then_inc(b_in, 16)
            load(0, 0)
            for part, src in ((1, b_gate_up[0, :, D:2 * D]), (2, b_down[0, :, :])):
                sp.wait_ge(b_mm, part)
                sp.dma_start(brow[:, 0:D], src).then_inc(b_in, 16)
            for c in range(1, CHUNKS):
                load(c, 0)
            nov = over_blocks(sp, body, first=1)
            store(nov + (NE - 1))
            sp.wait_ge(y_out, STORE * (NE + nov) + 2 * STORE)
            sp.sem_inc(spare_sp, 1)

        @block.scalar
        def _(act):
            act.preload_act_table_set("sigmoid_and_others")
            act.sem_inc(yp_ev, 2)

            def body(b, over):
                for ft in range(FT):
                    act.wait_ge(g_d, FT * b + ft + 1)
                    nc.scalar.activation(sg[:, ft % 2, :], gs[:, ft % 2, :], ACT.Sigmoid, scale=ALPHA).then_inc(sg_d, 1)
                act.wait_ge(b_d, b + 1)
                for dt in range(KD):
                    act.wait_ge(yp_mm, KD * b + dt + 1)
                    bias = bcur[:, 2 * KD + dt:2 * KD + dt + 1]
                    nc.scalar.activation(yT[:, dt, :], yp[:, dt % 2, 0:P], ACT.Identity, bias=bias)
                    nc.scalar.activation(yT2[:, dt, :], yp[:, dt % 2, P:CAP], ACT.Identity, bias=bias)\
                        .then_inc(yp_ev, 1)
            over_blocks(act, body)

        @block.gpsimd
        def _(pool):
            nc.gpsimd.iota(tokid[:, :], [[P, NT]], base=0, channel_multiplier=1).then_inc(tok_set, 1)
            for q in range(Q):
                pool.wait_ge(tok_set, q + 1)
                nc.gpsimd.memset(quarter[q * CAP2:(q + 1) * CAP2, :], float(q)).then_inc(tok_set, 1)
            pool.wait_ge(tok_set, 1 + Q)
            for t in range(NT):
                for j in range(TOPK):
                    pool.indirect_dma_start(out=slot_token[:, :], out_offset=bass.IndirectOffsetOnAxis(
                        ap=dest[:, t * TOPK + j:t * TOPK + j + 1], axis=0), in_=tokid[:, t:t + 1],
                        in_offset=None).then_inc(tok_out, 16)
            pool.wait_ge(tok_out, 16 * NT * TOPK)

            def load_idx(b):
                pool.dma_start(idx[:, 0:1].bitcast(I32), slot_token[bass.ds(b * CAP, P), :]).then_inc(idx_in, 16)
                for q in range(Q):
                    pool.dma_start(idx[q * CAP2:(q + 1) * CAP2, 1:2].bitcast(I32),
                                   slot_token[bass.ds(b * CAP + P, CAP2), :]).then_inc(idx_in, 16)

            def rows():
                nc.gpsimd.tensor_scalar(idx2[:, :], idx[:, 1:2], float(Q), quarter[:, 0:1], ALU.mult, ALU.add)\
                    .then_inc(idx2_d, 1)

            def gather():
                pool.indirect_dma_start(out=xg[:, :], out_offset=None, in_=xn_s[:, :],
                                        in_offset=bass.IndirectOffsetOnAxis(ap=idx[:, 0:1], axis=0)).then_inc(x_in, 16)
                pool.indirect_dma_start(out=xg2[:, :], out_offset=None, in_=xn_s.rearrange("t (q c) -> (t q) c", q=Q),
                                        in_offset=bass.IndirectOffsetOnAxis(ap=idx2[:, 0:1], axis=0)).then_inc(x_in, 16)

            load_idx(0)
            pool.wait_ge(idx_in, 16 * (1 + Q))
            rows()
            pool.wait_ge(idx2_d, 1)
            gather()

            def body(b, over):
                hold(pool, x_in, 32 * b + 32, spare)
                load_idx(b + 1)
                hold(pool, idx_in, 16 * (1 + Q) * (b + 2), spare)
                rows()
                hold(pool, idx2_d, b + 2, spare)
                hold(pool, tr_ev, 6 * b + 5, spare)
                gather()
            over_blocks(pool, body)

        @block.vector
        def _(dve):
            dve.sem_inc(gu_ev, 4)
            dve.sem_inc(tr_ev, 2)
            dve.sem_inc(y_out, 2 * STORE)
            for bank in (gu, yp):
                nc.vector.memset(bank[:, :, :], 0.0).then_inc(ini, 1)
            for buf in (yT, yT2):
                nc.vector.memset(buf[:, :, :], 0.0).then_inc(ini, 1)
            for part in range(3):
                dve.wait_ge(b_mm, part + 1)
                nc.vector.tensor_scalar(bT[:, part * KD:(part + 1) * KD, :],
                                        tr[:, part % 2, 0:KD * NE].rearrange("p (k e) -> p k e", k=KD),
                                        1.0 if part == 1 else 0.0, None, ALU.add).then_inc(b_ev, 1)

            def take_x(b):
                for g in range(3):
                    dve.wait_ge(tr_mm, 6 * b + g + 1)
                    if g < 2:
                        dst, src = xT[:, 4 * g:4 * g + 4, 0:P], tr[:, g, :].rearrange("p (k c) -> p k c", k=4)
                    else:
                        dst = xT[:, :, P:CAP].rearrange("p (q h) c -> p h q c", h=2)
                        src = tr[:, 0, 0:2 * P].rearrange("p (h q c) -> p h q c", h=2, q=Q)
                    nc.vector.tensor_copy(dst, src).then_inc(tr_ev, 1)

            def take_y(b, parts):
                for g in parts:
                    dve.wait_ge(tr_mm, 6 * b + 4 + g)
                    if g < 2:
                        nc.vector.tensor_copy(ytok[:, g * HALF:(g + 1) * HALF], tr[:, 1 - g, :]).then_inc(tr_ev, 1)
                    else:
                        nc.vector.tensor_copy(ytok2[:, :, :], tr[:, 1, 0:2 * P].rearrange("p (g f) -> p g f", g=2))\
                            .then_inc(tr_ev, 1)

            take_x(0)

            def body(b, over):
                e = over_expert(dve, b) if over else b
                hold(dve, yp_ev, KD * b + 2, spare_dve)
                nc.vector.tensor_copy(bcur[:, :], bT[:, :, bass.ds(e, 1)].rearrange("p k a -> p (k a)")).then_inc(b_d, 1)
                dve.wait_ge(b_d, b + 1)
                for ft in range(FT):
                    f = FT * b + ft
                    dve.wait_ge(gu_mm, f + 1)
                    nc.vector.tensor_scalar(gs[:, ft % 2, :], gu[:, ft % 4, 0:CAP], bcur[:, ft:ft + 1], LIMIT,
                                            ALU.add, ALU.min).then_inc(g_d, 1)
                    nc.vector.tensor_scalar(us[:, ft % 2, :], gu[:, ft % 4, 256:256 + CAP],
                                            bcur[:, KD + ft:KD + ft + 1], 1.0 - LIMIT, ALU.add, ALU.max)\
                        .then_inc(gu_ev, 1)
                    dve.wait_ge(sg_d, f + 1)
                    nc.vector.tensor_tensor(gs[:, ft % 2, :], gs[:, ft % 2, :], sg[:, ft % 2, :], ALU.mult)\
                        .then_inc(t_d, 1)
                    dve.wait_ge(gu_ev, f + 5)
                    dve.wait_ge(t_d, f + 1)
                    nc.vector.scalar_tensor_tensor(out=hid[:, ft, :], in0=us[:, ft % 2, :], scalar=1.0 + LIMIT,
                                                   in1=gs[:, ft % 2, :], op0=ALU.min, op1=ALU.mult).then_inc(hid_d, 1)
                    if ft == 1:
                        dve.wait_ge(y_out, STORE * b + STORE)
                        take_y(b, (0, 1))
                    if ft == 2:
                        take_y(b, (2,))
                take_x(b + 1)
            nov = over_blocks(dve, body)
            dve.wait_ge(y_out, STORE * (NE + nov) + STORE)
            take_y(NE + nov, (0, 1, 2))

        @block.tensor
        def _(pe):
            def turn_x(b, parts):
                for g in parts:
                    if g == 0:
                        pe.wait_ge(x_in, 32 * b + 32)
                    pe.wait_ge(tr_ev, 6 * b + g + 1)
                    for k in range(4 if g < 2 else 2):
                        src = xg[:, (4 * g + k) * P:(4 * g + k + 1) * P] if g < 2 else xg2[:, k * P:(k + 1) * P]
                        last = nc.tensor.transpose(tr[:, g % 2, k * P:(k + 1) * P], src, ident[:, :])
                    last.then_inc(tr_mm, 1)

            def turn_y(b, parts):
                for g in parts:
                    if g == 0:
                        pe.wait_ge(yp_ev, KD * b + 2)
                    pe.wait_ge(tr_ev, 6 * b + 4 + g)
                    for k in range(4 if g < 2 else 2):
                        src = yT[:, 4 * g + k, :] if g < 2 else \
                            yT2[:, 4 * k:4 * k + 4, :].rearrange("p d c -> p (d c)")
                        last = nc.tensor.transpose(tr[:, (1 + g) % 2, k * P:(k + 1) * P], src, ident[:, :])
                    last.then_inc(tr_mm, 1)

            for part in range(3):
                pe.wait_ge(b_in, 16 * (part + 1))
                after(pe, b_ev, part - 1)
                for k in range(KD):
                    last = nc.tensor.transpose(tr[:, part % 2, k * NE:(k + 1) * NE], brow[:, k * P:(k + 1) * P],
                                               ident[0:NE, 0:NE])
                last.then_inc(b_mm, 1)
            pe.wait_ge(b_ev, 3)
            turn_x(0, (0, 1, 2))
            pe.wait_ge(ini, 4)

            def gate_up(b, ft, width):
                if ft % 2 == 0:
                    pe.wait_ge(w_in_[ft // 2], 32 * b + 32)
                pe.wait_ge(gu_ev, FT * b + ft + 1)
                for part in range(2):
                    for k in range(KD):
                        last = nc.tensor.matmul(gu[:, ft % 4, 256 * part:256 * part + width],
                                                w_tile(ft // 2, ft % 2, k, part), xT[:, k, 0:width],
                                                start=k == 0, stop=k == KD - 1)
                last.then_inc(gu_mm, 1)

            def down(b, dts, width):
                if dts[0] % 4 == 0:
                    pe.wait_ge(w_in_[4 + dts[0] // 4], 32 * b + 32)
                pe.wait_ge(yp_ev, KD * b + dts[-1] + 1)
                for k in range(KD):
                    if dts[0] == 0:
                        pe.wait_ge(hid_d, FT * b + k + 1)
                    for dt in dts:
                        last = nc.tensor.matmul(yp[:, dt % 2, 0:width], w_tile(4 + dt // 4, dt % 4, k), hid[:, k, 0:width],
                                                start=k == 0, stop=k == KD - 1)
                        if k == KD - 1:
                            last.then_inc(yp_mm, 1)

            def multiply(b, width):
                pe.wait_ge(tr_ev, 6 * b + 5)
                for ft in range(FT):
                    gate_up(b, ft, width)
                    if ft == 1:
                        turn_y(b, (0, 1))
                    if ft == 2:
                        turn_y(b, (2,))
                down(b, (0, 1), width)
                turn_x(b + 1, (0, 1))
                for dt in range(2, KD):
                    down(b, (dt,), width)
                    if dt == 3:
                        turn_x(b + 1, (2,))

            def by_width(b, count, widths):
                if len(widths) == 1:
                    multiply(b, widths[0])
                    return
                with pe.If(count < widths[0] + 1):
                    multiply(b, widths[0])
                with pe.Else():
                    by_width(b, count, widths[1:])

            def body(b, over):
                if over:
                    multiply(b, CAP)
                else:
                    by_width(b, pe.value_load(tabs[0:1, bass.ds(b, 1)], min_val=0, max_val=T), WIDTHS)
            nov = over_blocks(pe, body)
            turn_y(NE + nov, (0, 1, 2))


def combine(nc, h_s, y_slots, gates, dest, out):
    SLOTS_ = 2
    with ExitStack() as ctx:
        sb = lambda n, s, d=F32: ctx.enter_context(nc.sbuf_tensor(n, s, d))
        sem = lambda n: ctx.enter_context(nc.semaphore(n))
        hbuf = sb("co_h", [P, NT, D])
        y = sb("co_y", [P, SLOTS_, TOPK, D])
        acc = sb("co_acc", [P, NT, 2, D])
        h_in = [sem(f"co_h_in{t}") for t in range(NT)]
        y_in = [sem(f"co_y_in{s}") for s in range(SLOTS_)]
        add_d, sum_d, y_out = sem("co_add"), sem("co_sum"), sem("co_out")
        out_t = out.rearrange("a (t p) d -> (a t) p d", p=P)
        h_t = h_s.rearrange("(t p) d -> t p d", p=P)
        with nc.Block() as block:
            @block.sync
            def _(sp):
                for t in range(NT):
                    sp.dma_start(hbuf[:, t, :], h_t[t]).then_inc(h_in[t], 16)
                for t in range(NT):
                    sp.wait_ge(sum_d, t + 1)
                    sp.dma_start(out_t[t], acc[:, t, 1, :]).then_inc(y_out, 16)
                sp.wait_ge(y_out, 16 * NT)

            @block.gpsimd
            def _(pool):
                for t in range(NT):
                    if t >= SLOTS_:
                        pool.wait_ge(sum_d, t - SLOTS_ + 1)
                    for j in range(TOPK):
                        pool.indirect_dma_start(out=y[:, t % SLOTS_, j, :], out_offset=None, in_=y_slots[:, :],
                                                in_offset=bass.IndirectOffsetOnAxis(
                                                    ap=dest[:, t * TOPK + j:t * TOPK + j + 1], axis=0))\
                            .then_inc(y_in[t % SLOTS_], 16)

            @block.vector
            def _(dve):
                for t in range(NT):
                    dve.wait_ge(h_in[t], 16)
                    dve.wait_ge(y_in[t % SLOTS_], 16 * TOPK * (t // SLOTS_ + 1))
                    for j in range(TOPK):
                        if j:
                            dve.wait_ge(add_d, (TOPK - 1) * t + j)
                        src = hbuf[:, t, :] if j == 0 else acc[:, t, (j - 1) % 2, :]
                        nc.vector.scalar_tensor_tensor(out=acc[:, t, j % 2, :], in0=y[:, t % SLOTS_, j, :],
                                                       scalar=gates[:, t, j:j + 1], in1=src,
                                                       op0=ALU.mult, op1=ALU.add)\
                            .then_inc(sum_d if j == TOPK - 1 else add_d, 1)


def build(nc, x, attn_norm_w, w_in, q_norm_w, k_norm_w, sinks, w_proj_swa, w_proj_sb, w_out, ffn_norm_w,
          router_w, router_b, w_gate_up, b_gate_up, w_down, b_down, out):
    dram = lambda n, s, d=F32: nc.dram_tensor(n, s, d, kind="Internal").ap()
    gT = dram("gT", (2 * KD, P, T))
    y_s = dram("y_s", (2, T, PAIRS * P))
    h_s = dram("h_s", (T, D))
    xn_s = dram("xn_s", (T, D))
    slot_token = dram("slot_token", (TABLE, 1), I32)
    y_slots = dram("y_slots", (NBLK * CAP, D))
    with ExitStack() as top:
        sbt = lambda n, s, d=F32: top.enter_context(nc.sbuf_tensor(n, s, d))
        ident = sbt("ident", [P, P])
        eps_col = sbt("eps_col", [P, 1])
        nhalf = sbt("nhalf", [P, 1])
        logits = sbt("logits", [P, NT, NE])
        gates = sbt("gates", [P, NT, TOPK])
        dest = sbt("dest", [P, NT * TOPK], U32)
        tabs = sbt("tabs", [1, NE + MAXOVER + 1], I32)
        make_constants(nc, ident, eps_col, nhalf)
        with ExitStack() as front:
            sbf = lambda n, s, d=F32: front.enter_context(nc.sbuf_tensor(n, s, d))
            xnT_hi = sbf("xnT_hi", [P, KD, T], F32R)
            xnT_lo = sbf("xnT_lo", [P, KD, T], F32R)
            norm_and_transpose(nc, x, attn_norm_w, ident, nhalf, xnT_hi, xnT_lo)
            va = sbf("va", [P, NT, PAIRS * HD])
            vb = sbf("vb", [P, NT, PAIRS * P])
            project_values(nc, w_in, xnT_hi, xnT_lo, va, vb)
            attention(nc, w_in, q_norm_w, k_norm_w, sinks, ident, eps_col, xnT_hi, xnT_lo, va, vb, gT,
                      y_s, y_slots)
        with ExitStack() as mid:
            sbm = lambda n, s, d=F32: mid.enter_context(nc.sbuf_tensor(n, s, d))
            mT_hi = sbm("mT_hi", [P, KD, T], F32R)
            mT_lo = sbm("mT_lo", [P, KD, T], F32R)
            merge(nc, w_proj_swa, w_proj_sb, ident, gT, y_s, mT_hi, mT_lo)
            output_and_logits(nc, x, w_out, ffn_norm_w, router_w, router_b, ident, nhalf, mT_hi, mT_lo,
                              h_s, xn_s, logits)
        route(nc, logits, gates, dest, tabs, slot_token)
        experts(nc, xn_s, w_gate_up, b_gate_up, w_down, b_down, ident, dest, tabs, slot_token, y_slots)
        combine(nc, h_s, y_slots, gates, dest, out)


_INS = ["x", "attn_norm_w", "w_in", "q_norm_w", "k_norm_w", "sinks", "w_proj_swa", "w_proj_sb", "w_out",
        "ffn_norm_w", "router_w", "router_b", "w_gate_up", "b_gate_up", "w_down", "b_down"]


def kernel(**inputs):
    import numpy as _np
    import concourse.bacc as _bacc
    from concourse import mybir as _mybir
    from concourse.bass_utils import run_bass_kernel_spmd as _run

    nc = _bacc.Bacc("TRN2", target_bir_lowering=False, num_devices=1)
    arrays, args = {}, []
    for name in _INS:
        a = _np.ascontiguousarray(inputs[name])
        arrays[f"in_{name}_dram"] = a
        args.append(nc.dram_tensor(f"in_{name}_dram", a.shape, _mybir.dt.from_np(a.dtype), kind="ExternalInput").ap())
    args.append(nc.dram_tensor("out_0_dram", (1, T, D), _mybir.dt.float32, kind="ExternalOutput").ap())
    build(nc, *args)
    r = _run(nc, [arrays], core_ids=[0])
    return r.results[0]["out_0_dram"]
```

```python
from contextlib import ExitStack

import concourse.bass as bass
from concourse import mybir

F32 = mybir.dt.float32
F32R = mybir.dt.float32r
BF16 = mybir.dt.bfloat16
I32 = mybir.dt.int32
U32 = mybir.dt.uint32
ALU = mybir.AluOpType
ACT = mybir.ActivationFunctionType
AX_X = mybir.AxisListType.X

P = 128
T = 1024
D = 1024
NT = T // P
KD = D // P
HALF = 512
HD = 64
PAIRS = 4
WIN = 128
QA, KA, VA, QB, KB, VB, GA = 0, 512, 640, 768, 1280, 1792, 2304
IN_WIDTH = 4352
EPS = 1e-5
SCALE = HD ** -0.5
NEG = -1.0e30

NE = 32
TOPK = 4
FF = 1024
LIMIT = 7.0
ALPHA = 1.702
CAP = 160
CAP2 = CAP - P
MAXOVER = (T * TOPK) // CAP
NBLK = NE + MAXOVER
WIDTHS = (128, 136, 144, 152, CAP)


def after(eng, sem, n):
    if not isinstance(n, int) or n > 0:
        eng.wait_ge(sem, n)


def split3(nc, out, w_hi, w_lo, x_hi, x_lo, first, last):
    nc.tensor.matmul(out, w_hi, x_hi, start=first, stop=False)
    nc.tensor.matmul(out, w_hi, x_lo, start=False, stop=False)
    return nc.tensor.matmul(out, w_lo, x_hi, start=False, stop=last)


def make_constants(nc, ident, eps_col, nhalf):
    with ExitStack() as ctx:
        cst = ctx.enter_context(nc.semaphore("cst_zeroed"))
        cst2 = ctx.enter_context(nc.semaphore("cst_done"))
        with nc.Block() as block:
            @block.gpsimd
            def _(pool):
                pool.memset(ident[:, :], 0.0).then_inc(cst, 1)
                pool.memset(eps_col[:, :], EPS).then_inc(cst, 1)
                pool.memset(nhalf[:, :], -0.5).then_inc(cst, 1)
                pool.wait_ge(cst, 3)
                pool.affine_select(out=ident[:, :], in_=ident[:, :], compare_op=ALU.not_equal, fill=1.0,
                                   base=0, pattern=[[-1, P]], channel_multiplier=1).then_inc(cst2, 1)
                pool.wait_ge(cst2, 1)


def norm_and_transpose(nc, x, attn_norm_w, w_in, ident, nhalf, xnT_hi, xnT_lo, raw_v, rawv_in):
    with ExitStack() as ctx:
        sb = lambda n, s, d=F32: ctx.enter_context(nc.sbuf_tensor(n, s, d))
        sem = lambda n: ctx.enter_context(nc.semaphore(n))
        xin = sb("n1_x", [P, NT, D])
        wB = sb("n1_w", [P, D])
        xs = sb("n1_xs", [P, 2, D])
        junk = sb("n1_junk", [P, D])
        ssq = sb("n1_ssq", [P, NT])
        ms = sb("n1_ms", [P, NT])
        rstd = sb("n1_rstd", [P, NT])
        tr = ctx.enter_context(nc.psum_tensor("n1_tr", [P, 4, HALF], F32))
        x_in = [sem(f"n1_x_in{t}") for t in range(NT)]
        w_in_ = sem("n1_w_in")
        sq_done, ms_done, rstd_done = sem("n1_sq"), sem("n1_ms_d"), sem("n1_rstd_d")
        xs_done, tr_done, hi_done, lo_done = sem("n1_xs_d"), sem("n1_tr_d"), sem("n1_hi"), sem("n1_lo")
        x_t = x.rearrange("a (t p) d -> (a t) p d", p=P)
        with nc.Block() as block:
            @block.sync
            def _(sp):
                for t in range(NT):
                    sp.dma_start(xin[:, t, :], x_t[t]).then_inc(x_in[t], 16)
                    if t == 0:
                        sp.dma_start(wB[:, :], attn_norm_w[0:1, :].to_broadcast([P, D])).then_inc(w_in_, 16)
                load_value_weights(sp, w_in, raw_v, rawv_in)

            @block.scalar
            def _(act):
                for t in range(NT):
                    act.wait_ge(x_in[t], 16)
                    if t:
                        act.wait_ge(sq_done, t)
                    nc.scalar.activation(junk[:, :], xin[:, t, :], ACT.Square,
                                         accum_out=ssq[:, t:t + 1]).then_inc(sq_done, 1)
                for m in range(2 * NT):
                    t, g = divmod(m, 2)
                    act.wait_ge(tr_done, m + 1)
                    nc.scalar.activation(xnT_hi[:, 4 * g:4 * g + 4, t * P:(t + 1) * P],
                                         tr[:, m % 4, :].rearrange("p (k c) -> p k c", k=4),
                                         ACT.Copy).then_inc(hi_done, 1)

            @block.gpsimd
            def _(pool):
                for t in range(NT):
                    pool.wait_ge(sq_done, t + 1)
                    nc.gpsimd.tensor_scalar(ms[:, t:t + 1], ssq[:, t:t + 1], 1.0 / D, EPS,
                                            ALU.mult, ALU.add).then_inc(ms_done, 1)
                    pool.wait_ge(ms_done, t + 1)
                    nc.gpsimd.tensor_tensor(rstd[:, t:t + 1], ms[:, t:t + 1], nhalf[:, 0:1],
                                            ALU.pow).then_inc(rstd_done, 1)

            @block.vector
            def _(dve):
                def scale_tile(t):
                    if t == 0:
                        dve.wait_ge(w_in_, 16)
                    dve.wait_ge(rstd_done, t + 1)
                    after(dve, tr_done, 2 * (t - 1))
                    nc.vector.scalar_tensor_tensor(out=xs[:, t % 2, :], in0=xin[:, t, :], scalar=rstd[:, t:t + 1],
                                                   in1=wB[:, :], op0=ALU.mult, op1=ALU.mult).then_inc(xs_done, 1)
                scale_tile(0)
                for t in range(NT):
                    if t + 1 < NT:
                        scale_tile(t + 1)
                    for g in range(2):
                        m = 2 * t + g
                        dve.wait_ge(hi_done, m + 1)
                        nc.vector.tensor_tensor(xnT_lo[:, 4 * g:4 * g + 4, t * P:(t + 1) * P],
                                                tr[:, m % 4, :].rearrange("p (k c) -> p k c", k=4),
                                                xnT_hi[:, 4 * g:4 * g + 4, t * P:(t + 1) * P].bitcast(F32),
                                                ALU.subtract).then_inc(lo_done, 1)

            @block.tensor
            def _(pe):
                for m in range(2 * NT):
                    t, g = divmod(m, 2)
                    pe.wait_ge(xs_done, t + 1)
                    after(pe, lo_done, m - 3)
                    for k in range(4):
                        last = nc.tensor.transpose(tr[:, m % 4, k * P:(k + 1) * P],
                                                   xs[:, t % 2, (4 * g + k) * P:(4 * g + k + 1) * P], ident[:, :])
                    last.then_inc(tr_done, 1)


VW = P + HALF
VH = VW // 2


def load_value_weights(sp, w_in, raw_v, rawv_in):
    w_v = w_in.rearrange("a (k p) c -> p (a k) c", p=P)
    sp.dma_start(raw_v[:, :, 0:P], w_v[:, :, VA:VA + P]).then_inc(rawv_in, 16)
    sp.dma_start(raw_v[:, :, P:VW], w_v[:, :, VB:VB + HALF]).then_inc(rawv_in, 16)


def load_first_tiles(sp, w_in, raw, raw_in):
    w_v = w_in.rearrange("a (k p) c -> p (a k) c", p=P)
    sp.dma_start(raw[:, 0, :, :], w_v[:, :, QA:QA + P]).then_inc(raw_in[0], 32)
    for d in range(2):
        sp.dma_start(raw[:, 1, :, d * HD:(d + 1) * HD], w_v[:, :, KA:KA + HD]).then_inc(raw_in[1], 16)


def project_values(nc, w_in, raw_v, rawv_in, raw, raw_in, xnT_hi, xnT_lo, va, vb):
    with ExitStack() as ctx:
        sb = lambda n, s, d=F32: ctx.enter_context(nc.sbuf_tensor(n, s, d))
        sem = lambda n: ctx.enter_context(nc.semaphore(n))
        w_hi = sb("pv_whi", [P, KD, VW], F32R)
        w_lo = sb("pv_wlo", [P, KD, VW], F32R)
        acc = ctx.enter_context(nc.psum_tensor("pv_acc", [P, 8, HALF], F32))
        hi_done, lo_done, mm_done = sem("pv_hi"), sem("pv_lo"), sem("pv_mm")
        ev_first, ev_second = sem("pv_ev_first"), sem("pv_ev_second")

        with nc.Block() as block:
            @block.sync
            def _(sp):
                load_first_tiles(sp, w_in, raw, raw_in)

            @block.scalar
            def _(act):
                act.wait_ge(rawv_in, 32)
                for k in range(KD):
                    nc.scalar.activation(w_hi[:, k, :], raw_v[:, k, :], ACT.Copy).then_inc(hi_done, 1)
                for t in range(NT):
                    bank = acc[:, 2 * (t % 4), :]
                    act.wait_ge(mm_done, 2 * t + 1)
                    nc.scalar.activation(va[:, t, :].rearrange("p (a o c) -> p a o c", a=2, o=2),
                                         bank[:, 0:P].rearrange("p (a o c) -> p a o c", a=2, o=1)
                                         .to_broadcast([P, 2, 2, HD]), ACT.Copy)
                    nc.scalar.activation(vb[:, t, 0:VH - P], bank[:, P:VH], ACT.Copy).then_inc(ev_first, 1)

            @block.vector
            def _(dve):
                for k in range(KD):
                    dve.wait_ge(hi_done, k + 1)
                    nc.vector.tensor_tensor(w_lo[:, k, :], raw_v[:, k, :], w_hi[:, k, :].bitcast(F32),
                                            ALU.subtract).then_inc(lo_done, 1)
                for t in range(NT):
                    dve.wait_ge(mm_done, 2 * t + 2)
                    nc.vector.tensor_copy(vb[:, t, VH - P:HALF], acc[:, 2 * (t % 4) + 1, 0:VH]).then_inc(ev_second, 1)

            @block.tensor
            def _(pe):
                for t in range(NT):
                    for h in range(2):
                        if t >= 4:
                            pe.wait_ge(ev_second if h else ev_first, t - 3)
                        for k in range(KD):
                            if t == 0 and h == 0:
                                pe.wait_ge(lo_done, k + 1)
                            last = split3(nc, acc[:, 2 * (t % 4) + h, 0:VH],
                                          xnT_hi[:, k, t * P:(t + 1) * P], xnT_lo[:, k, t * P:(t + 1) * P],
                                          w_hi[:, k, h * VH:(h + 1) * VH], w_lo[:, k, h * VH:(h + 1) * VH],
                                          k == 0, k == KD - 1)
                        last.then_inc(mm_done, 1)


def hold(eng, sem, value, spare):
    eng.wait_ge(sem, value)
    eng.sem_inc(spare, 1)


SB_UNITS = [("sb", i, (h,)) for i in range(NT - 1, NT // 2 - 1, -1) for h in range(2)] + \
           [("sb", i, (0, 1)) for i in range(NT // 2 - 1, -1, -1)]
SWA_UNITS = [("swa", n, (0, 1)) for n in range(NT)]
UNITS = SB_UNITS + SWA_UNITS
NU, NSB, NSWA = len(UNITS), len(SB_UNITS), len(SWA_UNITS)


def unit_tiles(unit):
    kind, i, heads = unit
    first = max(i - 1, 0) if kind == "swa" else 0
    return [(s, kb) for s in range(len(heads)) for kb in range(first, i + 1)]


GROUPS = [-(-len(unit_tiles(u)) // 4) for u in UNITS]
GROUP0 = [sum(GROUPS[:n]) for n in range(NU)]
NG = sum(GROUPS)
PAIR_TILES = ["qa", "ka", "qb", "kb"]
GATE_TILES = ["g"] * 4


def attention(nc, w_in, q_norm_w, k_norm_w, sinks, ident, eps_col, raw, raw_in, xnT_hi, xnT_lo, va, vb, gT, y_s,
              y_slots):
    with ExitStack() as ctx:
        sb = lambda n, s, d=F32: ctx.enter_context(nc.sbuf_tensor(n, s, d))
        sem = lambda n: ctx.enter_context(nc.semaphore(n))
        ps = lambda n, s: ctx.enter_context(nc.psum_tensor(n, s, F32))
        w_hi = sb("at_whi", [P, 2, KD, P], F32R)
        w_lo = sb("at_wlo", [P, 2, KD, P], F32R)
        cur = {k: sb(f"at_cur_{k}", [P, T]) for k in PAIR_TILES}
        nxt = {k: sb(f"at_nxt_{k}", [P, T]) for k in PAIR_TILES}
        t1 = sb("at_t1", [P, 2, 2 * HALF])
        soft = sb("at_soft", [P, 2, 2 * HALF])
        logw = sb("at_logw", [P, 2, 2 * HALF])
        prob = sb("at_prob", [P, 2, 2 * HALF])
        probT = sb("at_probT", [P, 2, 8, P])
        sq = sb("at_sq", [P, HALF])
        rs = sb("at_rs", [P, HALF])
        gst = sb("at_gst", [P, 2, HALF])
        yst = sb("at_yst", [P, 2, P])
        bias = sb("at_bias", [P, 8, 2 * P])
        rel = sb("at_rel", [P, 2 * P])
        ones_blk = sb("at_ones_blk", [P, P])
        one_col = sb("at_one", [P, 1])
        wcol = sb("at_wcol", [P, 2])
        sinkB = sb("at_sink", [P, 8])
        nsinkB = sb("at_nsink", [P, 8])
        stat = {k: sb(f"at_{k}", [P, 2, 2]) for k in ("mx", "negm", "dsink", "rsum", "esink", "den", "rden")}
        z = ps("at_z", [P, 4, HALF])
        job = ps("at_job", [P, HALF])
        aux = ps("at_aux", [P, HALF])
        tr = ps("at_tr", [P, HALF])
        pv = ps("at_pv", [P, HALF])

        ZW = 500
        zeros = sb("at_zeros", [P, 1, ZW])
        z_out = sem("z_out")
        c_in, c_set, c_rel, c_bias, c_sink = (sem(n) for n in ("c_in", "c_set", "c_rel", "c_bias", "c_sink"))
        whi_d, wlo_d = sem("whi_d"), sem("wlo_d")
        job_mm = sem("job_mm")
        job_ev = sem("job_ev")
        sq_d, ss_d, rs_d = sem("sq_d"), sem("ss_d"), sem("rs_d")
        g_out = [sem(f"g_out{s}") for s in range(2)]
        s_done = sem("s_done")
        z_free = sem("z_free")
        a_st = sem("a_st")
        d_soft = sem("d_soft")
        p_soft = sem("p_soft")
        d_scan = sem("d_scan")
        w_st, n_st = sem("w_st"), sem("n_st")
        a2_done = sem("a2_done")
        p_prob = sem("p_prob")
        tr_mm = sem("tr_mm")
        tr_ev = sem("tr_ev")
        pv_mm = sem("pv_mm")
        y_ev = sem("y_ev")
        y_out = [sem(f"y_out{s}") for s in range(2)]
        cur_d, cur_a = sem("cur_d"), sem("cur_a")
        spare_pool = sem("spare_pool")

        w_v = w_in.rearrange("a (k p) c -> p (a k) c", p=P)
        slot = lambda u: u % 2
        width = lambda unit: P * (unit[1] + 1)

        def zsl(u):
            kind, i, heads = UNITS[u]
            s = slot(u)
            if kind == "swa":
                return z[:, 2 * s:2 * s + 2, (0 if i else P):2 * P]
            if len(heads) == 2:
                return z[:, 2 * s:2 * s + 2, 0:width(UNITS[u])]
            return z[:, 2 * s:2 * s + 2, :].rearrange("p a c -> p (a c)")[:, 0:width(UNITS[u])]

        def bsl(buf, u):
            kind, i, heads = UNITS[u]
            s = slot(u)
            if kind == "swa":
                return buf[:, s, :].rearrange("p (a c) -> p a c", a=2)[:, :, (0 if i else P):2 * P]
            if len(heads) == 2:
                return buf[:, s, :].rearrange("p (a c) -> p a c", a=2)[:, :, 0:width(UNITS[u])]
            return buf[:, s, 0:width(UNITS[u])]

        def head_sl(buf, u, hs):
            v = bsl(buf, u)
            return v if len(UNITS[u][2]) == 1 else v[:, hs, :]

        def diag(buf, u):
            w = width(UNITS[u])
            v = bsl(buf, u)
            return v[:, w - P:w] if len(UNITS[u][2]) == 1 else v[:, :, w - P:w]

        block = ctx.enter_context(nc.Block())
        busy = {1, 2, 3, 4}
        steps_full = {u: n for n, u in enumerate(u for u in range(NU) if u not in busy)}
        steps_last = {0: 0} | {NSB + n: n for n in range(1, NSWA)}

        def over_pairs(eng, body):
            with eng.Fori(0, PAIRS - 1) as p:
                body(p, PAIR_TILES + GATE_TILES, steps_full)
            body(PAIRS - 1, GATE_TILES, steps_last)

        @block.sync
        def _(sp):
            sp.dma_start(wcol[0:HD, 0:1], q_norm_w.rearrange("a (c b) -> (a c) b", b=1)).then_inc(c_in, 16)
            sp.dma_start(wcol[HD:P, 0:1], q_norm_w.rearrange("a (c b) -> (a c) b", b=1)).then_inc(c_in, 16)
            sp.dma_start(wcol[0:HD, 1:2], k_norm_w.rearrange("a (c b) -> (a c) b", b=1)).then_inc(c_in, 16)
            sp.dma_start(wcol[HD:P, 1:2], k_norm_w.rearrange("a (c b) -> (a c) b", b=1)).then_inc(c_in, 16)
            sp.dma_start(sinkB[:, :], sinks[0:1, :].to_broadcast([P, 8])).then_inc(c_in, 16)
            for s in range(2):
                sp.sem_inc(g_out[s], 16)

            def load(f, kind, pair, kvh, tl):
                s = tl % 2
                sp.wait_ge(wlo_d, f + 1)
                if kind == "ka":
                    for d in range(2):
                        sp.dma_start(raw[:, s, :, d * HD:(d + 1) * HD],
                                     w_v[:, :, bass.ds(KA + HD * kvh, HD)]).then_inc(raw_in[s], 16)
                    return
                col = {"qa": QA + P * pair, "qb": QB + P * pair, "kb": KB + P * pair, "g": GA + P * pair}[kind]
                sp.dma_start(raw[:, s, :, :], w_v[:, :, bass.ds(col, P)]).then_inc(raw_in[s], 32)

            for tl in range(2, len(PAIR_TILES)):
                load(tl, PAIR_TILES[tl], 0, 0, tl)

            def body(p, tiles, steps, kvh_next):
                fb = 4 + 8 * p

                def ld(tl):
                    kind = tiles[tl]
                    gate = tl - (len(tiles) - len(GATE_TILES))
                    load(fb + tl, kind, 4 * p + gate if kind == "g" else p + 1, kvh_next, tl)

                ld(0)
                for tl, kind in enumerate(tiles):
                    if tl + 1 < len(tiles):
                        ld(tl + 1)
                    if kind == "g":
                        g = 4 * p + tl - (len(tiles) - len(GATE_TILES))
                        for half in range(2):
                            sp.wait_ge(job_ev, 2 * (fb + tl) + half + 2)
                            sp.dma_start(gT[bass.ds(g, 1), :, half * HALF:(half + 1) * HALF].rearrange("a p c -> (a p) c"),
                                         gst[:, half, :]).then_inc(g_out[half], 16)

            body(0, PAIR_TILES + GATE_TILES, steps_full, 0)
            with sp.Fori(1, PAIRS - 1) as p:
                body(p, PAIR_TILES + GATE_TILES, steps_full, 1)
            body(PAIRS - 1, GATE_TILES, steps_last, 1)
            for s in range(2):
                sp.wait_ge(g_out[s], 16 * (16 + 1))

        @block.scalar
        def _(act):
            act.preload_act_table_set("natural_log_exp_and_others")
            act.sem_inc(a2_done, 2)
            act.sem_inc(tr_ev, 1)
            act.sem_inc(job_ev, 1)
            for s in range(2):
                act.sem_inc(y_out[s], 16)

            def split_hi(f, tl):
                s = tl % 2
                act.wait_ge(raw_in[s], 16 * (f + 2 - tl % 2))
                act.wait_ge(job_mm, 2 * f + 2)
                nc.scalar.activation(w_hi[:, s, :, :], raw[:, s, :, :], ACT.Copy).then_inc(whi_d, 1)

            def finish_job(j, jl, kind, g, job=job):
                half = jl % 2
                act.wait_ge(job_mm, j + 5)
                if kind in ("qb", "kb"):
                    nc.scalar.activation(nxt[kind][:, half * HALF:(half + 1) * HALF], job[:, :], ACT.Copy,
                                         scale=SCALE if kind == "qb" else 1.0).then_inc(job_ev, 1)
                elif kind == "g":
                    act.wait_ge(g_out[half], 16 * (g + 1))
                    nc.scalar.activation(gst[:, half, :], job[:, :], ACT.Copy).then_inc(job_ev, 1)
                else:
                    nc.scalar.activation(sq[:, :], job[:, :], ACT.Square).then_inc(sq_d, 1)

            def finish_norm(nidx):
                act.wait_ge(ss_d, nidx + 1)
                nc.scalar.activation(rs[:, :], aux[:, :], ACT.Ln, bias=eps_col[:, 0:1], scale=1.0 / HD)\
                    .then_inc(rs_d, 1)
                act.wait_ge(rs_d, 2 * nidx + 1)
                nc.scalar.activation(rs[:, :], rs[:, :], ACT.Exp, scale=-0.5).then_inc(rs_d, 1)

            def promote(sb_scores, j_last):
                after(act, s_done, sb_scores)
                act.wait_ge(job_ev, j_last + 2)
                for kind in ("qb", "kb"):
                    nc.scalar.activation(cur[kind][:, :], nxt[kind][:, :], ACT.Copy).then_inc(cur_a, 1)

            def a1(p, u, part):
                if u >= NU or UNITS[u][0] != "sb":
                    return
                v = NSB * p + u
                if part == 0:
                    act.wait_ge(s_done, NU * p + u + 1)
                    act.wait_ge(d_soft, v + 1)
                    nc.scalar.activation(bsl(t1, u), zsl(u), ACT.Abs).then_inc(a_st, 1)
                    return
                act.wait_ge(a_st, 3 * v + 1)
                nc.scalar.activation(bsl(t1, u), bsl(t1, u), ACT.Exp, scale=-1.0).then_inc(a_st, 1)
                act.wait_ge(a_st, 3 * v + 2)
                nc.scalar.activation(bsl(t1, u), bsl(t1, u), ACT.Ln, bias=1.0).then_inc(a_st, 1)

            def a2(p, u):
                s = slot(u)
                act.wait_ge(pv_mm, NU * p + u + 1)
                if UNITS[u][0] == "sb":
                    act.wait_ge(z_free, NU * p + u + 3)
                    nc.scalar.activation(bsl(prob, u), bsl(logw, u), ACT.Exp).then_inc(a2_done, 1)
                    return
                w = NSWA * p + u - NSB
                act.wait_ge(w_st, 3 * w + 3)
                for h in range(2):
                    nc.scalar.activation(head_sl(prob, u, h), head_sl(logw, u, h), ACT.Exp,
                                         bias=stat["negm"][:, s, h:h + 1], accum_out=stat["rsum"][:, s, h:h + 1])
                nc.scalar.activation(stat["esink"][:, s, :], stat["dsink"][:, s, :], ACT.Exp).then_inc(a2_done, 1)

            def evac_tr(p, u, groups):
                tiles = unit_tiles(UNITS[u])
                for g in groups:
                    n = min(4, len(tiles) - 4 * g)
                    act.wait_ge(tr_mm, NG * p + GROUP0[u] + g + 1)
                    nc.scalar.activation(probT[:, slot(u), 4 * g:4 * g + n, :].rearrange("p a c -> p (a c)"),
                                         tr[:, 0:n * P], ACT.Copy).then_inc(tr_ev, 1)

            def store_y(p, u):
                kind, i, heads = UNITS[u]
                s, n = slot(u), len(heads) * HD
                act.wait_ge(y_ev, NU * p + u + 2)
                act.dma_start(y_s[1 if kind == "sb" else 0, i * P:(i + 1) * P, bass.ds(P * p + HD * heads[0], n)],
                              yst[:, s, 0:n]).then_inc(y_out[s], 16)

            split_hi(0, 0)
            split_hi(1, 1)
            for jl in range(8):
                if jl == 4:
                    act.wait_ge(job_ev, 5)
                finish_job(jl, jl, PAIR_TILES[jl // 2], 0, z[:, jl % 4, :])
                if jl in (1, 3):
                    split_hi(2 + jl // 2, 2 + jl // 2)
                if jl < 4:
                    act.wait_ge(job_ev, jl + 1)
                    finish_norm(jl)
            promote(0, 7)

            def body(p, tiles, steps):
                fb = 4 + 8 * p
                split_hi(fb, 0)
                for u in (0, 1):
                    a1(p, u, 0)
                    a1(p, u, 1)
                for u in range(NU):
                    norm = u in steps and tiles[steps[u] // 2] in ("qa", "ka")
                    a2(p, u)
                    evac_tr(p, u, (0,))
                    if u:
                        store_y(p, u - 1)
                    a1(p, u + 2, 0)
                    if not norm:
                        evac_tr(p, u, range(1, GROUPS[u]))
                    a1(p, u + 2, 1)
                    if u in steps:
                        jl = steps[u]
                        tl = jl // 2
                        if jl % 2 == 0 and tl + 1 < len(tiles):
                            split_hi(fb + tl + 1, tl + 1)
                        finish_job(2 * fb + jl, jl, tiles[tl], 4 * p + tl - (len(tiles) - 4))
                    if norm:
                        evac_tr(p, u, range(1, GROUPS[u]))
                        finish_norm(4 + 4 * p + steps[u])
                    if u == NSB + 4 and len(tiles) > 4:
                        promote(NU * p + NSB, 2 * fb + 7)
                store_y(p, NU - 1)
            over_pairs(act, body)
            for s in range(2):
                act.wait_ge(y_out[s], 16 * (NU // 2 * PAIRS + 1))

        @block.gpsimd
        def _(pool):
            pool.sem_inc(wlo_d, 2)
            nc.gpsimd.memset(ones_blk[:, :], 0.0).then_inc(c_set, 1)
            nc.gpsimd.memset(one_col[:, :], 1.0).then_inc(c_set, 1)
            nc.gpsimd.memset(zeros[:, :, :], 0.0).then_inc(c_set, 1)
            pool.wait_ge(c_set, 3)
            for h in range(2):
                nc.gpsimd.memset(ones_blk[h * HD:(h + 1) * HD, h * HD:(h + 1) * HD], 1.0).then_inc(c_set, 1)
                pool.wait_ge(c_set, 4 + h)

            def split_lo(f, tl):
                s = tl % 2
                pool.wait_ge(whi_d, f + 1)
                nc.gpsimd.tensor_tensor(w_lo[:, s, :, :], raw[:, s, :, :], w_hi[:, s, :, :].bitcast(F32),
                                        ALU.subtract).then_inc(wlo_d, 1)

            split_lo(0, 0)
            nc.gpsimd.iota(rel[:, :], [[-1, 2 * P]], base=P, channel_multiplier=1,
                           allow_small_or_imprecise_dtypes=True).then_inc(c_rel, 1)
            pool.wait_ge(c_rel, 1)
            for h in range(8):
                nc.gpsimd.tensor_scalar(bias[:, h, :], rel[:, :], -(2.0 ** -(h + 1)), None, ALU.mult).then_inc(c_bias, 1)
            pool.wait_ge(c_bias, 8)
            nc.gpsimd.affine_select(out=bias[:, :, :], in_=bias[:, :, :], compare_op=ALU.is_ge, fill=NEG, base=P,
                                    pattern=[[0, 8], [-1, 2 * P]], channel_multiplier=1).then_inc(c_bias, 1)
            pool.wait_ge(c_bias, 9)
            nc.gpsimd.affine_select(out=bias[:, :, :], in_=bias[:, :, :], compare_op=ALU.is_ge, fill=NEG, base=-1,
                                    pattern=[[0, 8], [1, 2 * P]], channel_multiplier=-1).then_inc(c_bias, 1)
            for tl in range(1, 4):
                split_lo(tl, tl)
            further = y_slots[NE * CAP:NBLK * CAP, :].rearrange("r c -> (r c)").rearrange("(p n c) -> p n c", p=P, c=ZW)
            pool.dma_start(further, zeros[:, :, :].to_broadcast([P, MAXOVER * CAP * D // (P * ZW), ZW])).then_inc(z_out, 16)

            def mask(buf, u, done):
                d = diag(buf, u)
                pat = [[-1, P]] if len(UNITS[u][2]) == 1 else [[0, 2], [-1, P]]
                nc.gpsimd.affine_select(out=d, in_=d, compare_op=ALU.is_gt, fill=0.0, base=0, pattern=pat,
                                        channel_multiplier=1).then_inc(done, 1)

            def body(p, tiles, steps):
                fb = 4 + 8 * p
                split_lo(fb, 0)
                for u in range(NU):
                    if UNITS[u][0] == "sb":
                        v = NSB * p + u
                        if u == 0:
                            hold(pool, d_soft, v + 3, spare_pool)
                            mask(soft, u, p_soft)
                        hold(pool, a2_done, NU * p + u + 3, spare_pool)
                        mask(prob, u, p_prob)
                        if u + 1 < NSB:
                            hold(pool, d_soft, v + 4, spare_pool)
                            mask(soft, u + 1, p_soft)
                    if u in steps and steps[u] % 2 == 0 and steps[u] // 2 + 1 < len(tiles):
                        tl = steps[u] // 2 + 1
                        split_lo(fb + tl, tl)
            over_pairs(pool, body)
            pool.wait_ge(z_out, 16)

        @block.vector
        def _(dve):
            dve.sem_inc(z_free, 2)
            dve.sem_inc(d_soft, 2)
            dve.sem_inc(y_ev, 1)
            dve.wait_ge(c_in, 80)
            nc.vector.tensor_scalar(nsinkB[:, :], sinkB[:, :], -1.0, None, ALU.mult).then_inc(c_sink, 1)
            nc.vector.tensor_scalar(wcol[:, 0:1], wcol[:, 0:1], SCALE, None, ALU.mult).then_inc(c_sink, 1)
            dve.wait_ge(c_sink, 2)

            def finish_norm(nidx, jl, kind, job=job):
                half = jl % 2
                c = 0 if kind == "qa" else 1
                dve.wait_ge(rs_d, 2 * nidx + 2)
                nc.vector.scalar_tensor_tensor(out=nxt[kind][:, half * HALF:(half + 1) * HALF], in0=job[:, :],
                                               scalar=wcol[:, c:c + 1], in1=rs[:, :], op0=ALU.mult,
                                               op1=ALU.mult).then_inc(job_ev, 1)

            def promote(p, j_last):
                after(dve, s_done, NU * p)
                dve.wait_ge(job_ev, j_last + 2)
                for kind in ("qa", "ka"):
                    nc.vector.tensor_copy(cur[kind][:, :], nxt[kind][:, :]).then_inc(cur_d, 1)

            def weights(p, u):
                v = NSB * p + u
                dve.wait_ge(a_st, 3 * v + 3)
                nc.vector.scalar_tensor_tensor(out=bsl(soft, u), in0=zsl(u), scalar=0.0, in1=bsl(t1, u),
                                               op0=ALU.max, op1=ALU.add).then_inc(d_soft, 1)
                dve.wait_ge(p_soft, v + 1)
                dve.wait_ge(a2_done, NU * p + u + 1)
                w = width(UNITS[u])
                for hs in range(len(UNITS[u][2])):
                    src, dst = head_sl(soft, u, hs), head_sl(logw, u, hs)
                    last = nc.vector.tensor_tensor_scan(out=dst[:, ::-1], data0=one_col[:, 0:1].to_broadcast([P, w]),
                                                        data1=src[:, ::-1], initial=0.0, op0=ALU.mult, op1=ALU.add)
                last.then_inc(d_scan, 1)
                dve.wait_ge(d_scan, v + 1)
                nc.vector.tensor_tensor(bsl(logw, u), zsl(u), bsl(logw, u), ALU.subtract).then_inc(z_free, 1)

            def scores(p, u):
                s, n = slot(u), UNITS[u][1]
                w = NSWA * p + u - NSB
                lo = 0 if n else P
                dve.wait_ge(s_done, NU * p + u + 1)
                dve.wait_ge(a2_done, NU * p + u + 1)
                nc.vector.tensor_tensor(bsl(logw, u), zsl(u), bias[:, bass.ds(2 * p, 2), lo:2 * P], ALU.add)\
                    .then_inc(z_free, 1)
                dve.wait_ge(z_free, NU * p + u + 3)
                nc.vector.tensor_reduce(stat["mx"][:, s, :], bsl(logw, u), AX_X, ALU.max).then_inc(w_st, 1)
                dve.wait_ge(w_st, 3 * w + 1)
                nc.vector.scalar_tensor_tensor(out=stat["negm"][:, s, :], in0=stat["mx"][:, s, :], scalar=-1.0,
                                               in1=nsinkB[:, bass.ds(2 * p, 2)], op0=ALU.mult, op1=ALU.min)\
                    .then_inc(w_st, 1)
                dve.wait_ge(w_st, 3 * w + 2)
                nc.vector.tensor_tensor(stat["dsink"][:, s, :], sinkB[:, bass.ds(2 * p, 2)], stat["negm"][:, s, :],
                                        ALU.add).then_inc(w_st, 1)

            def denominators(p, u):
                s = slot(u)
                w = NSWA * p + u - NSB
                dve.wait_ge(a2_done, NU * p + u + 3)
                nc.vector.tensor_tensor(stat["den"][:, s, :], stat["rsum"][:, s, :], stat["esink"][:, s, :],
                                        ALU.add).then_inc(n_st, 1)
                dve.wait_ge(n_st, 2 * w + 1)
                nc.vector.reciprocal(stat["rden"][:, s, :], stat["den"][:, s, :]).then_inc(n_st, 1)

            def result(p, u):
                kind, i, heads = UNITS[u]
                s, n = slot(u), len(heads) * HD
                if kind == "swa":
                    dve.wait_ge(n_st, 2 * (NSWA * p + u - NSB) + 2)
                dve.wait_ge(y_out[s], 16 * (NU // 2 * p + u // 2 + 1))
                dve.wait_ge(pv_mm, NU * p + u + 3)
                if kind == "sb":
                    nc.vector.tensor_copy(yst[:, s, 0:n], pv[:, 0:n]).then_inc(y_ev, 1)
                else:
                    nc.vector.tensor_scalar(yst[:, s, 0:HD], pv[:, 0:HD], stat["rden"][:, s, 0:1], None, ALU.mult)
                    nc.vector.tensor_scalar(yst[:, s, HD:P], pv[:, HD:P], stat["rden"][:, s, 1:2], None, ALU.mult)\
                        .then_inc(y_ev, 1)

            for jl in range(4):
                finish_norm(jl, jl, PAIR_TILES[jl // 2], z[:, jl, :])
            promote(0, 7)
            dve.wait_ge(c_set, 5)
            dve.wait_ge(c_bias, 10)

            def body(p, tiles, steps):
                fb = 4 + 8 * p

                def prepare(u):
                    weights(p, u) if UNITS[u][0] == "sb" else scores(p, u)

                prepare(0)
                for u in range(NU):
                    if u + 1 < NU:
                        prepare(u + 1)
                    if UNITS[u][0] == "swa":
                        denominators(p, u)
                    if u in steps and tiles[steps[u] // 2] in ("qa", "ka"):
                        finish_norm(4 + 4 * p + steps[u], steps[u], tiles[steps[u] // 2])
                    result(p, u)
                if len(tiles) > 4:
                    promote(p + 1, 2 * fb + 7)
            over_pairs(dve, body)

        @block.tensor
        def _(pe):
            pe.sem_inc(job_mm, 4)
            pe.sem_inc(pv_mm, 2)

            def project(j, f, tl, half, job=job, free=None):
                s = tl % 2
                pe.wait_ge(wlo_d, f + 3)
                after(pe, job_ev, j + 1 if free is None else free)
                for k in range(KD):
                    xh, xl = (v[:, k, half * HALF:(half + 1) * HALF] for v in (xnT_hi, xnT_lo))
                    last = split3(nc, job[:, :], w_hi[:, s, k, :], w_lo[:, s, k, :], xh, xl, k == 0, k == KD - 1)
                last.then_inc(job_mm, 1)

            def sum_squares(nidx):
                pe.wait_ge(sq_d, nidx + 1)
                nc.tensor.matmul(aux[:, :], ones_blk[:, :], sq[:, :], start=True, stop=True).then_inc(ss_d, 1)

            def score(p, u):
                kind, i, heads = UNITS[u]
                s = slot(u)
                q, k = (cur["qa"], cur["ka"]) if kind == "swa" else (cur["qb"], cur["kb"])
                pe.wait_ge(z_free, NU * p + u + 1)
                for hs, h in enumerate(heads):
                    lhs = q[h * HD:(h + 1) * HD, i * P:(i + 1) * P]
                    if kind == "swa":
                        lo = 0 if i else P
                        outs = [(z[:, 2 * s + hs, lo:2 * P], (i - 1) * P + lo, (i + 1) * P)]
                    elif len(heads) == 2:
                        outs = [(z[:, 2 * s + hs, 0:width(UNITS[u])], 0, width(UNITS[u]))]
                    else:
                        outs = [(z[:, 2 * s, :], 0, HALF), (z[:, 2 * s + 1, 0:width(UNITS[u]) - HALF], HALF, width(UNITS[u]))]
                    for out, k0, k1 in outs:
                        last = nc.tensor.matmul(out, lhs, k[h * HD:(h + 1) * HD, k0:k1], start=True, stop=True)
                last.then_inc(s_done, 1)

            def turn(p, u, groups):
                kind, i, heads = UNITS[u]
                tiles = unit_tiles(UNITS[u])
                if kind == "sb":
                    pe.wait_ge(p_prob, NSB * p + u + 1)
                else:
                    pe.wait_ge(a2_done, NU * p + u + 3)
                first = tiles[0][1]
                for g in groups:
                    pe.wait_ge(tr_ev, NG * p + GROUP0[u] + g + 1)
                    for n, (hs, kb) in enumerate(tiles[4 * g:4 * g + 4]):
                        src = head_sl(prob, u, hs)
                        c = (kb - first) * P
                        last = nc.tensor.transpose(tr[:, n * P:(n + 1) * P], src[:, c:c + P], ident[:, :])
                    last.then_inc(tr_mm, 1)

            def weigh(p, u):
                kind, i, heads = UNITS[u]
                tiles = unit_tiles(UNITS[u])
                pe.wait_ge(tr_ev, NG * p + GROUP0[u] + GROUPS[u] + 1)
                pe.wait_ge(y_ev, NU * p + u + 1)
                for hs, h in enumerate(heads):
                    mine = [(n, kb) for n, (a, kb) in enumerate(tiles) if a == hs]
                    for m, (n, kb) in enumerate(mine):
                        v = vb[:, kb, bass.ds(P * p + HD * h, HD)] if kind == "sb" else va[:, kb, bass.ds(HD * p, HD)]
                        last = nc.tensor.matmul(pv[:, hs * HD:(hs + 1) * HD], probT[:, slot(u), n, :], v,
                                                start=m == 0, stop=m == len(mine) - 1)
                last.then_inc(pv_mm, 1)

            pe.wait_ge(c_set, 5)
            for jl in range(8):
                project(jl, jl // 2, jl // 2, jl % 2, z[:, jl % 4, :], jl - 2 if jl > 3 else 0)
                if 1 <= jl <= 4:
                    after(pe, rs_d, 2 * jl - 3)
                    sum_squares(jl - 1)

            def body(p, tiles, steps):
                fb = 4 + 8 * p
                pe.wait_ge(cur_a, 2 * p + 2)
                score(p, 0)
                score(p, 1)
                for u in range(NU):
                    norm = u in steps and tiles[steps[u] // 2] in ("qa", "ka")

                    def job_of(u):
                        jl = steps[u]
                        project(2 * fb + jl, fb + jl // 2, jl // 2, jl % 2)

                    if u == 0:
                        job_of(u)
                    turn(p, u, (0,))
                    if u + 2 == NSB:
                        pe.wait_ge(cur_d, 2 * p + 2)
                    if u + 2 < NU:
                        score(p, u + 2)
                    if not norm:
                        turn(p, u, range(1, GROUPS[u]))
                    if u in steps and u:
                        job_of(u)
                    if norm:
                        turn(p, u, range(1, GROUPS[u]))
                        sum_squares(4 + 4 * p + steps[u])
                    weigh(p, u)

            over_pairs(pe, body)


def merge(nc, w_proj_swa, w_proj_sb, ident, gT, y_s, mT_hi, mT_lo, w_out, raw_o, raw_o_in):
    KA4 = PAIRS
    with ExitStack() as ctx:
        sb = lambda n, s, d=F32: ctx.enter_context(nc.sbuf_tensor(n, s, d))
        sem = lambda n: ctx.enter_context(nc.semaphore(n))
        yT_hi = sb("mg_yThi", [P, 2, KA4, T], F32R)
        yT_lo = sb("mg_yTlo", [P, 2, KA4, T], F32R)
        ytok = sb("mg_ytok", [P, 4, HALF])
        raw = sb("mg_raw", [P, 2, 2, KA4, P])
        w_hi = sb("mg_whi", [P, 2, 2, KA4, P], F32R)
        w_lo = sb("mg_wlo", [P, 2, 2, KA4, P], F32R)
        g = sb("mg_g", [P, 2, 2, HALF])
        prod = sb("mg_prod", [P, 2, 2, HALF])
        acc = ctx.enter_context(nc.psum_tensor("mg_acc", [P, 4, HALF], F32))
        tr = ctx.enter_context(nc.psum_tensor("mg_tr", [P, 4, HALF], F32))
        y_in = [sem(f"mg_y_in{s}") for s in range(4)]
        raw_in = [sem(f"mg_raw_in{s}") for s in range(2)]
        g_in = [sem(f"mg_g_in{s}") for s in range(2)]
        tr_mm, yhi, ylo = sem("mg_tr_mm"), sem("mg_yhi"), sem("mg_ylo")
        whi_d, wlo_d = sem("mg_whi_d"), sem("mg_wlo_d")
        mm_done = sem("mg_mm")
        sg_done = sem("mg_sg")
        pr_done = sem("mg_pr")
        sum_done, mhi, mlo = sem("mg_sum"), sem("mg_mhi"), sem("mg_mlo")
        pa_v = w_proj_swa.rearrange("a (k p) c -> p (a k) c", p=P)
        pb_v = w_proj_sb.rearrange("a (k p) c -> p (a k) c", p=P)

        def over_tiles(eng, body):
            with eng.Fori(0, KD // 2 - 1) as i:
                for s in range(2):
                    body(2 * i + s, s, True)
            body(KD - 2, 0, True)
            body(KD - 1, 1, False)

        with nc.Block() as block:
            @block.sync
            def _(sp):
                def load_w(m, s):
                    sp.wait_ge(wlo_d, m + 1)
                    for n, v in enumerate((pa_v, pb_v)):
                        sp.dma_start(raw[:, s, n, :, :], v[:, :, bass.ds(m * P, P)]).then_inc(raw_in[s], 16)

                def body(m, s, more):
                    for half in range(2):
                        sp.wait_ge(pr_done, 2 * m + half + 1)
                        for n in range(2):
                            sp.dma_start(g[:, half, n, :],
                                         gT[bass.ds(KD * n + m, 1), :, half * HALF:(half + 1) * HALF]
                                         .rearrange("a p c -> (a p) c")).then_inc(g_in[half], 16)
                    if more:
                        load_w(m + 1, 1 - s)

                for n in range(2 * NT):
                    t, a = divmod(n, 2)
                    after(sp, tr_mm, n - 3)
                    sp.dma_start(ytok[:, n % 4, :], y_s[a, t * P:(t + 1) * P, :]).then_inc(y_in[n % 4], 16)
                load_w(0, 0)
                over_tiles(sp, body)
                for k in range(4):
                    sp.dma_start(raw_o[:, k, :], w_out[0, k * P:(k + 1) * P, :]).then_inc(raw_o_in[k], 16)

            @block.scalar
            def _(act):
                def split_hi(m, s):
                    act.wait_ge(raw_in[s], 16 * (m + 2 - s))
                    act.wait_ge(mm_done, 2 * m + 1)
                    nc.scalar.activation(w_hi[:, s], raw[:, s], ACT.Copy).then_inc(whi_d, 1)

                def body(m, s, more):
                    if more:
                        split_hi(m + 1, 1 - s)
                    for half in range(2):
                        n = 2 * m + half
                        act.wait_ge(g_in[half], 32 * (m + 1))
                        nc.scalar.activation(g[:, half], g[:, half], ACT.Sigmoid).then_inc(sg_done, 1)
                    for half in range(2):
                        n = 2 * m + half
                        act.wait_ge(sum_done, n + 1)
                        nc.scalar.activation(mT_hi[:, bass.ds(m, 1), half * HALF:(half + 1) * HALF]
                                             .rearrange("p a c -> p (a c)"),
                                             prod[:, half, 0, :], ACT.Copy).then_inc(mhi, 1)

                for n in range(2 * NT):
                    t, a = divmod(n, 2)
                    act.wait_ge(tr_mm, n + 1)
                    nc.scalar.activation(yT_hi[:, a, :, t * P:(t + 1) * P],
                                         tr[:, n % 4, :].rearrange("p (k c) -> p k c", k=4), ACT.Copy).then_inc(yhi, 1)
                split_hi(0, 0)
                over_tiles(act, body)

            @block.gpsimd
            def _(pool):
                pool.sem_inc(wlo_d, 2)

                def split_lo(m, s):
                    pool.wait_ge(whi_d, m + 1)
                    nc.gpsimd.tensor_tensor(w_lo[:, s], raw[:, s], w_hi[:, s].bitcast(F32), ALU.subtract)\
                        .then_inc(wlo_d, 1)
                split_lo(0, 0)
                over_tiles(pool, lambda m, s, more: split_lo(m + 1, 1 - s) if more else None)

            @block.vector
            def _(dve):
                dve.sem_inc(pr_done, 2)
                dve.sem_inc(mlo, 2)
                for n in range(2 * NT):
                    t, a = divmod(n, 2)
                    dve.wait_ge(yhi, n + 1)
                    nc.vector.tensor_tensor(yT_lo[:, a, :, t * P:(t + 1) * P],
                                            tr[:, n % 4, :].rearrange("p (k c) -> p k c", k=4),
                                            yT_hi[:, a, :, t * P:(t + 1) * P].bitcast(F32), ALU.subtract).then_inc(ylo, 1)

                def body(m, s, more):
                    for half in range(2):
                        n = 2 * m + half
                        dve.wait_ge(mm_done, n + 5)
                        dve.wait_ge(sg_done, n + 1)
                        dve.wait_ge(mlo, n + 1)
                        nc.vector.tensor_tensor(prod[:, half], acc[:, 2 * half:2 * half + 2, :], g[:, half],
                                                ALU.mult).then_inc(pr_done, 1)
                        dve.wait_ge(pr_done, n + 3)
                        nc.vector.tensor_tensor(prod[:, half, 0, :], prod[:, half, 0, :], prod[:, half, 1, :],
                                                ALU.add).then_inc(sum_done, 1)
                    for half in range(2):
                        n = 2 * m + half
                        dve.wait_ge(mhi, n + 1)
                        sl = (slice(None), bass.ds(m, 1), slice(half * HALF, (half + 1) * HALF))
                        nc.vector.tensor_tensor(mT_lo[sl].rearrange("p a c -> p (a c)"), prod[:, half, 0, :],
                                                mT_hi[sl].rearrange("p a c -> p (a c)").bitcast(F32),
                                                ALU.subtract).then_inc(mlo, 1)
                over_tiles(dve, body)

            @block.tensor
            def _(pe):
                pe.sem_inc(mm_done, 4)
                for n in range(2 * NT):
                    t, a = divmod(n, 2)
                    pe.wait_ge(y_in[n % 4], 16 * (n // 4 + 1))
                    after(pe, ylo, n - 3)
                    for k in range(4):
                        last = nc.tensor.transpose(tr[:, n % 4, k * P:(k + 1) * P], ytok[:, n % 4, k * P:(k + 1) * P],
                                                   ident[:, :])
                    last.then_inc(tr_mm, 1)
                pe.wait_ge(ylo, 2 * NT)

                def body(m, s, more):
                    pe.wait_ge(wlo_d, m + 3)
                    for half in range(2):
                        pe.wait_ge(pr_done, 2 * m + half + 1)
                        for a in range(2):
                            for k in range(KA4):
                                last = split3(nc, acc[:, 2 * half + a, :], w_hi[:, s, a, k, :], w_lo[:, s, a, k, :],
                                              yT_hi[:, a, k, half * HALF:(half + 1) * HALF],
                                              yT_lo[:, a, k, half * HALF:(half + 1) * HALF], k == 0, k == KA4 - 1)
                        last.then_inc(mm_done, 1)
                over_tiles(pe, body)


def output_and_logits(nc, x, w_out, ffn_norm_w, router_w, router_b, ident, nhalf, mT_hi, mT_lo, raw,
                      raw_in, h_s, xn_s, logits):
    with ExitStack() as ctx:
        sb = lambda n, s, d=F32: ctx.enter_context(nc.sbuf_tensor(n, s, d))
        sem = lambda n: ctx.enter_context(nc.semaphore(n))
        w_hi = sb("op_whi", [P, KD, D], F32R)
        w_lo = sb("op_wlo", [P, KD, D], F32R)
        xt = sb("op_x", [P, 2, D])
        ht = sb("op_h", [P, 2, D])
        xn = sb("op_xn", [P, 2, D])
        xnT = sb("op_xnT", [P, KD, P])
        junk = sb("op_junk", [P, D])
        wB = sb("op_wB", [P, D])
        rw = sb("op_rw", [P, KD, NE])
        rbB = sb("op_rb", [P, NE])
        ssq, ms, rstd = (sb(f"op_{n}", [P, NT]) for n in ("ssq", "ms", "rstd"))
        acc = ctx.enter_context(nc.psum_tensor("op_acc", [P, 4, HALF], F32))
        tr = ctx.enter_context(nc.psum_tensor("op_tr", [P, 2, HALF], F32))
        lg = ctx.enter_context(nc.psum_tensor("op_lg", [P, HALF], F32))
        x_in = [sem(f"op_x_in{s}") for s in range(2)]
        h_out = [sem(f"op_h_out{s}") for s in range(2)]
        xn_out = [sem(f"op_xn_out{s}") for s in range(2)]
        c_in = sem("op_c_in")
        whi_d, wlo_d, mm_done, h_done = sem("op_whi_d"), sem("op_wlo_d"), sem("op_mm"), sem("op_h_d")
        sq_done, ms_done, rstd_done, xn_done = sem("op_sq"), sem("op_ms_d"), sem("op_rstd_d"), sem("op_xn_d")
        tr_mm, tr_ev, lg_mm, lg_ev = sem("op_tr_mm"), sem("op_tr_ev"), sem("op_lg_mm"), sem("op_lg_ev")
        x_t = x.rearrange("a (t p) d -> (a t) p d", p=P)
        h_t = h_s.rearrange("(t p) d -> t p d", p=P)
        xn_t = xn_s.rearrange("(t p) d -> t p d", p=P)
        with nc.Block() as block:
            @block.sync
            def _(sp):
                for k in range(4, KD):
                    sp.wait_ge(wlo_d, k - 3)
                    sp.dma_start(raw[:, k % 4, :], w_out[0, k * P:(k + 1) * P, :]).then_inc(raw_in[k % 4], 16)
                    if k == 5:
                        for t in range(2):
                            sp.dma_start(xt[:, t, :], x_t[t]).then_inc(x_in[t], 16)
                sp.dma_start(wB[:, :], ffn_norm_w[0:1, :].to_broadcast([P, D])).then_inc(c_in, 16)
                sp.dma_start(rbB[:, :], router_b[0:1, :].to_broadcast([P, NE])).then_inc(c_in, 16)
                sp.dma_start(rw[:, :, :], router_w.rearrange("a (k p) c -> p (a k) c", p=P)).then_inc(c_in, 16)
                for t in range(NT):
                    sp.wait_ge(h_done, t + 1)
                    sp.dma_start(h_t[t], ht[:, t % 2, :]).then_inc(h_out[t % 2], 16)
                    if t + 2 < NT:
                        sp.dma_start(xt[:, t % 2, :], x_t[t + 2]).then_inc(x_in[t % 2], 16)
                    sp.wait_ge(xn_done, t + 1)
                    sp.dma_start(xn_t[t], xn[:, t % 2, :]).then_inc(xn_out[t % 2], 16)
                for s in range(2):
                    sp.wait_ge(h_out[s], 16 * NT // 2)
                    sp.wait_ge(xn_out[s], 16 * NT // 2)

            @block.scalar
            def _(act):
                for k in range(KD):
                    act.wait_ge(raw_in[k % 4], 16 * (k // 4 + 1))
                    nc.scalar.activation(w_hi[:, k, :], raw[:, k % 4, :], ACT.Copy).then_inc(whi_d, 1)
                for t in range(NT):
                    act.wait_ge(h_done, t + 1)
                    if t:
                        act.wait_ge(sq_done, t)
                    nc.scalar.activation(junk[:, :], ht[:, t % 2, :], ACT.Square, accum_out=ssq[:, t:t + 1])\
                        .then_inc(sq_done, 1)
                    act.wait_ge(tr_mm, t + 1)
                    after(act, lg_mm, t)
                    nc.scalar.activation(xnT[:, :, :].rearrange("p k c -> p (k c)"),
                                         tr[:, :, :].rearrange("p a c -> p (a c)"), ACT.Copy).then_inc(tr_ev, 1)

            @block.gpsimd
            def _(pool):
                for t in range(NT):
                    pool.wait_ge(sq_done, t + 1)
                    nc.gpsimd.tensor_scalar(ms[:, t:t + 1], ssq[:, t:t + 1], 1.0 / D, EPS,
                                            ALU.mult, ALU.add).then_inc(ms_done, 1)
                    pool.wait_ge(ms_done, t + 1)
                    nc.gpsimd.tensor_tensor(rstd[:, t:t + 1], ms[:, t:t + 1], nhalf[:, 0:1],
                                            ALU.pow).then_inc(rstd_done, 1)

            @block.vector
            def _(dve):
                for k in range(KD):
                    dve.wait_ge(whi_d, k + 1)
                    nc.vector.tensor_tensor(w_lo[:, k, :], raw[:, k % 4, :], w_hi[:, k, :].bitcast(F32),
                                            ALU.subtract).then_inc(wlo_d, 1)
                dve.wait_ge(c_in, 48)

                def residual(t):
                    s = t % 2
                    dve.wait_ge(mm_done, t + 1)
                    dve.wait_ge(x_in[s], 16 * (t // 2 + 1))
                    after(dve, h_out[s], 16 * (t // 2))
                    nc.vector.tensor_tensor(ht[:, s, :], acc[:, 2 * s:2 * s + 2, :].rearrange("p a c -> p (a c)"),
                                            xt[:, s, :], ALU.add).then_inc(h_done, 1)

                def normalize(t):
                    s = t % 2
                    dve.wait_ge(rstd_done, t + 1)
                    after(dve, xn_out[s], 16 * (t // 2))
                    after(dve, tr_mm, t - 1)
                    nc.vector.scalar_tensor_tensor(out=xn[:, s, :], in0=ht[:, s, :], scalar=rstd[:, t:t + 1],
                                                   in1=wB[:, :], op0=ALU.mult, op1=ALU.mult).then_inc(xn_done, 1)

                residual(0)
                normalize(0)
                for t in range(NT):
                    if t + 1 < NT:
                        residual(t + 1)
                        normalize(t + 1)
                    dve.wait_ge(lg_mm, t + 1)
                    nc.vector.tensor_tensor(logits[:, t, :], lg[:, 0:NE], rbB[:, :], ALU.add).then_inc(lg_ev, 1)

            @block.tensor
            def _(pe):
                def project(t, nh):
                    after(pe, h_done, t - 1)
                    for k in range(KD):
                        if t == 0 and nh == 0:
                            pe.wait_ge(wlo_d, k + 1)
                        last = split3(nc, acc[:, 2 * (t % 2) + nh, :], mT_hi[:, k, t * P:(t + 1) * P],
                                      mT_lo[:, k, t * P:(t + 1) * P], w_hi[:, k, nh * HALF:(nh + 1) * HALF],
                                      w_lo[:, k, nh * HALF:(nh + 1) * HALF], k == 0, k == KD - 1)
                    if nh:
                        last.then_inc(mm_done, 1)

                for t in range(2):
                    project(t, 0)
                    project(t, 1)
                for t in range(NT):
                    pe.wait_ge(xn_done, t + 1)
                    after(pe, tr_ev, t)
                    for k in range(KD):
                        last = nc.tensor.transpose(tr[:, k // 4, (k % 4) * P:(k % 4 + 1) * P],
                                                   xn[:, t % 2, k * P:(k + 1) * P], ident[:, :])
                    last.then_inc(tr_mm, 1)
                    if t + 2 < NT:
                        project(t + 2, 0)
                    pe.wait_ge(tr_ev, t + 1)
                    after(pe, lg_ev, t)
                    for k in range(KD):
                        last = nc.tensor.matmul(lg[:, 0:NE], xnT[:, k, :], rw[:, k, :], start=k == 0, stop=k == KD - 1)
                    last.then_inc(lg_mm, 1)
                    if t + 2 < NT:
                        project(t + 2, 1)


SLOTS = (NBLK + 1) * CAP
TABLE = -(-SLOTS // P) * P


def route(nc, logits, gates, dest, tabs, slot_token):
    with ExitStack() as ctx:
        sb = lambda n, s, d=F32: ctx.enter_context(nc.sbuf_tensor(n, s, d))
        sem = lambda n: ctx.enter_context(nc.semaphore(n))
        top = sb("rt_top", [P, NT, 8])
        idx = sb("rt_idx", [P, NT, 8], U32)
        idxf = sb("rt_idxf", [P, NT, TOPK])
        ex = sb("rt_ex", [P, NT, TOPK])
        den = sb("rt_den", [P, NT])
        iota_e = sb("rt_iota", [P, NE])
        oh = sb("rt_oh", [P, NT, TOPK, NE])
        prod = sb("rt_prod", [P, NT, TOPK, NE])
        chosen = sb("rt_chosen", [P, NT, NE])
        chosen16 = sb("rt_chosen16", [P, NT, NE], BF16)
        upper = sb("rt_upper", [P, P], BF16)
        ones = sb("rt_ones", [P, P], BF16)
        one_col = sb("rt_one", [P, 1])
        cnt, over, cum, base0, base1, step_b = (sb(f"rt_{n}", [P, NE]) for n in
                                               ("cnt", "over", "cum", "base0", "base1", "stepb"))
        rank = sb("rt_rank", [P, NT, NE])
        place = sb("rt_place", [P, NT, NE])
        destf = sb("rt_destf", [P, NT * TOPK])
        cmp = sb("rt_cmp", [1, MAXOVER, NE])
        iota_b = sb("rt_iotab", [1, MAXOVER])
        tabf = sb("rt_tabf", [1, NE + MAXOVER + 1])
        zero = sb("rt_zero", [P, TABLE // P], I32)
        prk = ctx.enter_context(nc.psum_tensor("rt_prk", [P, HALF], F32))
        pct = ctx.enter_context(nc.psum_tensor("rt_pct", [P, HALF], F32))
        c_set, v, a_exp, mm, z_out = sem("rt_cset"), sem("rt_v"), sem("rt_exp"), sem("rt_mm"), sem("rt_zout")
        m16 = sem("rt_m16")
        with nc.Block() as block:
            @block.sync
            def _(sp):
                sp.wait_ge(c_set, 6)
                sp.dma_start(slot_token.rearrange("(p n) a -> p (n a)", p=P), zero[:, :]).then_inc(z_out, 16)
                sp.wait_ge(z_out, 16)

            @block.gpsimd
            def _(pool):
                nc.gpsimd.iota(iota_e[:, :], [[1, NE]], base=0, channel_multiplier=0,
                               allow_small_or_imprecise_dtypes=True).then_inc(c_set, 1)
                nc.gpsimd.iota(iota_b[:, :], [[1, MAXOVER]], base=0, channel_multiplier=0,
                               allow_small_or_imprecise_dtypes=True).then_inc(c_set, 1)
                nc.gpsimd.memset(ones[:, :], 1.0).then_inc(c_set, 1)
                nc.gpsimd.memset(upper[:, :], 1.0).then_inc(c_set, 1)
                nc.gpsimd.memset(one_col[:, :], 1.0).then_inc(c_set, 1)
                nc.gpsimd.memset(zero[:, :], 0).then_inc(c_set, 1)
                pool.wait_ge(c_set, 6)
                nc.gpsimd.affine_select(out=upper[:, :], in_=upper[:, :], compare_op=ALU.is_gt, fill=0.0, base=0,
                                        pattern=[[1, P]], channel_multiplier=-1).then_inc(c_set, 1)

            @block.scalar
            def _(act):
                act.wait_ge(v, 2 * NT + 1)
                nc.scalar.activation(ex[:, :, :], ex[:, :, :], ACT.Exp).then_inc(a_exp, 1)

            @block.vector
            def _(dve):
                n = [0]

                def step(ins):
                    n[0] += 1
                    ins.then_inc(v, 1)
                    dve.wait_ge(v, n[0])

                for t in range(NT):
                    step(nc.vector.max(top[:, t, :], logits[:, t, :]))
                    step(nc.vector.max_index(idx[:, t, :], top[:, t, :], logits[:, t, :]))
                step(nc.vector.tensor_tensor(ex[:, :, :], top[:, :, 0:TOPK], top[:, :, 0:1].to_broadcast([P, NT, TOPK]),
                                             ALU.subtract))
                step(nc.vector.tensor_copy(idxf[:, :, :], idx[:, :, 0:TOPK]))
                dve.wait_ge(c_set, 7)
                step(nc.vector.tensor_tensor(
                    oh[:, :, :, :].rearrange("p t j e -> p (t j) e"),
                    iota_e[:, :].rearrange("p (o e) -> p o e", o=1).to_broadcast([P, NT * TOPK, NE]),
                    idxf[:, :, :].rearrange("p t (j o) -> p (t j) o", o=1).to_broadcast([P, NT * TOPK, NE]), ALU.is_equal))
                step(nc.vector.tensor_reduce(chosen[:, :, :], oh[:, :, :, :].rearrange("p t j e -> p t e j"), AX_X, ALU.add))
                nc.vector.tensor_copy(chosen16[:, :, :], chosen[:, :, :]).then_inc(m16, 1)
                dve.wait_ge(a_exp, 1)
                step(nc.vector.tensor_reduce(den[:, :], ex[:, :, :], AX_X, ALU.add))
                step(nc.vector.reciprocal(den[:, :], den[:, :]))
                step(nc.vector.tensor_tensor(gates[:, :, :], ex[:, :, :],
                                             den[:, :].rearrange("p (t o) -> p t o", o=1).to_broadcast([P, NT, TOPK]),
                                             ALU.mult))
                dve.wait_ge(mm, 2)
                step(nc.vector.tensor_copy(cnt[:, :], pct[:, 0:NE]))
                step(nc.vector.tensor_scalar(over[:, :], cnt[:, :], float(CAP), None, ALU.is_gt))
                for m in range(2, -(-T // CAP)):
                    step(nc.vector.scalar_tensor_tensor(out=over[:, :], in0=cnt[:, :], scalar=float(CAP * m), in1=over[:, :],
                                                        op0=ALU.is_gt, op1=ALU.add))
                step(nc.vector.tensor_tensor_scan(out=cum[:, :], data0=one_col[:, 0:1].to_broadcast([P, NE]),
                                                  data1=over[:, :], initial=0.0, op0=ALU.mult, op1=ALU.add))
                step(nc.vector.tensor_tensor(base1[:, :], cum[:, :], over[:, :], ALU.subtract))
                step(nc.vector.tensor_scalar(base1[:, :], base1[:, :], float(NE - 1), float(CAP), ALU.add, ALU.mult))
                step(nc.vector.tensor_scalar(base0[:, :], iota_e[:, :], float(CAP), None, ALU.mult))
                step(nc.vector.tensor_tensor(step_b[:, :], base0[:, :], base1[:, :], ALU.subtract))
                step(nc.vector.tensor_copy(rank[:, :, :], prk[:, 0:NT * NE].rearrange("p (t e) -> p t e", e=NE)))
                step(nc.vector.tensor_scalar(place[:, :, :], rank[:, :, :], float(CAP), None, ALU.is_lt))
                over_t = lambda b: b[:, :].rearrange("p (o e) -> p o e", o=1).to_broadcast([P, NT, NE])
                step(nc.vector.tensor_tensor(place[:, :, :], place[:, :, :], over_t(step_b), ALU.mult))
                step(nc.vector.tensor_tensor(place[:, :, :], place[:, :, :], over_t(base1), ALU.add))
                step(nc.vector.tensor_tensor(place[:, :, :], place[:, :, :], rank[:, :, :], ALU.add))
                for j in range(TOPK):
                    step(nc.vector.tensor_tensor(prod[:, :, j, :], oh[:, :, j, :], place[:, :, :], ALU.mult))
                step(nc.vector.tensor_reduce(destf[:, :], prod[:, :, :, :].rearrange("p t j e -> p (t j) e"), AX_X, ALU.add))
                step(nc.vector.tensor_copy(dest[:, :], destf[:, :]))
                step(nc.vector.tensor_tensor(cmp[:, :, :],
                                             cum[0:1, :].rearrange("p (o e) -> p o e", o=1).to_broadcast([1, MAXOVER, NE]),
                                             iota_b[:, :].rearrange("p (b o) -> p b o", o=1).to_broadcast([1, MAXOVER, NE]),
                                             ALU.is_le))
                step(nc.vector.tensor_reduce(tabf[:, NE:NE + MAXOVER], cmp[:, :, :], AX_X, ALU.add))
                step(nc.vector.tensor_scalar(tabf[:, NE:NE + MAXOVER], tabf[:, NE:NE + MAXOVER], float(NE - 1), None, ALU.min))
                step(nc.vector.tensor_copy(tabf[:, 0:NE], cnt[0:1, :]))
                step(nc.vector.tensor_copy(tabf[:, NE + MAXOVER:NE + MAXOVER + 1], cum[0:1, NE - 1:NE]))
                step(nc.vector.tensor_copy(tabs[:, :], tabf[:, :]))

            @block.tensor
            def _(pe):
                pe.wait_ge(c_set, 7)
                pe.wait_ge(m16, 1)
                for t in range(NT):
                    for b in range(t + 1):
                        last = nc.tensor.matmul(prk[:, t * NE:(t + 1) * NE], (upper if b == t else ones)[:, :],
                                                chosen16[:, b, :], start=b == 0, stop=b == t)
                last.then_inc(mm, 1)
                for b in range(NT):
                    last = nc.tensor.matmul(pct[:, 0:NE], ones[:, :], chosen16[:, b, :], start=b == 0, stop=b == NT - 1)
                last.then_inc(mm, 1)


CHUNKS = 6
CW = 4096
FT = FF // P
Q = P // CAP2
XW = D // Q


def experts(nc, xn_s, h_s, w_gate_up, b_gate_up, w_down, b_down, ident, dest, tabs, slot_token, y_slots, hbuf, h_in):
    with ExitStack() as ctx:
        sb = lambda n, s, d=F32: ctx.enter_context(nc.sbuf_tensor(n, s, d))
        sem = lambda n: ctx.enter_context(nc.semaphore(n))
        w = sb("ex_w", [P, CHUNKS, CW])
        idx = sb("ex_idx", [P, 2], U32)
        idx2 = sb("ex_idx2", [P, 1], U32)
        quarter = sb("ex_quarter", [P, 1])
        xg = sb("ex_xg", [P, D])
        xg2 = sb("ex_xg2", [P, XW])
        xT = sb("ex_xT", [P, KD, CAP])
        gs = sb("ex_g", [P, 2, CAP])
        us = sb("ex_u", [P, 2, CAP])
        sg = sb("ex_sg", [P, 2, CAP])
        hid = sb("ex_hid", [P, FT, CAP])
        yT = sb("ex_yT", [P, KD, P])
        yT2 = sb("ex_yT2", [P, KD, CAP2])
        ytok = sb("ex_ytok", [P, D])
        ytok2 = sb("ex_ytok2", [P, 2, P])
        bT = sb("ex_bT", [P, 3 * KD, NE])
        bcur = sb("ex_bcur", [P, 3 * KD])
        brow = hid[0:NE, :, :].rearrange("p a c -> p (a c)")
        tokid = sb("ex_tokid", [P, NT], I32)
        ps = lambda n, s: ctx.enter_context(nc.psum_tensor(n, s, F32))
        gu = ps("ex_gu", [P, 4, HALF])
        yp = ps("ex_yp", [P, 2, HALF])
        tr = ps("ex_tr", [P, 2, HALF])

        b_in, b_mm, b_ev, b_d = sem("b_in"), sem("b_mm"), sem("b_ev"), sem("b_d")
        ini, tok_out, tok_set = sem("ini"), sem("tok_out"), sem("tok_set")
        w_in_ = [sem(f"e_w_in{c}") for c in range(CHUNKS)]
        idx_in, idx2_d, x_in = sem("idx_in"), sem("idx2_d"), sem("x_in")
        tr_mm = sem("e_tr_mm")
        tr_ev = sem("e_tr_ev")
        gu_mm = sem("gu_mm")
        g_d = sem("g_d")
        gu_ev = sem("gu_ev")
        sg_d, t_d, hid_d = sem("sg_d"), sem("t_d"), sem("hid_d")
        yp_mm = sem("yp_mm")
        yp_ev = sem("yp_ev")
        y_out = sem("e_y_out")
        spare, spare_sp, spare_dve = sem("spare"), sem("spare_sp"), sem("spare_dve")
        STORE = 16 * (1 + Q)

        gate_up_v = w_gate_up.rearrange("a e (k p) c -> (a e) p k c", p=P)
        down_v = w_down.rearrange("a e (k p) c -> (a e) p k c", p=P)
        nov_ap = tabs[0:1, NE + MAXOVER:NE + MAXOVER + 1]

        def over_blocks(eng, body, first=0):
            with eng.Fori(first, NE) as b:
                body(b, False)
            nov = eng.value_load(nov_ap, min_val=0, max_val=MAXOVER)
            with eng.Fori(0, MAXOVER) as i:
                with eng.If(i < nov):
                    body(NE + i, True)
            return nov

        def over_expert(eng, b):
            return eng.value_load(tabs[0:1, bass.ds(b, 1)], min_val=0, max_val=NE - 1)

        def w_tile(c, j, k, part=0):
            if c < 4:
                return w[:, c, :].rearrange("p (h k q) -> p h k q", h=2, k=KD)[:, part, k, j * P:(j + 1) * P]
            return w[:, c, :].rearrange("p (k q) -> p k q", k=KD)[:, k, j * P:(j + 1) * P]

        block = ctx.enter_context(nc.Block())

        @block.sync
        def _(sp):
            def load(c, e):
                if c < 4:
                    v = w[:, c, :].rearrange("p (h k q) -> p h k q", h=2, k=KD)
                    for h in range(2):
                        sp.dma_start(v[:, h, :, :],
                                     gate_up_v[bass.ds(e, 1), :, :, h * FF + 2 * P * c:h * FF + 2 * P * (c + 1)]
                                     .rearrange("a p k c -> (a p) k c")).then_inc(w_in_[c], 16)
                else:
                    v = w[:, c, :].rearrange("p (k q) -> p k q", k=KD)
                    for h in range(2):
                        sp.dma_start(v[:, 4 * h:4 * h + 4, :],
                                     down_v[bass.ds(e, 1), :, 4 * h:4 * h + 4, (c - 4) * HALF:(c - 3) * HALF]
                                     .rearrange("a p k c -> (a p) k c")).then_inc(w_in_[c], 16)

            def store(b):
                sp.wait_ge(tr_ev, 6 * b + 14)
                sp.dma_start(y_slots[bass.ds(b * CAP, P), :], ytok[:, :]).then_inc(y_out, 16)
                for d in range(Q):
                    sp.dma_start(y_slots[bass.ds(b * CAP + P, CAP2), :]
                                 .rearrange("s (g d f) -> s g d f", g=2, d=Q)[:, :, d, :],
                                 ytok2[d * CAP2:(d + 1) * CAP2, :, :]).then_inc(y_out, 16)

            def body(b, over):
                e = over_expert(sp, b) if over else b
                for c in range(CHUNKS):
                    if c < 4:
                        sp.wait_ge(gu_mm, FT * (b - 1) + 2 * c + 2)
                    else:
                        sp.wait_ge(yp_mm, KD * (b - 1) + 4 * (c - 3))
                    load(c, e)
                    if c == 5:
                        store(b - 1)

            sp.dma_start(brow[:, 0:D], b_gate_up[0, :, 0:D]).then_inc(b_in, 16)
            load(0, 0)
            for part, src in ((1, b_gate_up[0, :, D:2 * D]), (2, b_down[0, :, :])):
                sp.wait_ge(b_mm, part)
                sp.dma_start(brow[:, 0:D], src).then_inc(b_in, 16)
            load(1, 0)
            sp.wait_ge(x_in, 32)
            for c in range(2, CHUNKS):
                load(c, 0)
            nov = over_blocks(sp, body, first=1)
            h_t = h_s.rearrange("(t p) d -> t p d", p=P)
            for t in range(NT):
                sp.dma_start(hbuf[:, t, :], h_t[t]).then_inc(h_in, 16)
            store(nov + (NE - 1))
            sp.wait_ge(y_out, STORE * (NE + nov) + 2 * STORE)
            sp.sem_inc(spare_sp, 1)

        @block.scalar
        def _(act):
            act.preload_act_table_set("sigmoid_and_others")
            act.sem_inc(yp_ev, 2)

            def body(b, over):
                for ft in range(FT):
                    act.wait_ge(g_d, FT * b + ft + 1)
                    nc.scalar.activation(sg[:, ft % 2, :], gs[:, ft % 2, :], ACT.Sigmoid, scale=ALPHA).then_inc(sg_d, 1)
                act.wait_ge(b_d, b + 1)
                for dt in range(KD):
                    act.wait_ge(yp_mm, KD * b + dt + 1)
                    bias = bcur[:, 2 * KD + dt:2 * KD + dt + 1]
                    nc.scalar.activation(yT[:, dt, :], yp[:, dt % 2, 0:P], ACT.Identity, bias=bias)
                    nc.scalar.activation(yT2[:, dt, :], yp[:, dt % 2, P:CAP], ACT.Identity, bias=bias)\
                        .then_inc(yp_ev, 1)
            over_blocks(act, body)

        @block.gpsimd
        def _(pool):
            nc.gpsimd.iota(tokid[:, :], [[P, NT]], base=0, channel_multiplier=1).then_inc(tok_set, 1)
            for q in range(Q):
                pool.wait_ge(tok_set, q + 1)
                nc.gpsimd.memset(quarter[q * CAP2:(q + 1) * CAP2, :], float(q)).then_inc(tok_set, 1)
            pool.wait_ge(tok_set, 1 + Q)
            for t in range(NT):
                for j in range(TOPK):
                    pool.indirect_dma_start(out=slot_token[:, :], out_offset=bass.IndirectOffsetOnAxis(
                        ap=dest[:, t * TOPK + j:t * TOPK + j + 1], axis=0), in_=tokid[:, t:t + 1],
                        in_offset=None).then_inc(tok_out, 16)
            pool.wait_ge(tok_out, 16 * NT * TOPK)

            def load_idx(b):
                pool.dma_start(idx[:, 0:1].bitcast(I32), slot_token[bass.ds(b * CAP, P), :]).then_inc(idx_in, 16)
                for q in range(Q):
                    pool.dma_start(idx[q * CAP2:(q + 1) * CAP2, 1:2].bitcast(I32),
                                   slot_token[bass.ds(b * CAP + P, CAP2), :]).then_inc(idx_in, 16)

            def rows():
                nc.gpsimd.tensor_scalar(idx2[:, :], idx[:, 1:2], float(Q), quarter[:, 0:1], ALU.mult, ALU.add)\
                    .then_inc(idx2_d, 1)

            def gather():
                pool.indirect_dma_start(out=xg[:, :], out_offset=None, in_=xn_s[:, :],
                                        in_offset=bass.IndirectOffsetOnAxis(ap=idx[:, 0:1], axis=0)).then_inc(x_in, 16)
                pool.indirect_dma_start(out=xg2[:, :], out_offset=None, in_=xn_s.rearrange("t (q c) -> (t q) c", q=Q),
                                        in_offset=bass.IndirectOffsetOnAxis(ap=idx2[:, 0:1], axis=0)).then_inc(x_in, 16)

            load_idx(0)
            pool.wait_ge(idx_in, 16 * (1 + Q))
            rows()
            pool.wait_ge(idx2_d, 1)
            gather()

            def body(b, over):
                hold(pool, x_in, 32 * b + 32, spare)
                load_idx(b + 1)
                hold(pool, idx_in, 16 * (1 + Q) * (b + 2), spare)
                rows()
                hold(pool, idx2_d, b + 2, spare)
                hold(pool, tr_ev, 6 * b + 5, spare)
                gather()
            over_blocks(pool, body)

        @block.vector
        def _(dve):
            dve.sem_inc(gu_ev, 4)
            dve.sem_inc(tr_ev, 2)
            dve.sem_inc(y_out, 2 * STORE)
            for bank in (gu, yp):
                nc.vector.memset(bank[:, :, :], 0.0).then_inc(ini, 1)
            for buf in (yT, yT2):
                nc.vector.memset(buf[:, :, :], 0.0).then_inc(ini, 1)
            for part in range(3):
                dve.wait_ge(b_mm, part + 1)
                nc.vector.tensor_scalar(bT[:, part * KD:(part + 1) * KD, :],
                                        tr[:, part % 2, 0:KD * NE].rearrange("p (k e) -> p k e", k=KD),
                                        1.0 if part == 1 else 0.0, None, ALU.add).then_inc(b_ev, 1)

            def take_x(b):
                for g in range(3):
                    dve.wait_ge(tr_mm, 6 * b + g + 1)
                    if g < 2:
                        dst, src = xT[:, 4 * g:4 * g + 4, 0:P], tr[:, g, :].rearrange("p (k c) -> p k c", k=4)
                    else:
                        dst = xT[:, :, P:CAP].rearrange("p (q h) c -> p h q c", h=2)
                        src = tr[:, 0, 0:2 * P].rearrange("p (h q c) -> p h q c", h=2, q=Q)
                    nc.vector.tensor_copy(dst, src).then_inc(tr_ev, 1)

            def take_y(b, parts):
                for g in parts:
                    dve.wait_ge(tr_mm, 6 * b + 4 + g)
                    if g < 2:
                        nc.vector.tensor_copy(ytok[:, g * HALF:(g + 1) * HALF], tr[:, 1 - g, :]).then_inc(tr_ev, 1)
                    else:
                        nc.vector.tensor_copy(ytok2[:, :, :], tr[:, 1, 0:2 * P].rearrange("p (g f) -> p g f", g=2))\
                            .then_inc(tr_ev, 1)

            take_x(0)

            def body(b, over):
                e = over_expert(dve, b) if over else b
                hold(dve, yp_ev, KD * b + 2, spare_dve)
                nc.vector.tensor_copy(bcur[:, :], bT[:, :, bass.ds(e, 1)].rearrange("p k a -> p (k a)")).then_inc(b_d, 1)
                dve.wait_ge(b_d, b + 1)
                for ft in range(FT):
                    f = FT * b + ft
                    dve.wait_ge(gu_mm, f + 1)
                    nc.vector.tensor_scalar(gs[:, ft % 2, :], gu[:, ft % 4, 0:CAP], bcur[:, ft:ft + 1], LIMIT,
                                            ALU.add, ALU.min).then_inc(g_d, 1)
                    nc.vector.tensor_scalar(us[:, ft % 2, :], gu[:, ft % 4, 256:256 + CAP],
                                            bcur[:, KD + ft:KD + ft + 1], 1.0 - LIMIT, ALU.add, ALU.max)\
                        .then_inc(gu_ev, 1)
                    dve.wait_ge(sg_d, f + 1)
                    nc.vector.tensor_tensor(gs[:, ft % 2, :], gs[:, ft % 2, :], sg[:, ft % 2, :], ALU.mult)\
                        .then_inc(t_d, 1)
                    dve.wait_ge(gu_ev, f + 5)
                    dve.wait_ge(t_d, f + 1)
                    nc.vector.scalar_tensor_tensor(out=hid[:, ft, :], in0=us[:, ft % 2, :], scalar=1.0 + LIMIT,
                                                   in1=gs[:, ft % 2, :], op0=ALU.min, op1=ALU.mult).then_inc(hid_d, 1)
                    if ft == 1:
                        dve.wait_ge(y_out, STORE * b + STORE)
                        take_y(b, (0, 1))
                    if ft == 2:
                        take_y(b, (2,))
                take_x(b + 1)
            nov = over_blocks(dve, body)
            dve.wait_ge(y_out, STORE * (NE + nov) + STORE)
            take_y(NE + nov, (0, 1, 2))

        @block.tensor
        def _(pe):
            def turn_x(b, parts):
                for g in parts:
                    if g == 0:
                        pe.wait_ge(x_in, 32 * b + 32)
                    pe.wait_ge(tr_ev, 6 * b + g + 1)
                    for k in range(4 if g < 2 else 2):
                        src = xg[:, (4 * g + k) * P:(4 * g + k + 1) * P] if g < 2 else xg2[:, k * P:(k + 1) * P]
                        last = nc.tensor.transpose(tr[:, g % 2, k * P:(k + 1) * P], src, ident[:, :])
                    last.then_inc(tr_mm, 1)

            def turn_y(b, parts):
                for g in parts:
                    if g == 0:
                        pe.wait_ge(yp_ev, KD * b + 2)
                    pe.wait_ge(tr_ev, 6 * b + 4 + g)
                    for k in range(4 if g < 2 else 2):
                        src = yT[:, 4 * g + k, :] if g < 2 else \
                            yT2[:, 4 * k:4 * k + 4, :].rearrange("p d c -> p (d c)")
                        last = nc.tensor.transpose(tr[:, (1 + g) % 2, k * P:(k + 1) * P], src, ident[:, :])
                    last.then_inc(tr_mm, 1)

            for part in range(3):
                pe.wait_ge(b_in, 16 * (part + 1))
                after(pe, b_ev, part - 1)
                for k in range(KD):
                    last = nc.tensor.transpose(tr[:, part % 2, k * NE:(k + 1) * NE], brow[:, k * P:(k + 1) * P],
                                               ident[0:NE, 0:NE])
                last.then_inc(b_mm, 1)
            pe.wait_ge(b_ev, 3)
            turn_x(0, (0, 1, 2))
            pe.wait_ge(ini, 4)

            def gate_up(b, ft, width):
                if ft % 2 == 0:
                    pe.wait_ge(w_in_[ft // 2], 32 * b + 32)
                pe.wait_ge(gu_ev, FT * b + ft + 1)
                for part in range(2):
                    for k in range(KD):
                        last = nc.tensor.matmul(gu[:, ft % 4, 256 * part:256 * part + width],
                                                w_tile(ft // 2, ft % 2, k, part), xT[:, k, 0:width],
                                                start=k == 0, stop=k == KD - 1)
                last.then_inc(gu_mm, 1)

            def down(b, dts, width):
                if dts[0] % 4 == 0:
                    pe.wait_ge(w_in_[4 + dts[0] // 4], 32 * b + 32)
                pe.wait_ge(yp_ev, KD * b + dts[-1] + 1)
                for k in range(KD):
                    if dts[0] == 0:
                        pe.wait_ge(hid_d, FT * b + k + 1)
                    for dt in dts:
                        last = nc.tensor.matmul(yp[:, dt % 2, 0:width], w_tile(4 + dt // 4, dt % 4, k), hid[:, k, 0:width],
                                                start=k == 0, stop=k == KD - 1)
                        if k == KD - 1:
                            last.then_inc(yp_mm, 1)

            def multiply(b, width):
                pe.wait_ge(tr_ev, 6 * b + 5)
                for ft in range(FT):
                    gate_up(b, ft, width)
                    if ft == 1:
                        turn_y(b, (0, 1))
                    if ft == 2:
                        turn_y(b, (2,))
                down(b, (0, 1), width)
                turn_x(b + 1, (0, 1))
                for dt in range(2, KD):
                    down(b, (dt,), width)
                    if dt == 3:
                        turn_x(b + 1, (2,))

            def by_width(b, count, widths):
                if len(widths) == 1:
                    multiply(b, widths[0])
                    return
                with pe.If(count < widths[0] + 1):
                    multiply(b, widths[0])
                with pe.Else():
                    by_width(b, count, widths[1:])

            def body(b, over):
                if over:
                    multiply(b, CAP)
                else:
                    by_width(b, pe.value_load(tabs[0:1, bass.ds(b, 1)], min_val=0, max_val=T), WIDTHS)
            nov = over_blocks(pe, body)
            turn_y(NE + nov, (0, 1, 2))


def combine(nc, hbuf, h_in, y_slots, gates, dest, out):
    IN_FLIGHT = 4
    with ExitStack() as ctx:
        sb = lambda n, s, d=F32: ctx.enter_context(nc.sbuf_tensor(n, s, d))
        sem = lambda n: ctx.enter_context(nc.semaphore(n))
        y = sb("co_y", [P, IN_FLIGHT, TOPK, D])
        acc = sb("co_acc", [P, NT, 2, D])
        y_in = [sem(f"co_y_in{s}") for s in range(IN_FLIGHT)]
        add_d, sum_d, y_out = sem("co_add"), sem("co_sum"), sem("co_out")
        out_t = out.rearrange("a (t p) d -> (a t) p d", p=P)
        with nc.Block() as block:
            @block.sync
            def _(sp):
                for t in range(NT):
                    sp.wait_ge(sum_d, t + 1)
                    sp.dma_start(out_t[t], acc[:, t, 1, :]).then_inc(y_out, 16)
                sp.wait_ge(y_out, 16 * NT)

            @block.gpsimd
            def _(pool):
                for t in range(NT):
                    if t >= IN_FLIGHT:
                        pool.wait_ge(sum_d, t - IN_FLIGHT + 1)
                    for j in range(TOPK):
                        pool.indirect_dma_start(out=y[:, t % IN_FLIGHT, j, :], out_offset=None, in_=y_slots[:, :],
                                                in_offset=bass.IndirectOffsetOnAxis(
                                                    ap=dest[:, t * TOPK + j:t * TOPK + j + 1], axis=0))\
                            .then_inc(y_in[t % IN_FLIGHT], 16)

            @block.vector
            def _(dve):
                dve.wait_ge(h_in, 16 * NT)
                for t in range(NT):
                    dve.wait_ge(y_in[t % IN_FLIGHT], 16 * TOPK * (t // IN_FLIGHT + 1))
                    for j in range(TOPK):
                        if j:
                            dve.wait_ge(add_d, (TOPK - 1) * t + j)
                        src = hbuf[:, t, :] if j == 0 else acc[:, t, (j - 1) % 2, :]
                        nc.vector.scalar_tensor_tensor(out=acc[:, t, j % 2, :], in0=y[:, t % IN_FLIGHT, j, :],
                                                       scalar=gates[:, t, j:j + 1], in1=src,
                                                       op0=ALU.mult, op1=ALU.add)\
                            .then_inc(sum_d if j == TOPK - 1 else add_d, 1)


def build(nc, x, attn_norm_w, w_in, q_norm_w, k_norm_w, sinks, w_proj_swa, w_proj_sb, w_out, ffn_norm_w,
          router_w, router_b, w_gate_up, b_gate_up, w_down, b_down, out):
    dram = lambda n, s, d=F32: nc.dram_tensor(n, s, d, kind="Internal").ap()
    gT = dram("gT", (2 * KD, P, T))
    y_s = dram("y_s", (2, T, PAIRS * P))
    h_s = dram("h_s", (T, D))
    xn_s = dram("xn_s", (T, D))
    slot_token = dram("slot_token", (TABLE, 1), I32)
    y_slots = dram("y_slots", (NBLK * CAP, D))
    with ExitStack() as top:
        sbt = lambda n, s, d=F32: top.enter_context(nc.sbuf_tensor(n, s, d))
        ident = sbt("ident", [P, P])
        eps_col = sbt("eps_col", [P, 1])
        nhalf = sbt("nhalf", [P, 1])
        logits = sbt("logits", [P, NT, NE])
        gates = sbt("gates", [P, NT, TOPK])
        dest = sbt("dest", [P, NT * TOPK], U32)
        tabs = sbt("tabs", [1, NE + MAXOVER + 1], I32)
        make_constants(nc, ident, eps_col, nhalf)
        with ExitStack() as front:
            sbf = lambda n, s, d=F32: front.enter_context(nc.sbuf_tensor(n, s, d))
            xnT_hi = sbf("xnT_hi", [P, KD, T], F32R)
            xnT_lo = sbf("xnT_lo", [P, KD, T], F32R)
            va = sbf("va", [P, NT, PAIRS * HD])
            vb = sbf("vb", [P, NT, PAIRS * P])
            raw = sbf("at_raw", [P, 2, KD, P])
            raw_in = [front.enter_context(nc.semaphore(f"raw_in{s}")) for s in range(2)]
            with ExitStack() as values:
                raw_v = values.enter_context(nc.sbuf_tensor("raw_v", [P, KD, VW], F32))
                rawv_in = values.enter_context(nc.semaphore("rawv_in"))
                norm_and_transpose(nc, x, attn_norm_w, w_in, ident, nhalf, xnT_hi, xnT_lo, raw_v, rawv_in)
                project_values(nc, w_in, raw_v, rawv_in, raw, raw_in, xnT_hi, xnT_lo, va, vb)
            attention(nc, w_in, q_norm_w, k_norm_w, sinks, ident, eps_col, raw, raw_in, xnT_hi, xnT_lo, va, vb,
                      gT, y_s, y_slots)
        with ExitStack() as mid:
            sbm = lambda n, s, d=F32: mid.enter_context(nc.sbuf_tensor(n, s, d))
            mT_hi = sbm("mT_hi", [P, KD, T], F32R)
            mT_lo = sbm("mT_lo", [P, KD, T], F32R)
            raw_o = sbm("raw_o", [P, 4, D])
            raw_o_in = [mid.enter_context(nc.semaphore(f"raw_o_in{s}")) for s in range(4)]
            merge(nc, w_proj_swa, w_proj_sb, ident, gT, y_s, mT_hi, mT_lo, w_out, raw_o, raw_o_in)
            output_and_logits(nc, x, w_out, ffn_norm_w, router_w, router_b, ident, nhalf, mT_hi, mT_lo,
                              raw_o, raw_o_in, h_s, xn_s, logits)
        route(nc, logits, gates, dest, tabs, slot_token)
        hbuf = sbt("hbuf", [P, NT, D])
        h_in = top.enter_context(nc.semaphore("h_in"))
        experts(nc, xn_s, h_s, w_gate_up, b_gate_up, w_down, b_down, ident, dest, tabs, slot_token, y_slots,
                hbuf, h_in)
        combine(nc, hbuf, h_in, y_slots, gates, dest, out)


_INS = ["x", "attn_norm_w", "w_in", "q_norm_w", "k_norm_w", "sinks", "w_proj_swa", "w_proj_sb", "w_out",
        "ffn_norm_w", "router_w", "router_b", "w_gate_up", "b_gate_up", "w_down", "b_down"]


def kernel(**inputs):
    import numpy as _np
    import concourse.bacc as _bacc
    from concourse import mybir as _mybir
    from concourse.bass_utils import run_bass_kernel_spmd as _run

    nc = _bacc.Bacc("TRN2", target_bir_lowering=False, num_devices=1)
    arrays, args = {}, []
    for name in _INS:
        a = _np.ascontiguousarray(inputs[name])
        arrays[f"in_{name}_dram"] = a
        args.append(nc.dram_tensor(f"in_{name}_dram", a.shape, _mybir.dt.from_np(a.dtype), kind="ExternalInput").ap())
    args.append(nc.dram_tensor("out_0_dram", (1, T, D), _mybir.dt.float32, kind="ExternalOutput").ap())
    build(nc, *args)
    r = _run(nc, [arrays], core_ids=[0])
    return r.results[0]["out_0_dram"]
```
